# Optimizing a Trainium2 kernel written in Bass

```python
import math
import jax, jax.numpy as jnp
from jax import lax
import numpy as np
import jax
import jax.numpy as jnp

D_MODEL = 1024
BATCH = 1
SEQ = 512
DEPTH = 2

RG_WIDTH = D_MODEL // 2
RG_BLOCKS = 8
RG_BLOCK = RG_WIDTH // RG_BLOCKS
CONV_WIDTH = 4
RG_C = 8.0
GLA_HEADS = 4
GLA_VDIM = D_MODEL // 2
GLA_KDIM = GLA_VDIM // 2
GLA_HK = GLA_KDIM // GLA_HEADS
GLA_HV = GLA_VDIM // GLA_HEADS
GLA_LOWRANK = 16
GLA_GATE_TAU = 16.0
GLA_CHUNK = 64
EVEN_IN = 2 * RG_WIDTH + 2 * GLA_KDIM + 2 * GLA_VDIM + GLA_LOWRANK
MIX_WIDTH = RG_WIDTH + GLA_VDIM

FOX_HEADS = 16
FOX_HD = D_MODEL // FOX_HEADS
FOX_BLOCK = 128
ODD_IN = 4 * D_MODEL + FOX_HEADS

D_FF = 4 * D_MODEL
N_EVEN = (DEPTH + 1) // 2
N_ODD = DEPTH // 2
ALPHA = (2 * DEPTH) ** 0.25
BETA = (8 * DEPTH) ** -0.25
LN_EPS = 1e-5
RMS_EPS = 1e-6


def layer_norm(x, g, b):
    xf = x.astype(jnp.float32)
    mu = jnp.mean(xf, axis=-1, keepdims=True)
    var = jnp.mean(jnp.square(xf - mu), axis=-1, keepdims=True)
    return ((xf - mu) * lax.rsqrt(var + LN_EPS) * g.astype(jnp.float32)
            + b.astype(jnp.float32)).astype(x.dtype)

def rms_norm(x, g):
    xf = x.astype(jnp.float32)
    y = xf * lax.rsqrt(jnp.mean(xf * xf, axis=-1, keepdims=True) + RMS_EPS)
    return (y * g.astype(jnp.float32)).astype(x.dtype)

def ada_mod(c, w, b):
    m = (jax.nn.silu(c) @ w + b)[:, None, :]
    shift, scale, gate = jnp.split(m, 3, axis=-1)
    return shift, scale, 1.0 + gate

def causal_dwconv(x, w, b):
    k_len, ch = w.shape
    y = lax.conv_general_dilated(
        x, w[:, None, :].astype(x.dtype), window_strides=(1,),
        padding=[(k_len - 1, 0)], dimension_numbers=('NWC', 'WIO', 'NWC'),
        feature_group_count=ch)
    return y + b

def rg_lru(x, w_a, b_a, w_x, b_x, lam):
    bn, sn, _ = x.shape
    xf = x.astype(jnp.float32)
    xb = xf.reshape(bn, sn, RG_BLOCKS, RG_BLOCK)
    r = jax.nn.sigmoid(jnp.einsum('bsni,nij->bsnj', xb, w_a.astype(jnp.float32)).reshape(bn, sn, RG_WIDTH) + b_a)
    i = jax.nn.sigmoid(jnp.einsum('bsni,nij->bsnj', xb, w_x.astype(jnp.float32)).reshape(bn, sn, RG_WIDTH) + b_x)
    log_a = RG_C * r * jax.nn.log_sigmoid(lam.astype(jnp.float32))
    a = jnp.exp(log_a)
    u = jnp.sqrt(-jnp.expm1(2.0 * log_a)) * (i * xf)

    def combine(left, right):
        a1, h1 = left
        a2, h2 = right
        return a1 * a2, a2 * h1 + h2

    _, h = lax.associative_scan(combine, (a, u), axis=1)
    return h.astype(x.dtype)

def gla_chunked(q, k, v, log_alpha):
    bn, sn, nh, dk = q.shape
    dv = v.shape[-1]
    n_chunks = sn // GLA_CHUNK

    def blocks(t):
        return t.astype(jnp.float32).reshape(bn, n_chunks, GLA_CHUNK, nh, t.shape[-1]).transpose(1, 0, 3, 2, 4)

    qc = blocks(q) * (dk ** -0.5)
    kc = blocks(k)
    vc = blocks(v)
    bcum = jnp.cumsum(blocks(log_alpha), axis=3)
    b_last = bcum[:, :, :, -1:, :]
    q_dec = qc * jnp.exp(bcum)
    k_dec = kc * jnp.exp(-bcum)
    k_end = kc * jnp.exp(b_last - bcum)
    causal = jnp.tril(jnp.ones((GLA_CHUNK, GLA_CHUNK), dtype=bool))
    att = jnp.where(causal, jnp.einsum('nbhtd,nbhsd->nbhts', q_dec, k_dec), 0.0)
    o_intra = jnp.einsum('nbhts,nbhsv->nbhtv', att, vc)
    kv = jnp.einsum('nbhsd,nbhsv->nbhdv', k_end, vc)
    decay = jnp.exp(b_last[:, :, :, 0, :])

    def step(state, inp):
        dcy, kv_n = inp
        return dcy[..., None] * state + kv_n, state

    _, s_prev = lax.scan(step, jnp.zeros((bn, nh, dk, dv), jnp.float32), (decay, kv))
    o = o_intra + jnp.einsum('nbhtd,nbhdv->nbhtv', q_dec, s_prev)
    return o.transpose(1, 0, 3, 2, 4).reshape(bn, sn, nh, dv).astype(q.dtype)

def even_mixer(u, w_in, conv_w, conv_b, rg_wa, rg_ba, rg_wx, rg_bx, rg_lam,
               gla_w_up, gla_b_up, gla_norm_g, w_out):
    bn, sn, _ = u.shape
    proj = u @ w_in
    s1 = RG_WIDTH
    s2 = s1 + RG_WIDTH
    s3 = s2 + GLA_KDIM
    s4 = s3 + GLA_KDIM
    s5 = s4 + GLA_VDIM
    s6 = s5 + GLA_VDIM
    xr, yr, q, k, v, g, zl = jnp.split(proj, [s1, s2, s3, s4, s5, s6], axis=-1)
    h = rg_lru(causal_dwconv(xr, conv_w, conv_b), rg_wa, rg_ba, rg_wx, rg_bx, rg_lam)
    rg_out = h * jax.nn.gelu(yr)
    log_alpha = jax.nn.log_sigmoid((zl @ gla_w_up + gla_b_up).astype(jnp.float32)) / GLA_GATE_TAU
    o = gla_chunked(q.reshape(bn, sn, GLA_HEADS, GLA_HK),
                    k.reshape(bn, sn, GLA_HEADS, GLA_HK),
                    v.reshape(bn, sn, GLA_HEADS, GLA_HV),
                    log_alpha.reshape(bn, sn, GLA_HEADS, GLA_HK))
    o = rms_norm(o, gla_norm_g.reshape(GLA_HEADS, GLA_HV)) * jax.nn.silu(g).reshape(bn, sn, GLA_HEADS, GLA_HV)
    mix = jnp.concatenate([rg_out, o.reshape(bn, sn, GLA_VDIM)], axis=-1)
    return mix @ w_out

def fox_attention(u, w_in, b_f, q_norm_g, k_norm_g, w_out):
    bn, sn, _ = u.shape
    proj = u @ w_in
    q, k, v, g, fl = jnp.split(proj, [D_MODEL, 2 * D_MODEL, 3 * D_MODEL, 4 * D_MODEL], axis=-1)
    q = rms_norm(q.reshape(bn, sn, FOX_HEADS, FOX_HD), q_norm_g).transpose(0, 2, 1, 3) * (FOX_HD ** -0.5)
    k = rms_norm(k.reshape(bn, sn, FOX_HEADS, FOX_HD), k_norm_g).transpose(0, 2, 1, 3)
    v = v.reshape(bn, sn, FOX_HEADS, FOX_HD).transpose(0, 2, 1, 3)
    log_f = jax.nn.log_sigmoid((fl + b_f).astype(jnp.float32))
    f_cum = jnp.cumsum(log_f, axis=1).transpose(0, 2, 1)
    outs = []
    for blk in range(sn // FOX_BLOCK):
        t0 = blk * FOX_BLOCK
        t1 = t0 + FOX_BLOCK
        s = jnp.einsum('bhtd,bhsd->bhts', q[:, :, t0:t1], k[:, :, :t1]).astype(jnp.float32)
        s = s + f_cum[:, :, t0:t1, None] - f_cum[:, :, None, :t1]
        mask = (t0 + jnp.arange(FOX_BLOCK))[:, None] >= jnp.arange(t1)[None, :]
        p = jax.nn.softmax(jnp.where(mask, s, -jnp.inf), axis=-1)
        outs.append(jnp.einsum('bhts,bhsd->bhtd', p.astype(v.dtype), v[:, :, :t1]))
    o = jnp.concatenate(outs, axis=2).transpose(0, 2, 1, 3).reshape(bn, sn, D_MODEL)
    return (o * jax.nn.sigmoid(g)) @ w_out

def first_inputs(seed: int = 0) -> dict:
    key = jax.random.key(seed)
    ks = jax.random.split(key, 32)
    D = D_MODEL

    def nrm(i, shape, scale):
        return scale * jax.random.normal(ks[i], shape, jnp.float32)

    lam_a = jax.random.uniform(ks[13], (N_EVEN, RG_WIDTH), jnp.float32, 0.9, 0.999)
    lam_root = lam_a ** (1.0 / RG_C)
    ev_lam = jnp.log(lam_root) - jnp.log1p(-lam_root)
    return {
        "x": nrm(0, (BATCH, SEQ, D), 1.0),
        "c": nrm(1, (BATCH, D), 1.0),
        "ada_w": nrm(2, (DEPTH, 2, D, 3 * D), 0.1 * D ** -0.5),
        "ada_b": nrm(3, (DEPTH, 2, 3 * D), 0.02),
        "ln_g": 1.0 + nrm(4, (DEPTH, 2, D), 0.05),
        "ln_b": nrm(5, (DEPTH, 2, D), 0.02),
        "ev_w_in": nrm(6, (N_EVEN, D, EVEN_IN), D ** -0.5),
        "ev_conv_w": nrm(7, (N_EVEN, CONV_WIDTH, RG_WIDTH), CONV_WIDTH ** -0.5),
        "ev_conv_b": nrm(8, (N_EVEN, RG_WIDTH), 0.02),
        "ev_rg_wa": nrm(9, (N_EVEN, RG_BLOCKS, RG_BLOCK, RG_BLOCK), RG_BLOCK ** -0.5),
        "ev_rg_ba": nrm(10, (N_EVEN, RG_WIDTH), 0.02),
        "ev_rg_wx": nrm(11, (N_EVEN, RG_BLOCKS, RG_BLOCK, RG_BLOCK), RG_BLOCK ** -0.5),
        "ev_rg_bx": nrm(12, (N_EVEN, RG_WIDTH), 0.02),
        "ev_rg_lam": ev_lam,
        "ev_gla_w_up": nrm(14, (N_EVEN, GLA_LOWRANK, GLA_KDIM), GLA_LOWRANK ** -0.5),
        "ev_gla_b_up": nrm(15, (N_EVEN, GLA_KDIM), 0.02),
        "ev_gla_norm_g": 1.0 + nrm(16, (N_EVEN, GLA_VDIM), 0.05),
        "ev_w_out": nrm(17, (N_EVEN, MIX_WIDTH, D), BETA * MIX_WIDTH ** -0.5),
        "od_w_in": nrm(18, (N_ODD, D, ODD_IN), D ** -0.5),
        "od_b_f": 3.0 + 3.0 * jax.random.uniform(ks[19], (N_ODD, FOX_HEADS), jnp.float32),
        "od_q_norm_g": 1.0 + nrm(20, (N_ODD, FOX_HD), 0.05),
        "od_k_norm_g": 1.0 + nrm(21, (N_ODD, FOX_HD), 0.05),
        "od_w_out": nrm(22, (N_ODD, D, D), BETA * D ** -0.5),
        "mlp_w1": nrm(23, (DEPTH, D, D_FF), D ** -0.5),
        "mlp_b1": nrm(24, (DEPTH, D_FF), 0.02),
        "mlp_w2": nrm(25, (DEPTH, D_FF, D), BETA * D_FF ** -0.5),
        "mlp_b2": nrm(26, (DEPTH, D), 0.02),
    }

def first_block(x, c, ada_w, ada_b, ln_g, ln_b,
              ev_w_in, ev_conv_w, ev_conv_b, ev_rg_wa, ev_rg_ba, ev_rg_wx, ev_rg_bx, ev_rg_lam,
              ev_gla_w_up, ev_gla_b_up, ev_gla_norm_g, ev_w_out,
              od_w_in, od_b_f, od_q_norm_g, od_k_norm_g, od_w_out,
              mlp_w1, mlp_b1, mlp_w2, mlp_b2):
    for layer in range(DEPTH):
        shift, scale, gate = ada_mod(c, ada_w[layer, 0], ada_b[layer, 0])
        u = x * (1.0 + scale) + shift
        if layer % 2 == 0:
            e = layer // 2
            y = even_mixer(u, ev_w_in[e], ev_conv_w[e], ev_conv_b[e], ev_rg_wa[e], ev_rg_ba[e],
                           ev_rg_wx[e], ev_rg_bx[e], ev_rg_lam[e], ev_gla_w_up[e], ev_gla_b_up[e],
                           ev_gla_norm_g[e], ev_w_out[e])
        else:
            o = layer // 2
            y = fox_attention(u, od_w_in[o], od_b_f[o], od_q_norm_g[o], od_k_norm_g[o], od_w_out[o])
        x = layer_norm(ALPHA * x + gate * y, ln_g[layer, 0], ln_b[layer, 0])
        shift, scale, gate = ada_mod(c, ada_w[layer, 1], ada_b[layer, 1])
        u = x * (1.0 + scale) + shift
        y = jnp.square(jax.nn.relu(u @ mlp_w1[layer] + mlp_b1[layer])) @ mlp_w2[layer] + mlp_b2[layer]
        x = layer_norm(ALPHA * x + gate * y, ln_g[layer, 1], ln_b[layer, 1])
    return x


HEAD_DIM = 64
ATTN_SCALE = HEAD_DIM ** -0.5
ROPE_THETA = 10000.0
Q_BLOCK = 128
NEG_INF = -1e30
NORM_EPS = 1e-6

A_HEADS = D_MODEL // (4 * HEAD_DIM)
A_KV_HEADS = max(1, A_HEADS // 2)
A_WINDOW = 128

B_HEADS = D_MODEL // (4 * HEAD_DIM)
B_KV_HEADS = 1
CMP_STRIDE = 16
CMP_LEN = 2 * CMP_STRIDE
CMP_HIDDEN = 4 * HEAD_DIM
SLC_LEN = 64
SLC_TOPK = 16
NSA_WINDOW = 512
SLC_FORCED_SCORE = 1e9

C_HEAD_DIM = 128
C_HEADS = D_MODEL // (2 * C_HEAD_DIM)
GDN_CHUNK = 64

D_FF_RAW = -(-8 * D_MODEL // 3)
D_FF_2 = -(-D_FF_RAW // 256) * 256

A_Q = A_HEADS * HEAD_DIM
A_KV = A_KV_HEADS * HEAD_DIM
B_Q = B_HEADS * HEAD_DIM
B_KV = B_KV_HEADS * HEAD_DIM
B_GATES = 3 * B_HEADS
C_QK = C_HEADS * C_HEAD_DIM
MIX_WIDTH_2 = A_Q + B_Q + C_QK
IN_SPLITS = (A_Q, A_KV, A_KV, B_Q, B_KV, B_KV, B_KV, B_KV, B_KV, B_KV, B_GATES, 3 * C_QK, C_QK, C_HEADS, C_HEADS)
IN_WIDTH = sum(IN_SPLITS)


def rms_norm_2(x, gain):
    xf = x.astype(jnp.float32)
    y = xf * lax.rsqrt(jnp.mean(xf * xf, axis=-1, keepdims=True) + NORM_EPS)
    return (y * gain.astype(jnp.float32)).astype(x.dtype)

def l2norm(x):
    return x * lax.rsqrt(jnp.sum(x * x, axis=-1, keepdims=True) + NORM_EPS)

def rope_tables(seq, dim):
    inv = 1.0 / (ROPE_THETA ** (jnp.arange(0, dim, 2, dtype=jnp.float32) / dim))
    ang = jnp.arange(seq, dtype=jnp.float32)[:, None] * inv[None, :]
    return jnp.cos(ang), jnp.sin(ang)

def apply_rope(x, cos, sin):
    x1, x2 = jnp.split(x.astype(jnp.float32), 2, axis=-1)
    c = cos[None, :, None, :]
    s = sin[None, :, None, :]
    return jnp.concatenate([x1 * c - x2 * s, x2 * c + x1 * s], axis=-1).astype(x.dtype)

def banded_attention(q, k, v, window, sink=None):
    B, S, H, d = q.shape
    Hkv = k.shape[2]
    G = H // Hkv
    nb = S // Q_BLOCK
    n_prev = window // Q_BLOCK
    span = (n_prev + 1) * Q_BLOCK
    pad = ((0, 0), (window, 0), (0, 0), (0, 0))
    kb = jnp.pad(k, pad).reshape(B, nb + n_prev, Q_BLOCK, Hkv, d)
    vb = jnp.pad(v, pad).reshape(B, nb + n_prev, Q_BLOCK, Hkv, d)
    k_ctx = jnp.concatenate([kb[:, j:j + nb] for j in range(n_prev + 1)], axis=2)
    v_ctx = jnp.concatenate([vb[:, j:j + nb] for j in range(n_prev + 1)], axis=2)
    qb = q.reshape(B, nb, Q_BLOCK, Hkv, G, d)
    s = jnp.einsum('bnqhgd,bnkhd->bnhgqk', qb, k_ctx, preferred_element_type=jnp.float32) * ATTN_SCALE
    q_rel = jnp.arange(Q_BLOCK)[:, None]
    k_rel = jnp.arange(span)[None, :] - window
    band = (k_rel <= q_rel) & (k_rel > q_rel - window)
    in_seq = (jnp.arange(nb)[:, None] * Q_BLOCK + k_rel) >= 0
    mask = band[None, :, :] & in_seq[:, None, :]
    s = jnp.where(mask[None, :, None, None], s, NEG_INF)
    if sink is None:
        p = jax.nn.softmax(s, axis=-1)
    else:
        sink_col = jnp.broadcast_to(sink.astype(jnp.float32).reshape(1, 1, Hkv, G, 1, 1), s.shape[:-1] + (1,))
        p = jax.nn.softmax(jnp.concatenate([s, sink_col], axis=-1), axis=-1)[..., :-1]
    o = jnp.einsum('bnhgqk,bnkhd->bnqhgd', p.astype(v.dtype), v_ctx)
    return o.reshape(B, S, H, d)

def compress_tokens(x, w1, w2, pe):
    B, S, Hkv, d = x.shape
    strides = x.reshape(B, S // CMP_STRIDE, CMP_STRIDE, Hkv, d)
    win = jnp.concatenate([strides[:, :-1], strides[:, 1:]], axis=2) + pe[:, None, :]
    flat = win.transpose(0, 1, 3, 2, 4).reshape(B, S // CMP_STRIDE - 1, Hkv, CMP_LEN * d)
    return jax.nn.silu(flat @ w1) @ w2

def nsa_mixer(q, k_cmp_in, v_cmp_in, k_slc, v_slc, k_win, v_win, gate_logits, cos, sin,
              cmp_k_w1, cmp_k_w2, cmp_v_w1, cmp_v_w2, cmp_pe_k, cmp_pe_v):
    B, S, H, d = q.shape
    Hkv = k_slc.shape[2]
    G = H // Hkv
    n_cmp = S // CMP_STRIDE - 1
    n_slc = S // SLC_LEN
    nb = S // Q_BLOCK
    ratio = SLC_LEN // CMP_STRIDE
    top_k = min(SLC_TOPK, n_slc)

    k_cmp = compress_tokens(k_cmp_in, cmp_k_w1, cmp_k_w2, cmp_pe_k)
    v_cmp = compress_tokens(v_cmp_in, cmp_v_w1, cmp_v_w2, cmp_pe_v)
    q_rot = apply_rope(q, cos, sin)
    ks_blocks = apply_rope(k_slc, cos, sin).reshape(B, n_slc, SLC_LEN, Hkv, d).transpose(0, 3, 1, 2, 4)
    vs_blocks = v_slc.reshape(B, n_slc, SLC_LEN, Hkv, d).transpose(0, 3, 1, 2, 4)
    cmp_end = jnp.arange(n_cmp) * CMP_STRIDE + (CMP_LEN - 1)
    blk_ids = jnp.arange(n_slc)
    gather = jax.vmap(jax.vmap(lambda blocks, ids: blocks[ids]))

    def block_fn(args):
        i, qb, qrb = args
        t = i * Q_BLOCK + jnp.arange(Q_BLOCK)
        s = jnp.einsum('bqhgd,bnhd->bhgqn', qb, k_cmp, preferred_element_type=jnp.float32) * ATTN_SCALE
        valid = cmp_end[None, :] <= t[:, None]
        p_cmp = jnp.where(valid, jax.nn.softmax(jnp.where(valid, s, NEG_INF), axis=-1), 0.0)
        o_cmp = jnp.einsum('bhgqn,bnhd->bqhgd', p_cmp.astype(v_cmp.dtype), v_cmp)
        imp = jnp.pad(p_cmp.sum(axis=2), ((0, 0), (0, 0), (0, 0), (0, ratio * n_slc - n_cmp)))
        imp = imp.reshape(B, Hkv, Q_BLOCK, n_slc, ratio)
        imp = imp.sum(-1) + jnp.pad(imp[..., :-1, -1], ((0, 0), (0, 0), (0, 0), (1, 0)))
        cur = (t // SLC_LEN)[:, None]
        forced = (blk_ids == 0) | (blk_ids == cur) | (blk_ids == cur - 1)
        causal = blk_ids * SLC_LEN <= t[:, None]
        score = jnp.where(forced, SLC_FORCED_SCORE, jnp.where(causal, imp, NEG_INF))
        _, idx = lax.top_k(score, top_k)
        kg = gather(ks_blocks, idx).reshape(B, Hkv, Q_BLOCK, top_k * SLC_LEN, d)
        vg = gather(vs_blocks, idx).reshape(B, Hkv, Q_BLOCK, top_k * SLC_LEN, d)
        kpos = (idx[..., None] * SLC_LEN + jnp.arange(SLC_LEN)).reshape(B, Hkv, Q_BLOCK, top_k * SLC_LEN)
        sel_ok = kpos <= t[None, None, :, None]
        s = jnp.einsum('bqhgd,bhqkd->bhgqk', qrb, kg, preferred_element_type=jnp.float32) * ATTN_SCALE
        p = jax.nn.softmax(jnp.where(sel_ok[:, :, None], s, NEG_INF), axis=-1)
        o_slc = jnp.einsum('bhgqk,bhqkd->bqhgd', p.astype(vg.dtype), vg)
        return o_cmp, o_slc

    def to_blocks(a):
        return a.reshape(B, nb, Q_BLOCK, Hkv, G, d).transpose(1, 0, 2, 3, 4, 5)

    def from_blocks(a):
        return a.transpose(1, 0, 2, 3, 4, 5).reshape(B, S, H, d)

    o_cmp, o_slc = lax.map(block_fn, (jnp.arange(nb), to_blocks(q), to_blocks(q_rot)))
    o_win = banded_attention(q_rot, apply_rope(k_win, cos, sin), v_win, NSA_WINDOW)
    gates = jax.nn.sigmoid(gate_logits.astype(jnp.float32)).reshape(B, S, 3, H, 1).astype(q.dtype)
    o = gates[:, :, 0] * from_blocks(o_cmp) + gates[:, :, 1] * from_blocks(o_slc) + gates[:, :, 2] * o_win
    return o.reshape(B, S, H * d)

def short_causal_conv(x, w):
    y = lax.conv_general_dilated(x, w[:, None, :].astype(x.dtype), window_strides=(1,),
                                 padding=[(CONV_WIDTH - 1, 0)], dimension_numbers=('NWC', 'WIO', 'NWC'),
                                 feature_group_count=x.shape[-1])
    return jax.nn.silu(y)

def gated_delta_net(qkv, a, b, z, conv_w, A_log, dt_bias, norm_w):
    B, S, _ = qkv.shape
    H, dk = C_HEADS, C_HEAD_DIM
    C = GDN_CHUNK
    nc = S // C
    f32 = jnp.float32
    q, k, v = jnp.split(short_causal_conv(qkv, conv_w).astype(f32), 3, axis=-1)
    q = l2norm(q.reshape(B, S, H, dk)) * (dk ** -0.5)
    k = l2norm(k.reshape(B, S, H, dk))
    v = v.reshape(B, S, H, dk)
    beta = jax.nn.sigmoid(b.astype(f32))
    g = -jnp.exp(A_log.astype(f32)) * jax.nn.softplus(a.astype(f32) + dt_bias.astype(f32))

    def chunk(t):
        return t.reshape(B, nc, C, H, dk).transpose(0, 3, 1, 2, 4)

    q, k, v = chunk(q), chunk(k), chunk(v)
    beta = beta.reshape(B, nc, C, H).transpose(0, 3, 1, 2)
    gc = jnp.cumsum(g.reshape(B, nc, C, H).transpose(0, 3, 1, 2), axis=-1)
    lower = jnp.tril(jnp.ones((C, C), dtype=bool))
    strict = jnp.tril(jnp.ones((C, C), dtype=bool), -1)
    decay = jnp.where(lower, jnp.exp(jnp.where(lower, gc[..., :, None] - gc[..., None, :], 0.0)), 0.0)
    k_beta = k * beta[..., None]
    a_mat = jnp.where(strict, jnp.einsum('bhncd,bhnsd->bhncs', k_beta, k) * decay, 0.0)
    rhs = jnp.concatenate([v * beta[..., None], k_beta * jnp.exp(gc)[..., None]], axis=-1)
    sol = lax.linalg.triangular_solve(a_mat + jnp.eye(C, dtype=f32), rhs, left_side=True, lower=True,
                                      unit_diagonal=True)
    u, w = sol[..., :dk], sol[..., dk:]
    qk = jnp.where(lower, jnp.einsum('bhncd,bhnsd->bhncs', q, k) * decay, 0.0)
    q_dec = q * jnp.exp(gc)[..., None]
    k_dec = k * jnp.exp(gc[..., -1:] - gc)[..., None]
    g_last = jnp.exp(gc[..., -1])

    def step(state, inp):
        u_c, w_c, qk_c, qd_c, kd_c, gl_c = inp
        v_new = u_c - jnp.einsum('bhcd,bhde->bhce', w_c, state)
        o_c = jnp.einsum('bhcd,bhde->bhce', qd_c, state) + jnp.einsum('bhcs,bhse->bhce', qk_c, v_new)
        state = state * gl_c[..., None, None] + jnp.einsum('bhcd,bhce->bhde', kd_c, v_new)
        return state, o_c

    xs = tuple(jnp.moveaxis(t, 2, 0) for t in (u, w, qk, q_dec, k_dec, g_last))
    _, o = lax.scan(step, jnp.zeros((B, H, dk, dk), f32), xs)
    o = o.transpose(1, 0, 3, 2, 4).reshape(B, S, H, dk)
    o = rms_norm_2(o, norm_w) * jax.nn.silu(z.reshape(B, S, H, dk).astype(f32))
    return o.reshape(B, S, H * dk).astype(z.dtype)

def hybrid_layer(x, c, cos, sin, norm_mix, norm_ffn, ada_w, ada_b, w_in, attn_sinks,
                 cmp_k_w1, cmp_k_w2, cmp_v_w1, cmp_v_w2, cmp_pe_k, cmp_pe_v,
                 conv_w, A_log, dt_bias, gdn_norm, w_out, w_gate_up, w_down):
    B, S, _ = x.shape
    mod = jax.nn.silu(c) @ ada_w + ada_b
    sh_m, sc_m, gt_m, sh_f, sc_f, gt_f = jnp.split(mod[:, None, :], 6, axis=-1)

    h = rms_norm_2(x, norm_mix) * (1 + sc_m) + sh_m
    points = np.cumsum(IN_SPLITS)[:-1].tolist()
    (aq, ak, av, bq, bkc, bvc, bks, bvs, bkw, bvw, bg, cqkv, cz, ca, cb) = jnp.split(h @ w_in, points, axis=-1)

    def heads(t, n):
        return t.reshape(B, S, n, -1)

    o_a = banded_attention(apply_rope(heads(aq, A_HEADS), cos, sin), apply_rope(heads(ak, A_KV_HEADS), cos, sin),
                           heads(av, A_KV_HEADS), A_WINDOW, attn_sinks).reshape(B, S, A_Q)
    o_b = nsa_mixer(heads(bq, B_HEADS), heads(bkc, B_KV_HEADS), heads(bvc, B_KV_HEADS),
                    heads(bks, B_KV_HEADS), heads(bvs, B_KV_HEADS), heads(bkw, B_KV_HEADS), heads(bvw, B_KV_HEADS),
                    bg, cos, sin, cmp_k_w1, cmp_k_w2, cmp_v_w1, cmp_v_w2, cmp_pe_k, cmp_pe_v)
    o_c = gated_delta_net(cqkv, ca, cb, cz, conv_w, A_log, dt_bias, gdn_norm)
    x = x + gt_m * (jnp.concatenate([o_a, o_b, o_c], axis=-1) @ w_out)

    h = rms_norm_2(x, norm_ffn) * (1 + sc_f) + sh_f
    gate, up = jnp.split(h @ w_gate_up, 2, axis=-1)
    return x + gt_f * ((jax.nn.silu(gate) * up) @ w_down)

def second_inputs(seed: int = 0) -> dict:
    key = jax.random.key(seed)
    ks = jax.random.split(key, 24)
    f32 = jnp.float32
    L, D = DEPTH, D_MODEL
    cmp_in = CMP_LEN * HEAD_DIM

    def nrm(k, shape, scale):
        return jax.random.normal(k, shape, f32) * scale

    dt = jnp.exp(jax.random.uniform(ks[16], (L, C_HEADS), f32, math.log(1e-3), math.log(1e-1)))
    return {
        'x': nrm(ks[0], (BATCH, SEQ, D), 1.0),
        'c': nrm(ks[1], (BATCH, D), 1.0),
        'norm_mix': 1.0 + nrm(ks[2], (L, D), 0.1),
        'norm_ffn': 1.0 + nrm(ks[3], (L, D), 0.1),
        'ada_w': nrm(ks[4], (L, D, 6 * D), 0.5 * D ** -0.5),
        'ada_b': nrm(ks[5], (L, 6 * D), 0.01),
        'w_in': nrm(ks[6], (L, D, IN_WIDTH), D ** -0.5),
        'attn_sinks': nrm(ks[7], (L, A_HEADS), 1.0),
        'cmp_k_w1': nrm(ks[8], (L, cmp_in, CMP_HIDDEN), cmp_in ** -0.5),
        'cmp_k_w2': nrm(ks[9], (L, CMP_HIDDEN, HEAD_DIM), CMP_HIDDEN ** -0.5),
        'cmp_v_w1': nrm(ks[10], (L, cmp_in, CMP_HIDDEN), cmp_in ** -0.5),
        'cmp_v_w2': nrm(ks[11], (L, CMP_HIDDEN, HEAD_DIM), CMP_HIDDEN ** -0.5),
        'cmp_pe_k': nrm(ks[12], (L, CMP_LEN, HEAD_DIM), 0.1),
        'cmp_pe_v': nrm(ks[13], (L, CMP_LEN, HEAD_DIM), 0.1),
        'gdn_conv_w': nrm(ks[14], (L, CONV_WIDTH, 3 * C_QK), CONV_WIDTH ** -0.5),
        'gdn_A_log': jnp.log(jax.random.uniform(ks[15], (L, C_HEADS), f32, 1.0, 16.0)),
        'gdn_dt_bias': dt + jnp.log(-jnp.expm1(-dt)),
        'gdn_norm': 1.0 + nrm(ks[17], (L, C_HEAD_DIM), 0.1),
        'w_out': nrm(ks[18], (L, MIX_WIDTH_2, D), MIX_WIDTH_2 ** -0.5),
        'w_gate_up': nrm(ks[19], (L, D, 2 * D_FF_2), D ** -0.5),
        'w_down': nrm(ks[20], (L, D_FF_2, D), D_FF_2 ** -0.5),
        'final_norm': 1.0 + nrm(ks[21], (D,), 0.1),
    }

def second_block(x, c, norm_mix, norm_ffn, ada_w, ada_b, w_in, attn_sinks, cmp_k_w1, cmp_k_w2, cmp_v_w1,
              cmp_v_w2, cmp_pe_k, cmp_pe_v, gdn_conv_w, gdn_A_log, gdn_dt_bias, gdn_norm, w_out,
              w_gate_up, w_down, final_norm):
    cos, sin = rope_tables(x.shape[1], HEAD_DIM)
    for l in range(DEPTH):
        x = hybrid_layer(x, c, cos, sin, norm_mix[l], norm_ffn[l], ada_w[l], ada_b[l], w_in[l], attn_sinks[l],
                         cmp_k_w1[l], cmp_k_w2[l], cmp_v_w1[l], cmp_v_w2[l], cmp_pe_k[l], cmp_pe_v[l],
                         gdn_conv_w[l], gdn_A_log[l], gdn_dt_bias[l], gdn_norm[l], w_out[l],
                         w_gate_up[l], w_down[l])
    return rms_norm_2(x, final_norm)


def setup_inputs(seed=0):
    out = dict(first_inputs(seed))
    for name, value in second_inputs(seed + 1).items():
        if name != "x":
            out[name + "_2"] = value
    return out


def reference(
    x, c, ada_w, ada_b, ln_g, ln_b, ev_w_in, ev_conv_w, ev_conv_b, ev_rg_wa, ev_rg_ba, ev_rg_wx,
    ev_rg_bx, ev_rg_lam, ev_gla_w_up, ev_gla_b_up, ev_gla_norm_g, ev_w_out, od_w_in, od_b_f,
    od_q_norm_g, od_k_norm_g, od_w_out, mlp_w1, mlp_b1, mlp_w2, mlp_b2, c_2, norm_mix_2,
    norm_ffn_2, ada_w_2, ada_b_2, w_in_2, attn_sinks_2, cmp_k_w1_2, cmp_k_w2_2, cmp_v_w1_2,
    cmp_v_w2_2, cmp_pe_k_2, cmp_pe_v_2, gdn_conv_w_2, gdn_A_log_2, gdn_dt_bias_2, gdn_norm_2,
    w_out_2, w_gate_up_2, w_down_2, final_norm_2,
):
    x = first_block(
        x, c, ada_w, ada_b, ln_g, ln_b, ev_w_in, ev_conv_w, ev_conv_b, ev_rg_wa, ev_rg_ba,
        ev_rg_wx, ev_rg_bx, ev_rg_lam, ev_gla_w_up, ev_gla_b_up, ev_gla_norm_g, ev_w_out,
        od_w_in, od_b_f, od_q_norm_g, od_k_norm_g, od_w_out, mlp_w1, mlp_b1, mlp_w2, mlp_b2,
    )
    return second_block(
        x, c_2, norm_mix_2, norm_ffn_2, ada_w_2, ada_b_2, w_in_2, attn_sinks_2, cmp_k_w1_2,
        cmp_k_w2_2, cmp_v_w1_2, cmp_v_w2_2, cmp_pe_k_2, cmp_pe_v_2, gdn_conv_w_2, gdn_A_log_2,
        gdn_dt_bias_2, gdn_norm_2, w_out_2, w_gate_up_2, w_down_2, final_norm_2,
    )


_drawn_inputs = setup_inputs


def setup_inputs(seed=0):
    import zlib

    import numpy as np

    out = dict(_drawn_inputs(seed))
    spreads = {}
    factors = {'ev_conv_b': 3.51,
     'ev_rg_ba': 54.325,
     'ev_rg_bx': 37.568,
     'ev_gla_w_up': 3.088,
     'ev_gla_b_up': 8.0,
     'ev_gla_norm_g': 6.621,
     'od_b_f': 37.488,
     'od_q_norm_g': 8.0,
     'od_k_norm_g': 8.0,
     'mlp_b1': 3.945,
     'mlp_b2': 2.772,
     'ada_b_2': 3.769,
     'attn_sinks_2': 8.0,
     'cmp_k_w1_2': 4.316,
     'cmp_k_w2_2': 4.387,
     'cmp_pe_k_2': 8.0,
     'cmp_pe_v_2': 8.0,
     'gdn_norm_2': 2.7}
    for name, (base, spread) in spreads.items():
        noise = np.random.default_rng([zlib.crc32(name.encode()), seed]).standard_normal(out[name].shape)
        drawn = base * np.exp(spread * noise) if base else spread * noise
        out[name] = jnp.asarray(drawn.astype(out[name].dtype))
    for name, factor in factors.items():
        out[name] = (out[name] * factor).astype(out[name].dtype)
    return out
```

```python
import numpy as np
import concourse.bass as bass
from concourse import mybir
from concourse.alu_op_type import AluOpType as ALU

P = 128
D = 1024
T = 512
KT = D // P
NTB = T // P
RING = 8
BODY = RING
F32 = mybir.dt.float32
I32 = mybir.dt.int32
ACT = mybir.ActivationFunctionType
AXX = mybir.AxisListType.X
NEG = -1e30

L1 = 2
RGW = 512
GLA_CH = 64
ALPHA = float((2 * L1) ** 0.25)
FF1 = 4096
FOX_H = 16
L2 = 2
FF2 = 2816
FF2_T = FF2 // P
N_CMP = T // 16 - 1
GH = 4



class Columns:

    def __init__(self, items):
        self.at, self.n = {}, 0
        for name, width in items:
            self.at[name] = (self.n, width)
            self.n += width


CONST = Columns([("ident", 128), ("ones", 128), ("mean", 128), ("one64", 128), ("mean64", 128), ("tri", 128),
                 ("rot", 128), ("causal", 128), ("band", 128), ("decay_mask", 128), ("strict", 128),
                 ("levels", 6 * 128), ("gla_mask", 64), ("chunk_reset", T), ("cos", T), ("sin", T),
                 ("cmp_add", NTB * N_CMP), ("cmp_mul", NTB * N_CMP), ("head_row", FOX_H * 128)])
VEC1 = Columns([("c", 8), ("ada_b", 4 * 24), ("ln_g", 32), ("ln_b", 32), ("conv_w", 16), ("conv_b", 4),
                ("rg_ba", 4), ("rg_bx", 4), ("rg_lam", 4), ("gla_b", 2), ("gla_g", 4), ("gla_up", 256),
                ("fox_bf", 1), ("fox_qg", 1), ("fox_kg", 1), ("mlp_b1", 64), ("mlp_b2", 16), ("c2", 8),
                ("final", 8)])
VEC2 = Columns([("ada_b", 48), ("norm_mix", 8), ("norm_ffn", 8), ("conv_w", 48), ("gdn_norm", 1), ("sinks", 4),
                ("A_log", 4), ("dt_bias", 4), ("pe_k", 16), ("pe_v", 16)])


def constants():
    out = np.zeros((P, CONST.n), np.float32)

    def put(name, a, rows=P):
        c, w = CONST.at[name]
        out[:rows, c:c + w] = np.asarray(a, np.float32).reshape(rows, w)

    r, c = np.arange(P)[:, None], np.arange(P)[None, :]
    same = r // 64 == c // 64
    put("ident", r == c)
    put("ones", np.ones((P, P)))
    put("mean", np.full((P, P), 1.0 / D))
    put("one64", same)
    put("mean64", same / 64.0)
    put("tri", same & (r <= c))
    rot = np.zeros((P, P))
    for h in (0, 64):
        for d in range(32):
            rot[h + 32 + d, h + d] = -1.0
            rot[h + d, h + 32 + d] = 1.0
    put("rot", rot)
    put("causal", np.where(c <= r, 0.0, NEG))
    put("band", np.where(c > r, 0.0, NEG))
    put("decay_mask", np.where(same & (r <= c), 0.0, NEG))
    put("strict", same & (r < c))
    put("levels", np.stack([((c >> k) & 1 == 1) & ((r >> k) & 1 == 0) & (r >> (k + 1) == c >> (k + 1))
                            for k in range(6)], 1))
    put("gla_mask", np.tile(np.triu(np.ones((64, 64))), (2, 1)))
    t = np.arange(T)
    put("chunk_reset", np.broadcast_to(t % 64 != 0, (P, T)))
    inv = (1.0 / (10000.0 ** (np.arange(0, 64, 2, dtype=np.float32) / 64))).astype(np.float32)
    ang = (t.astype(np.float32)[None, :] * inv[:, None]).astype(np.float32)
    put("cos", np.tile(np.cos(ang), (4, 1)))
    put("sin", np.tile(np.sin(ang), (4, 1)))
    ends = np.arange(N_CMP) * 16 + 31
    valid = ends[None, None, :] <= (np.arange(NTB)[None, :, None] * P + np.arange(P)[:, None, None])
    put("cmp_add", np.where(valid, 0.0, NEG))
    put("cmp_mul", valid)
    put("head_row", np.repeat(np.eye(FOX_H), P, axis=1), FOX_H)
    return out


def columns_of(v):
    v = np.asarray(v)
    return np.ascontiguousarray(v.reshape(-1, P).T)


def pack(layout, values):
    out = np.zeros((P, layout.n), np.float32)
    for name, (c, w) in layout.at.items():
        a = values[name]
        out[:a.shape[0], c:c + w] = a
    return out


def panels_of(w):
    k, n = w.shape
    pk, pn = -k % D, -n % P
    if pk or pn:
        w = np.pad(w, ((0, pk), (0, pn)))
    kg, m = w.shape[0] // D, w.shape[1] // P
    return w.reshape(kg, KT, P, m, P).transpose(3, 0, 2, 1, 4).reshape(m * kg, P, KT * P)


def weight_stream(i):
    out = []

    def add(w):
        out.append(panels_of(w))

    def mlp(l):
        add(i["mlp_w1"][l])
        add(i["mlp_w2"][l])

    add(i["ada_w"][0, 0])
    ev = i["ev_w_in"][0]
    add(ev)
    wa, wx = i["ev_rg_wa"][0], i["ev_rg_wx"][0]
    rg = np.zeros((P, 8, P), np.float32)
    for g, w in enumerate((wa, wx)):
        for b in range(8):
            o = 64 * (b % 2)
            rg[o:o + 64, 4 * g + b // 2, o:o + 64] = w[b]
    out.append(rg.reshape(1, P, KT * P))
    add(i["ev_w_out"][0])
    add(i["ada_w"][0, 1])
    mlp(0)
    add(i["ada_w"][1, 0])
    od = i["od_w_in"][0]
    add(od[:, 4 * D:])
    for hp in range(KT):
        for s in range(4):
            add(od[:, s * D + hp * P:s * D + hp * P + P])
    add(i["od_w_out"][0])
    add(i["ada_w"][1, 1])
    mlp(1)
    for l in range(L2):
        w = i["w_in_2"][l]
        add(i["ada_w_2"][l])
        add(w[:, 0:384])
        add(w[:, 512:768])
        for a, b in ((768, 768), (832, 832), (896, 1024)):
            add(np.concatenate([w[:, a:a + 64], w[:, b:b + 64]], 1))
        add(w[:, 384:512])
        add(np.concatenate([w[:, 960:1024], w[:, 1088:1152]], 1))
        add(np.concatenate([w[:, 1152:1164], w[:, 3212:3220]], 1))
        add(i["cmp_k_w1_2"][l])
        add(i["cmp_v_w1_2"][l])
        add(np.concatenate([i["cmp_k_w2_2"][l], i["cmp_v_w2_2"][l]], 1))
        add(w[:, 1164:3212])
        add(i["w_out_2"][l])
        gu = i["w_gate_up_2"][l]
        for m in range(FF2_T):
            add(gu[:, m * P:m * P + P])
            add(gu[:, FF2 + m * P:FF2 + m * P + P])
        add(i["w_down_2"][l])
    return np.concatenate(out)


def vectors1(i):
    two = lambda g: np.concatenate([g, g])[:, None]
    return pack(VEC1, {
        "c": columns_of(i["c"]), "ada_b": columns_of(i["ada_b"]), "ln_g": columns_of(i["ln_g"]),
        "ln_b": columns_of(i["ln_b"]), "conv_w": columns_of(i["ev_conv_w"]), "conv_b": columns_of(i["ev_conv_b"]),
        "rg_ba": columns_of(i["ev_rg_ba"]), "rg_bx": columns_of(i["ev_rg_bx"]), "rg_lam": columns_of(i["ev_rg_lam"]),
        "gla_b": columns_of(i["ev_gla_b_up"]), "gla_g": columns_of(i["ev_gla_norm_g"]), "gla_up": i["ev_gla_w_up"][0],
        "fox_bf": i["od_b_f"].reshape(FOX_H, 1), "fox_qg": two(i["od_q_norm_g"][0]), "fox_kg": two(i["od_k_norm_g"][0]),
        "mlp_b1": columns_of(i["mlp_b1"]), "mlp_b2": columns_of(i["mlp_b2"]), "c2": columns_of(i["c_2"]),
        "final": columns_of(i["final_norm_2"])})


def vectors2(i, l):
    rows = lambda v: np.broadcast_to(v[None, :], (P, v.shape[0]))
    return pack(VEC2, {
        "ada_b": columns_of(i["ada_b_2"][l]), "norm_mix": columns_of(i["norm_mix_2"][l]),
        "norm_ffn": columns_of(i["norm_ffn_2"][l]), "conv_w": columns_of(i["gdn_conv_w_2"][l]),
        "gdn_norm": columns_of(i["gdn_norm_2"][l]), "sinks": rows(i["attn_sinks_2"][l]),
        "A_log": rows(i["gdn_A_log_2"][l]), "dt_bias": rows(i["gdn_dt_bias_2"][l]),
        "pe_k": columns_of(i["cmp_pe_k_2"][l]), "pe_v": columns_of(i["cmp_pe_v_2"][l])})




class Count:

    def __init__(self, handle):
        self.handle, self.const, self.terms = handle, 0, ()

    def token(self):
        return (self, self.const, self.terms)


class Engine:

    def __init__(self, prog, eng, sem, chained):
        self.prog, self.eng, self.sem, self.chained, self.seen = prog, eng, sem, chained, {}

    def wait(self, *tokens):
        for t in tokens:
            if isinstance(t, list):
                self.wait(*t)
                continue
            sem, const, terms = t
            known = [x[0] for x in self.prog.loops]
            assert all(x[0] in known for x in terms), "a token of a loop that has ended"
            if const == 0 and not terms:
                continue
            old = self.seen.get(id(sem))
            if old is not None and old[1] == terms and old[0] >= const:
                continue
            self.seen[id(sem)] = (const, terms)
            value = const
            for loop, k in terms:
                if k:
                    value = loop.i * k + value
            self.eng.wait_ge(sem.handle, value)

    def done(self, ins, sem=None, by=1):
        sem = sem or self.sem
        ins.then_inc(sem.handle, by)
        sem.const += by
        return sem.token()

    def __call__(self, op, *args, after=(), **kw):
        if self.chained:
            self.wait(self.sem.token())
        self.wait(*after)
        return self.done(op(*args, **kw))


class Loop:
    i = None


class Program:
    def __init__(self, nc, plan):
        self.nc, self.plan, self.found, self.loops = nc, plan, {}, []
        self.sems = []
        self.V = Engine(self, nc.vector, self.count("vector_done"), True)
        self.A = Engine(self, nc.scalar, self.count("scalar_done"), True)
        self.G = Engine(self, nc.gpsimd, self.count("gpsimd_done"), True)
        self.PE = Engine(self, nc.tensor, self.count("tensor_done"), False)
        self.used = self.count("panels_used")
        self.landed = [self.count(f"panel_landed_{k}") for k in range(RING)]
        self.panel = 0
        self.banks = [Bank(nc.alloc_psum_tensor(f"bank{k}", [P, 512], F32)) for k in range(8)]

    def count(self, name):
        c = Count(self.nc.alloc_semaphore(name))
        self.sems.append(c)
        return c

    def tensor_now(self):
        return [self.PE.sem.token(), self.used.token()]

    def engines_seen_clear(self):
        for e in (self.V, self.A, self.G, self.PE):
            e.seen = {}

    def loop(self, name, trips, fence=True):
        return LoopScope(self, name, trips, fence)

    def take(self):
        slot = self.panel % RING
        self.PE.wait(self.landed[slot].token_after(16))
        return self.ring[:, slot, :].rearrange("p (k c) -> p k c", k=KT)

    def release(self, matmul):
        slot = self.panel % RING
        self.landed[slot].const += 16
        self.panel += 1
        return self.PE.done(matmul, self.used)


def _token_after(self, by):
    return (self, self.const + by, self.terms)


Count.token_after = _token_after


class Bank:

    def __init__(self, t):
        self.t, self.free = t, []

    def __getitem__(self, k):
        return self.t[k]


class LoopScope:

    def __init__(self, prog, name, trips, fence):
        self.prog, self.name, self.trips, self.fence = prog, name, trips, fence

    def __enter__(self):
        p = self.prog
        self.scope = p.nc.Fori(0, self.trips, engines=(mybir.EngineType.PE, mybir.EngineType.Activation,
                                                       mybir.EngineType.DVE, mybir.EngineType.Pool))
        self.loop = Loop()
        self.loop.i = self.scope.__enter__()
        self.start = [c.const for c in p.sems]
        per = p.plan.get(self.name, [0] * len(p.sems))
        for c, k in zip(p.sems, per):
            c.terms = c.terms + ((self.loop, k),)
        p.loops.append((self.loop, self.name))
        self.first = p.panel
        p.engines_seen_clear()
        if self.fence:
            p.PE.wait(p.V.sem.token(), p.A.sem.token())
        for b in p.banks:
            b.free = []
        return self.loop.i

    def __exit__(self, *e):
        p = self.prog
        per = [c.const - s for c, s in zip(p.sems, self.start)]
        p.found[self.name] = per
        for c, s, k in zip(p.sems, self.start, per):
            c.const = s + k * self.trips
            c.terms = c.terms[:-1]
        p.loops.pop()
        used = p.panel - self.first
        assert used % RING == 0
        p.panel = self.first + used * self.trips
        self.scope.__exit__(None, None, None)
        p.engines_seen_clear()
        for b in p.banks:
            b.free = [p.V.sem.token(), p.A.sem.token()]




def build(nc, io, n_panels, plan):
    pr = Program(nc, plan)
    V, A, G, PE = pr.V, pr.A, pr.G, pr.PE
    v, s, g, pe = nc.vector, nc.scalar, nc.gpsimd, nc.tensor
    B = pr.banks

    def sb(name, shape, dt=F32):
        return nc.alloc_sbuf_tensor(name, shape, dt)

    X = sb("residual", [P, KT, T])
    U = sb("mixer_in", [P, KT, T])
    M = sb("mixer_out", [P, KT, T])
    H = sb("hidden", [P, 32, T])
    ring = sb("weight_ring", [P, RING, KT * P])
    pr.ring = ring
    C = sb("constants", [P, CONST.n])
    V1 = sb("vectors1", [P, VEC1.n])
    V2 = sb("vectors2", [P, VEC2.n])
    MOD = [sb("mod0", [P, 48]), sb("mod1", [P, 24])]
    SC = sb("silu_c", [P, 2, 8])
    COL = sb("columns", [P, 256])
    PB = sb("probs", [P, 2, T])
    PT = sb("probs_T", [P, 2, T])
    TMP = sb("tmp", [P, 2, T + 3])

    def const(name, rows=P):
        c, w = CONST.at[name]
        return C[0:rows, c:c + w]

    def vec1(name, a=0, b=None, rows=P):
        c, w = VEC1.at[name]
        return V1[0:rows, c + a:c + (w if b is None else b)]

    def vec2(name, a=0, b=None):
        c, w = VEC2.at[name]
        return V2[:, c + a:c + (w if b is None else b)]

    ident, ones = const("ident"), const("ones")

    loads = pr.count("loads")
    A.done(s.dma_start(H[:, 0:8, :].rearrange("p (b h) t -> p b (h t)", b=NTB),
                       io["x"].rearrange("(b p) d -> p b d", p=P)), loads, 16)
    A.done(s.dma_start(C[:, :], io["consts"]), loads, 16)
    A.done(s.dma_start(V1[:, :], io["vec1"]), loads, 16)
    all_loads = loads.token()

    stream = nc.sync
    whole = n_panels // RING
    with stream.Fori(0, whole) as i:
        for k in range(RING):
            stream.wait_ge(free_sem(pr), i * RING + k + 1)
            stream.dma_start(ring[:, k, :], io["stream"][i * RING + k]).then_inc(pr.landed[k].handle, 16)
    for n in range(whole * RING, n_panels):
        stream.wait_ge(free_sem(pr), n + 1)
        stream.dma_start(ring[:, n % RING, :], io["stream"][n]).then_inc(pr.landed[n % RING].handle, 16)

    PE.wait(all_loads)
    pe.sem_inc(pr.used.handle, RING)
    pr.used.const = RING

    def matmuls(bank_ap, pairs, after=(), start=True, stop=True, last=True, bank=None):
        if bank is not None:
            PE.wait(bank.free)
        PE.wait(*after)
        n = len(pairs)
        for k, (lhsT, rhs) in enumerate(pairs):
            ins = pe.matmul(bank_ap, lhsT, rhs, start=start and k == 0, stop=stop and k == n - 1)
        return PE.done(ins) if last else None

    gemm_turn = [0]

    def gemm(rhs, ktiles, evac, after=(), bank=None):
        if bank is None:
            bank = B[gemm_turn[0] % 2]
            gemm_turn[0] += 1
        PE.wait(bank.free)
        PE.wait(*after)
        k = 0
        while k < ktiles:
            w = pr.take()
            n = min(KT, ktiles - k)
            for j in range(n):
                ins = pe.matmul(bank[:, :], w[:, j, :], rhs(k + j), start=(k + j == 0), stop=(k + j == ktiles - 1))
            k += n
            tok = pr.release(ins)
        bank.free = evac(bank, tok)

    def gemm_tok(act, width, evac, after=()):
        bank = B[gemm_turn[0] % 2]
        gemm_turn[0] += 1
        PE.wait(bank.free)
        PE.wait(*after)
        w = pr.take()
        for b in range(NTB):
            for j in range(KT):
                ins = pe.matmul(bank[:, b * P:b * P + width], act(j)[:, b * P:b * P + P], w[:, j, 0:width],
                                start=(j == 0), stop=(j == KT - 1))
        tok = pr.release(ins)
        bank.free = evac(bank, tok)

    def ada(name, mod, silu_c, bias, groups):
        with pr.loop(name, groups) as i:
            for j in range(BODY):
                w = pr.take()
                for k in range(KT):
                    ins = pe.matmul(B[0][:, j:j + 1], w[:, k, :], silu_c[:, k:k + 1], start=(k == 0), stop=(k == KT - 1))
                tok = pr.release(ins)
            V(v.tensor_tensor, mod[:, bass.ds(i * BODY, BODY)], B[0][:, 0:BODY], bias(i), ALU.add, after=[tok])

    def ada_bias1(stage):
        c = VEC1.at["ada_b"][0] + 24 * stage
        return lambda i: V1[:, bass.ds(i * BODY + c, BODY)]

    def plus_one(ap):
        return V(v.tensor_scalar, ap, ap, 1.0, None, ALU.add)

    def modulate(mod):
        plus_one(mod[:, 8:24])
        t = V.sem.token()
        for k in range(KT):
            A(s.activation, U[:, k, :], X[:, k, :], ACT.Identity, bias=mod[:, k:k + 1], scale=mod[:, 8 + k:9 + k],
              after=[t] + pr.tensor_now())

    def stats(src, bank, sq):
        for k in range(KT):
            t = A(s.activation, sq(k), src(k), ACT.Square, after=[V.sem.token()] + (pr.tensor_now() if k == 0 else []))
            if k == 0:
                PE.wait(bank.free)
            PE.wait(t)
            ins = pe.matmul(bank[:, :], const("mean"), sq(k), start=(k == 0), stop=(k == KT - 1))
        return PE.done(ins)

    def inv_sqrt(bank, tok, eps, out, width=T):
        t = V(v.tensor_scalar, out, bank[:, 0:width], eps, None, ALU.add, after=[tok])
        t2 = A(s.activation, out, out, ACT.Sqrt, after=[t])
        bank.free = [t]
        return V(v.reciprocal, out, out, after=[t2])

    R = TMP[:, 0, 0:T]

    def layer_norm(gcol, bcol):
        bank = B[2]
        PE.wait(bank.free, V.sem.token(), A.sem.token())
        for k in range(KT):
            ins = pe.matmul(bank[:, :], const("mean"), X[:, k, :], start=(k == 0), stop=(k == KT - 1))
        t = PE.done(ins)
        for k in range(KT):
            V(v.tensor_tensor, X[:, k, :], X[:, k, :], bank[:, :], ALU.subtract, after=[t])
        bank.free = [V.sem.token()]
        tok = stats(lambda k: X[:, k, :], B[3], lambda k: H[:, k, :])
        inv_sqrt(B[3], tok, 1e-5, R)
        for k in range(KT):
            t = V(v.scalar_tensor_tensor, X[:, k, :], X[:, k, :], gcol[:, k:k + 1], R, ALU.mult, ALU.mult,
                  after=[A.sem.token()])
            A(s.activation, X[:, k, :], X[:, k, :], ACT.Identity, bias=bcol[:, k:k + 1], after=[t])

    def rms_norm_all(gain, shift, out):
        tok = stats(lambda k: X[:, k, :], B[3], lambda k: H[:, k, :])
        inv_sqrt(B[3], tok, 1e-6, R)
        for k in range(KT):
            t = V(v.scalar_tensor_tensor, out(k), X[:, k, :], gain[:, k:k + 1], R, ALU.mult, ALU.mult,
                  after=[A.sem.token()] + pr.tensor_now())
            if shift is not None:
                A(s.activation, out(k), out(k), ACT.Identity, bias=shift[:, k:k + 1], after=[t])

    def now():
        return [V.sem.token(), A.sem.token()]

    def softplus_neg(out, x, tmp, after=()):
        t = A(s.activation, tmp, x, ACT.Abs, after=list(after) + [V.sem.token()])
        A(s.activation, tmp, tmp, ACT.Exp, scale=-1.0)
        t = A(s.activation, tmp, tmp, ACT.Ln, bias=1.0)
        V(v.tensor_scalar, out, x, 0.0, None, ALU.min, after=[t])
        return V(v.tensor_tensor, out, tmp, out, ALU.subtract)

    def attention(items):
        n = len(items)
        held = [None] * n

        def scores(j):
            it = items[j]
            bank = B[2 + j % 2]
            PE.wait(bank.free)
            PE.wait(*it.get("after", ()))
            w = it["width"]
            ins = pe.matmul(bank[:, 0:w], it["q"], it["k"], start=True, stop=True)
            for m, (lhsT, rhs, c, cw) in enumerate(it["extra"]):
                ins = pe.matmul(bank[:, c:c + cw], lhsT, rhs, start=False, stop=True, skip_group_check=True)
            tok = PE.done(ins)
            c = 8 * (j % 4)
            nm, tot, es = COL[:, c:c + 1], COL[:, c + 1:c + 2], COL[:, c + 2:c + 3]
            probs = PB[:, j % 2, 0:w]
            t = V(v.tensor_reduce, nm, bank[:, 0:w], AXX, ALU.max, negate=True, after=[tok, A.sem.token()])
            if it.get("sink") is not None:
                V(v.tensor_scalar, es, it["sink"], -1.0, None, ALU.mult)
                t = V(v.tensor_tensor, nm, nm, es, ALU.min)
            t = A(s.activation, probs, bank[:, 0:w], ACT.Exp, bias=nm, accum_out=tot,
                  after=[t] + ([held[j - 2]] if j >= 2 else pr.tensor_now()))
            bank.free = [t]
            if it.get("sink") is not None:
                t = A(s.activation, es, it["sink"], ACT.Exp, bias=nm)
                V(v.tensor_tensor, tot, tot, es, ALU.add, after=[t])
            V(v.reciprocal, tot, tot, after=[t])
            if it.get("gate") is not None:
                V(v.tensor_tensor, tot, tot, it["gate"], ALU.mult)
            if it.get("valid") is not None:
                t = V(v.scalar_tensor_tensor, probs, probs, tot, it["valid"], ALU.mult, ALU.mult)
            else:
                t = V(v.tensor_scalar, probs, probs, tot, None, ALU.mult)
            it["ready"] = t

        def turn(j):
            it = items[j]
            bank = B[4 + j % 2]
            w = it["width"]
            PE.wait(bank.free, it["ready"])
            chunks = [(c, min(P, w - c)) for c in range(0, w, P)]
            for c, cw in chunks:
                ins = pe.transpose(bank[0:cw, c:c + P], PB[:, j % 2, c:c + cw], ident)
            tok = PE.done(ins)
            held[j] = tok
            rows = min(P, w)
            cols = P * len(chunks)
            after = [tok] + ([items[j - 2]["used"]] if j >= 2 else pr.tensor_now())
            if j % 2:
                t = V(v.tensor_copy, PT[0:rows, j % 2, 0:cols], bank[0:rows, 0:cols], after=after)
            else:
                t = A(s.activation, PT[0:rows, j % 2, 0:cols], bank[0:rows, 0:cols], ACT.Copy, after=after)
            bank.free = [t]
            it["turned"] = t

        def product(j):
            it = items[j]
            if it["start"]:
                PE.wait(it["bank"].free)
            PE.wait(it["turned"])
            m = len(it["v"])
            for c, lhsT in enumerate(it["v"]):
                rows = min(P, it["width"])
                ins = pe.matmul(it["out"], lhsT, PT[0:rows, j % 2, c * P:c * P + P],
                                start=it["start"] and c == 0, stop=it["stop"] and c == m - 1, skip_group_check=True)
            it["used"] = PE.done(ins)
            if it.get("evac"):
                it["bank"].free = it["evac"](it["used"])

        for j in range(n + 2):
            if j < n:
                scores(j)
            if 1 <= j <= n:
                turn(j - 1)
            if j >= 2:
                product(j - 2)

    for k in range(KT):
        bank = B[2 + k % 2]
        PE.wait(bank.free, all_loads)
        for b in range(NTB):
            ins = pe.transpose(bank[:, b * P:b * P + P],
                               H[:, 2 * b + k // 4, (k % 4) * P:(k % 4) * P + P], ident)
        tok = PE.done(ins)
        bank.free = [A(s.activation, X[:, k, :], bank[:, :], ACT.Copy, after=[tok, all_loads])]
    V.wait(all_loads)
    A.wait(all_loads)
    A(s.activation, SC[:, 0, :], vec1("c"), ACT.Silu)
    A(s.activation, SC[:, 1, :], vec1("c2"), ACT.Silu)
    PE.wait(A.sem.token())

    ada("ada0", MOD[0], SC[:, 0, :], ada_bias1(0), 3)
    modulate(MOD[0])
    u = lambda k: U[:, k, :]
    XR, YR, Q, K_, GG, VT = 0, 4, 8, 10, 12, 16
    ready = now()

    def conv4(src, tile, wcol, bias):
        V(v.tensor_scalar, tile, src[:, 0:T], wcol(0), bias, ALU.mult, ALU.add if bias is not None else ALU.bypass)
        for j in range(1, 4):
            t = V(v.scalar_tensor_tensor, tile, src[:, j:j + T], wcol(j), tile, ALU.mult, ALU.add)
        return t

    V(v.memset, TMP[:, :, 0:3], 0.0)
    for m in range(4):
        def evac(bank, tok, m=m):
            src = TMP[:, m % 2, :]
            t = A(s.activation, src[:, 3:3 + T], bank[:, :], ACT.Copy, after=[tok, V.sem.token()])
            V.wait(t)
            conv4(src, H[:, XR + m, :], lambda j: vec1("conv_w", 4 * j + m, 4 * j + m + 1), vec1("conv_b", m, m + 1))
            return [t]
        gemm(u, KT, evac, after=ready)
    for m in range(4):
        gemm(u, KT, lambda bank, tok, m=m: [A(s.activation, H[:, YR + m, :], bank[:, :], ACT.Copy, after=[tok])])
    for m in range(2):
        gemm(u, KT, lambda bank, tok, m=m: [A(s.activation, H[:, Q + m, :], bank[:, :], ACT.Copy, scale=0.125, after=[tok])])
    for m in range(2):
        gemm(u, KT, lambda bank, tok, m=m: [A(s.activation, H[:, K_ + m, :], bank[:, :], ACT.Copy, after=[tok])])
    vt = H[:, VT:VT + 4, :]
    for m in range(4):
        gemm_tok(u, P, lambda bank, tok, m=m: [A(s.activation, vt[:, :, m * P:m * P + P],
                 bank[:, :].rearrange("p (b c) -> p b c", b=NTB), ACT.Copy, after=[tok])])
    for m in range(4):
        gemm(u, KT, lambda bank, tok, m=m: [A(s.activation, H[:, GG + m, :], bank[:, :], ACT.Silu, after=[tok])])
    ZL = TMP[0:16, 0, 0:T]
    gemm(u, KT, lambda bank, tok: [A(s.activation, ZL, bank[0:16, :], ACT.Copy, after=[tok, V.sem.token()])])

    LS = COL[:, 64:68]
    softplus_neg(LS, vec1("rg_lam"), COL[:, 68:72])
    V(v.tensor_scalar, LS, LS, -8.0, None, ALU.mult)
    w = pr.take()
    PE.wait(*now())
    RT, IT, AT_, HT = 20, 22, 24, 26
    for m in range(4):
        e = m % 2
        for half, bank in ((0, B[2]), (1, B[3])):
            PE.wait(bank.free)
            ins = pe.matmul(bank[:, :], w[:, 4 * half + m, :], H[:, XR + m, :], start=True, stop=True)
            tok = pr.release(ins) if (m, half) == (3, 1) else PE.done(ins)
            dst = H[:, (RT, IT)[half] + e, :]
            bias = vec1(("rg_ba", "rg_bx")[half], m, m + 1)
            t = A(s.activation, dst, bank[:, :], ACT.Sigmoid, bias=bias, after=[tok, V.sem.token()])
            bank.free = [t]
        r, it_, a = H[:, RT + e, :], H[:, IT + e, :], H[:, AT_ + e, :]
        th = H[:, HT + e, :]
        V(v.tensor_tensor, it_, it_, H[:, XR + m, :], ALU.mult, after=[t])
        t = A(s.activation, a, r, ACT.Exp, scale=LS[:, m:m + 1], after=[V.sem.token()])
        t = A(s.activation, th, r, ACT.Tanh, scale=LS[:, m:m + 1])
        V(v.tensor_scalar, r, th, -1.0, 1.0, ALU.mult, ALU.add, after=[t])
        V(v.reciprocal, r, r)
        V(v.tensor_tensor, th, th, r, ALU.mult)
        t = A(s.activation, th, th, ACT.Sqrt, scale=-2.0, after=[V.sem.token()])
        V(v.tensor_tensor, it_, it_, th, ALU.mult, after=[t])
        V(v.tensor_tensor_scan, r, a, it_, 0.0, ALU.mult, ALU.add)
        y = H[:, YR + m, :]
        t = A(s.activation, th, y, ACT.Square, after=[V.sem.token()])
        V(v.tensor_scalar, th, th, 0.044715, 1.0, ALU.mult, ALU.add, after=[t])
        V(v.tensor_tensor, th, th, y, ALU.mult)
        t = A(s.activation, th, th, ACT.Sigmoid, scale=float(2.0 * np.sqrt(2.0 / np.pi)), after=[V.sem.token()])
        V(v.tensor_tensor, y, y, th, ALU.mult, after=[t])
        V(v.tensor_tensor, M[:, m, :], y, r, ALU.mult)

    EB, ENB, QD, KD, KE = 20, 22, 24, 26, 28
    for m in range(2):
        tok = matmuls(B[2 + m][:, :], [(vec1("gla_up", m * P, m * P + P, rows=16), ZL)], after=now(), bank=B[2 + m])
        la, bc = H[:, KD + m, :], H[:, KE + m, :]
        x = H[:, QD + m, :]
        t = A(s.activation, x, B[2 + m][:, :], ACT.Identity, bias=vec1("gla_b", m, m + 1), after=[tok, V.sem.token()])
        B[2 + m].free = [t]
        softplus_neg(la, x, bc)
        V(v.tensor_scalar, la, la, -1.0 / 16.0, None, ALU.mult)
        V(v.tensor_tensor_scan, bc, const("chunk_reset"), la, 0.0, ALU.mult, ALU.add)
        eb, enb, qd, kd = (H[:, z + m, :] for z in (EB, ENB, QD, KD))
        t = A(s.activation, eb, bc, ACT.Exp, after=[V.sem.token()])
        t = A(s.activation, enb, bc, ACT.Exp, scale=-1.0)
        V(v.tensor_tensor, qd, H[:, Q + m, :], eb, ALU.mult, after=[t])
        V(v.tensor_tensor, kd, H[:, K_ + m, :], enb, ALU.mult)
        bc3 = bc.rearrange("p (c t) -> p c t", t=GLA_CH)
        enb3 = enb.rearrange("p (c t) -> p c t", t=GLA_CH)
        V(v.tensor_tensor, enb3, bc3[:, :, GLA_CH - 1:GLA_CH].broadcast_to([P, 8, GLA_CH]), bc3, ALU.subtract)
        t = A(s.activation, enb, enb, ACT.Exp, after=[V.sem.token()])
        V(v.tensor_tensor, bc, H[:, K_ + m, :], enb, ALU.mult, after=[t])
    for m in range(2):
        bank = B[2 + m]
        PE.wait(bank.free, *now())
        for b in range(NTB):
            ins = pe.transpose(bank[:, b * P:b * P + P], H[:, KE + m, b * P:b * P + P], ident)
        tok = PE.done(ins)
        ket = H[:, 30:32, :].rearrange("p (b x) t -> p b (x t)", b=1)[:, 0, :].rearrange("p (b k) -> p b k", b=NTB)
        bank.free = [A(s.activation, ket[:, :, m * P:m * P + P], bank[:, :].rearrange("p (b c) -> p b c", b=NTB),
                       ACT.Copy, after=[tok])]
    ATT = TMP[:, 1, 0:4 * 64]
    S = TMP[:, 0, 0:2 * P].rearrange("p (m c) -> p m c", m=2)
    V(v.memset, ATT, 0.0, after=now())
    V(v.memset, S, 0.0, after=pr.tensor_now())
    OG = [Q, Q + 1, K_, K_ + 1]
    mask = const("gla_mask").bitcast(I32)
    for c in range(8):
        b, o = c // 2, 64 * (c % 2)
        tc_ = slice(c * 64, c * 64 + 64)
        PE.wait(B[4].free, B[5].free, B[6].free)
        PE.wait(*now())
        for h in range(4):
            hp, ho = h // 2, 64 * (h % 2)
            ins = pe.matmul(B[4 + h % 2][o:o + 64, hp * 64:hp * 64 + 64], H[ho:ho + 64, KD + hp, tc_],
                            H[ho:ho + 64, QD + hp, tc_], start=True, stop=True)
        t_att = PE.done(ins)
        for h in range(4):
            hp, ho = h // 2, 64 * (h % 2)
            ins = pe.matmul(B[6 + h % 2][ho:ho + 64, hp * P:hp * P + P], ket[o:o + 64, b, h * 64:h * 64 + 64],
                            vt[o:o + 64, b, h * P:h * P + P], start=True, stop=True)
        t_kv = PE.done(ins)
        for h in range(4):
            t = V(v.copy_predicated, ATT[o:o + 64, h * 64:h * 64 + 64], mask[o:o + 64, :],
                  B[4 + h % 2][o:o + 64, (h // 2) * 64:(h // 2) * 64 + 64], after=[t_att] + pr.tensor_now())
        B[4].free = B[5].free = [t]
        bank = B[2 + c % 2]
        PE.wait(bank.free, t)
        for h in range(4):
            hp, ho = h // 2, 64 * (h % 2)
            pe.matmul(bank[:, h * 64:h * 64 + 64], vt[o:o + 64, b, h * P:h * P + P],
                      ATT[o:o + 64, h * 64:h * 64 + 64], start=True, stop=True)
            ins = pe.matmul(B[4 + h % 2][:, 256 + hp * 64:320 + hp * 64], S[ho:ho + 64, hp, :],
                            H[ho:ho + 64, QD + hp, tc_], start=True, stop=True)
        t_o = PE.done(ins)
        for h in range(4):
            t = A(s.activation, H[:, OG[h], tc_], bank[:, h * 64:h * 64 + 64], ACT.Copy, after=[t_o, V.sem.token()])
        bank.free = [t]
        for h in range(4):
            hp = h // 2
            t = V(v.tensor_tensor, H[:, OG[h], tc_], H[:, OG[h], tc_], B[4 + h % 2][:, 256 + hp * 64:320 + hp * 64],
                  ALU.add, after=[A.sem.token()])
        B[4].free = B[5].free = [t]
        for h in range(4):
            hp, ho = h // 2, 64 * (h % 2)
            t = V(v.scalar_tensor_tensor, S[ho:ho + 64, hp, :], S[ho:ho + 64, hp, :],
                  H[ho:ho + 64, EB + hp, c * 64 + 63:c * 64 + 64],
                  B[6 + h % 2][ho:ho + 64, hp * P:hp * P + P], ALU.mult, ALU.add, after=[t_o, t_kv])
        B[6].free = B[7].free = [t]
    for h in range(4):
        o = H[:, OG[h], :]
        sq = H[:, QD + h % 2, :]
        bank = B[2 + h % 2]
        t = A(s.activation, sq, o, ACT.Square, after=[V.sem.token()] + pr.tensor_now())
        tok = matmuls(bank[:, :], [(ones, sq)], after=[t], bank=bank)
        rs = H[:, KD + h % 2, :]
        t = V(v.tensor_scalar, rs, bank[:, :], 1.0 / P, 1e-6, ALU.mult, ALU.add, after=[tok])
        bank.free = [t]
        t = A(s.activation, rs, rs, ACT.Sqrt, after=[t])
        V(v.reciprocal, rs, rs, after=[t])
        V(v.scalar_tensor_tensor, o, o, vec1("gla_g", h, h + 1), rs, ALU.mult, ALU.mult)
        V(v.tensor_tensor, M[:, 4 + h, :], o, H[:, GG + h, :], ALU.mult)

    def add_residual(mod, bias=None):
        def evac_of(m):
            def evac(bank, tok):
                tmp = TMP[:, m % 2, 0:T]
                gcol = mod[:, 16 + m:17 + m]
                if bias is None:
                    t = A(s.activation, tmp, bank[:, :], ACT.Copy, scale=gcol, after=[tok, V.sem.token()])
                else:
                    t = A(s.activation, tmp, bank[:, :], ACT.Identity, scale=gcol, bias=bias[:, m:m + 1],
                          after=[tok, V.sem.token()])
                V(v.scalar_tensor_tensor, X[:, m, :], X[:, m, :], ALPHA, tmp, ALU.mult, ALU.add, after=[t])
                return [t]
            return evac
        return evac_of

    def project(src, mod):
        ev = add_residual(mod)
        ready = now()
        for m in range(KT):
            gemm(src, KT, ev(m), after=ready)

    mix = lambda k: M[:, k, :]

    def mlp1(l, mod):
        modulate(mod)
        b1 = VEC1.at["mlp_b1"][0] + 32 * l
        with pr.loop(f"mlp_up{l}", FF1 // D) as i:
            for j in range(BODY):
                def evac(bank, tok, j=j):
                    h = H[:, bass.ds(i * BODY + j, 1), :].rearrange("p a t -> p (a t)")
                    t = A(s.activation, h, bank[:, :], ACT.Relu, bias=V1[:, bass.ds(i * BODY + (b1 + j), 1)], after=[tok])
                    V(v.tensor_tensor, h, h, h, ALU.mult, after=[t])
                    return [t]
                gemm(u, KT, evac, after=[A.sem.token()] if j == 0 else ())
        gb = COL[:, 72:80]
        V(v.tensor_tensor, gb, mod[:, 16:24], vec1("mlp_b2", 8 * l, 8 * l + 8), ALU.mult)
        ready = now()
        ev = add_residual(mod, gb)
        for m in range(KT):
            gemm(lambda k: H[:, k, :], FF1 // P, ev(m), after=ready)

    project(mix, MOD[0])
    ada("ada1", MOD[1], SC[:, 0, :], ada_bias1(1), 3)
    layer_norm(vec1("ln_g", 0, 8), vec1("ln_b", 0, 8))
    mlp1(0, MOD[1])
    ada("ada2", MOD[0], SC[:, 0, :], ada_bias1(2), 3)
    layer_norm(vec1("ln_g", 8, 16), vec1("ln_b", 8, 16))

    modulate(MOD[0])
    NF = H[0:FOX_H, 31, :]
    ready = now()

    def evac_f(bank, tok):
        z, tmp = TMP[0:FOX_H, 0, 0:T], TMP[0:FOX_H, 1, 0:T]
        t = A(s.activation, z, bank[0:FOX_H, :], ACT.Identity, bias=vec1("fox_bf", rows=FOX_H), after=[tok, V.sem.token()])
        softplus_neg(H[0:FOX_H, 30, :], z, tmp)
        V(v.tensor_tensor_scan, NF, const("ones", FOX_H)[:, 0:1].broadcast_to([FOX_H, T]), H[0:FOX_H, 30, :], 0.0,
          ALU.mult, ALU.add)
        return [t]
    gemm(u, KT, evac_f, after=ready)
    QG = COL[:, 80:81]
    V(v.tensor_scalar, QG, vec1("fox_qg"), 0.125, None, ALU.mult)
    with pr.loop("fox", KT // 2) as i:
        for half in range(2):
            q, k_, gt = H[:, 0, :], H[:, 1, :], H[:, 2, :]
            vtok = H[:, 3, :].rearrange("p (b c) -> p b c", b=NTB)
            sq, rs = H[:, 4, :], H[:, 5, :]
            for src, gain, dst in ((0, QG, q), (1, vec1("fox_kg"), k_)):
                def evac(bank, tok, gain=gain, dst=dst):
                    t = A(s.activation, dst, bank[:, :], ACT.Copy, after=[tok, V.sem.token()] + pr.tensor_now())
                    return [t]
                gemm(u, KT, evac)
            gemm_tok(u, P, lambda bank, tok: [A(s.activation, vtok, bank[:, :].rearrange("p (b c) -> p b c", b=NTB),
                                                ACT.Copy, after=[tok] + pr.tensor_now())])
            gemm(u, KT, lambda bank, tok: [A(s.activation, gt, bank[:, :], ACT.Sigmoid, after=[tok, V.sem.token()])])
            for gain, dst in ((QG, q), (vec1("fox_kg"), k_)):
                t = A(s.activation, sq, dst, ACT.Square, after=pr.tensor_now())
                tok = matmuls(B[2][:, :], [(const("mean64"), sq)], after=[t], bank=B[2])
                inv_sqrt(B[2], tok, 1e-6, rs)
                V(v.scalar_tensor_tensor, dst, dst, gain, rs, ALU.mult, ALU.mult)
            items = []
            for e in range(2):
                hr = slice(64 * e, 64 * e + 64)
                for b in range(NTB):
                    w_ = (b + 1) * P
                    items.append(dict(
                        q=q[hr, b * P:w_], k=k_[hr, 0:w_], width=w_, head=e,
                        extra=[(None, NF[:, 0:w_], 0, w_), (ident, const("causal"), b * P, P)],
                        v=[vtok[:, c, hr] for c in range(b + 1)], out=B[6][hr, b * P:w_], bank=B[6],
                        start=True, stop=True, after=now() if (e, b) == (0, 0) else ()))
            c0 = CONST.at["head_row"][0]
            sel = H[0:FOX_H, 6, 0:256]
            t = V(v.tensor_copy, sel, C[0:FOX_H, bass.ds(i * (4 * P) + (c0 + half * 2 * P), 2 * P)], after=pr.tensor_now())
            items[0]["after"] = now()
            for it in items:
                e = it["head"]
                it["extra"][0] = (sel[:, e * P:e * P + P],) + it["extra"][0][1:]

            def evac(tok):
                o = M[:, bass.ds(i * 2 + half, 1), :].rearrange("p a t -> p (a t)")
                return [V(v.tensor_tensor, o, B[6][:, :], gt, ALU.mult, after=[tok, A.sem.token()])]
            items[-1]["evac"] = evac
            attention(items)
    project(mix, MOD[0])
    ada("ada3", MOD[1], SC[:, 0, :], ada_bias1(3), 3)
    layer_norm(vec1("ln_g", 16, 24), vec1("ln_b", 16, 24))
    mlp1(1, MOD[1])
    layer_norm(vec1("ln_g", 24, 32), vec1("ln_b", 24, 32))

    mod = MOD[0]
    with pr.loop("hybrid", L2, fence=False) as l:
        vec_load = loads
        A.wait(V.sem.token(), *pr.tensor_now())
        tok = A.done(s.dma_start(V2[:, :], io["vec2"][l]), vec_load, 16)
        V(v.memset, COL[:, 88:89], 0.0, after=[tok])
        A(s.activation, COL[:, 89:90], V2[:, 0:1], ACT.Copy, after=[tok])
        ada("ada_h", mod, SC[:, 1, :], lambda i: V2[:, bass.ds(i * BODY, BODY)], 6)
        GM, GF = COL[:, 96:104], COL[:, 104:112]
        plus_one(mod[:, 8:16])
        plus_one(mod[:, 32:40])
        V(v.tensor_tensor, GM, mod[:, 8:16], vec2("norm_mix"), ALU.mult)
        V(v.tensor_tensor, GF, mod[:, 32:40], vec2("norm_ffn"), ALU.mult)
        rms_norm_all(GM, mod[:, 0:8], u)
        ready = now()
        AQ, AK, BQ, BQR, KC, VC, KSW = 0, 2, 3, 5, 7, 8, 9
        AV, VSW, SM, XK = 10, 11, 12, 13

        def rope(bank, tok, dst, scale, raw=None):
            x = raw if raw is not None else TMP[:, 0, 0:T]
            t = A(s.activation, x, bank[:, :], ACT.Copy, scale=scale, after=[tok, V.sem.token()] + pr.tensor_now())
            tok2 = matmuls(B[2][:, :], [(const("rot"), x)], after=[t], bank=B[2])
            V(v.tensor_tensor, TMP[:, 1, 0:T], B[2][:, :], const("sin"), ALU.mult, after=[tok2])
            B[2].free = [V.sem.token()]
            V(v.tensor_tensor, dst, x, const("cos"), ALU.mult)
            V(v.tensor_tensor, dst, dst, TMP[:, 1, 0:T], ALU.add)
            return [t]

        for m in range(2):
            gemm(u, KT, lambda bank, tok, m=m: rope(bank, tok, H[:, AQ + m, :], 0.125), after=ready)
        gemm(u, KT, lambda bank, tok: rope(bank, tok, H[:, AK, :], 1.0))
        for m in range(2):
            gemm(u, KT, lambda bank, tok, m=m: rope(bank, tok, H[:, BQR + m, :], 0.125, raw=H[:, BQ + m, :]))
        for dst in (KC, VC):
            def evac(bank, tok, dst=dst):
                A(s.activation, H[0:64, dst, :], bank[0:64, :], ACT.Copy, after=[tok])
                V(v.memset, H[64:P, dst, T - 1:T], 0.0, after=[A.sem.token()])
                t = A(s.activation, H[64:P, dst, 0:T - 1], bank[64:P, 1:T], ACT.Copy, after=[V.sem.token()])
                return [t]
            gemm(u, KT, evac)
        gemm(u, KT, lambda bank, tok: rope(bank, tok, H[:, KSW, :], 1.0))
        r4 = lambda ap: ap.rearrange("p (b c) -> p b c", b=NTB)
        av, vsw, sm = r4(H[:, AV, :]), r4(H[:, VSW, :]), r4(H[:, SM, :])
        for dst in (av, vsw):
            gemm_tok(u, P, lambda bank, tok, dst=dst: [A(s.activation, dst, r4(bank[:, :]), ACT.Copy, after=[tok])])
        gemm_tok(u, 20, lambda bank, tok: [A(s.activation, sm[:, :, 0:20], r4(bank[:, :])[:, :, 0:20], ACT.Copy,
                                             after=[tok])])
        A(s.activation, sm[:, :, 32:44], sm[:, :, 0:12], ACT.Sigmoid)
        xw = lambda ap: ap.rearrange("p (j n) -> p j n", j=16)
        for which, (src, pos) in enumerate(((KC, "pe_k"), (VC, "pe_v"))):
            x = H[:, XK + which, 0:16 * N_CMP]
            base = H[:, src, :]
            t = None
            for jp in range(16):
                t = V(v.tensor_scalar, x[:, jp * N_CMP:(jp + 1) * N_CMP], base[:, 2 * jp:2 * jp + 16 * (N_CMP - 1) + 1:16],
                      vec2(pos, jp, jp + 1), None, ALU.add, after=[A.sem.token()])
        hid = H[:, 15, 0:4 * 32].rearrange("p (w m n) -> p w m n", w=2, m=2)
        for which in range(2):
            x = xw(H[:, XK + which, 0:16 * N_CMP])
            for m in range(2):
                bank = B[2 + m]
                PE.wait(bank.free, V.sem.token())
                for kg in range(2):
                    w = pr.take()
                    for j in range(KT):
                        ins = pe.matmul(bank[:, 0:N_CMP], w[:, j, :], x[:, kg * KT + j, :], start=(kg + j == 0),
                                        stop=(kg == 1 and j == KT - 1))
                    tok = pr.release(ins)
                bank.free = [A(s.activation, hid[:, which, m, 0:N_CMP], bank[:, 0:N_CMP], ACT.Silu, after=[tok])]
        w = pr.take()
        PE.wait(B[2].free, B[3].free, *now())
        for m in range(2):
            pe.matmul(B[2][0:64, 0:N_CMP], w[:, m, 0:64], hid[:, 0, m, 0:N_CMP], start=(m == 0), stop=(m == 1))
        for m in range(2):
            pe.matmul(B[4][64:P, 0:N_CMP], w[:, m, 0:64], hid[:, 0, m, 0:N_CMP], start=(m == 0), stop=(m == 1))
        for m in range(2):
            ins = pe.matmul(B[3][0:N_CMP, 0:64], hid[:, 1, m, 0:N_CMP], w[:, m, 64:128], start=(m == 0), stop=(m == 1))
        tok = pr.release(ins)
        kcmp, vcmp = H[:, 16, 0:N_CMP], H[0:N_CMP, 16, 64:128]
        A(s.activation, H[0:64, 16, 0:N_CMP], B[2][0:64, 0:N_CMP], ACT.Copy, after=[tok])
        A(s.activation, H[64:P, 16, 0:N_CMP], B[4][64:P, 0:N_CMP], ACT.Copy)
        t = A(s.activation, vcmp, B[3][0:N_CMP, 0:64], ACT.Copy)
        B[2].free = B[3].free = B[4].free = [t]
        KS2, KW2 = 17, 18
        PE.wait(B[3].free, *now())
        pe.matmul(B[3][64:P, :], ident[:, 0:64], H[:, KSW, :], start=True, stop=True)
        ins = pe.matmul(B[4][0:64, :], ident[:, 64:P], H[:, KSW, :], start=True, stop=True)
        tok = PE.done(ins)
        A(s.activation, H[64:P, KS2, :], B[3][64:P, :], ACT.Copy, after=[tok])
        A(s.activation, H[0:64, KS2, :], H[0:64, KSW, :], ACT.Copy)
        A(s.activation, H[0:64, KW2, :], B[4][0:64, :], ACT.Copy)
        t = A(s.activation, H[64:P, KW2, :], H[64:P, KSW, :], ACT.Copy)
        B[3].free = B[4].free = [t]
        PE.wait(B[5].free, B[6].free, *now())
        pe.matmul(B[5][64:P, :], ident[:, 0:64], H[:, AK, :], start=True, stop=True)
        ins = pe.matmul(B[6][0:64, :], ident[:, 64:P], H[:, AK, :], start=True, stop=True)
        tok = PE.done(ins)
        A(s.activation, H[64:P, 19, :], B[5][64:P, :], ACT.Copy, after=[tok])
        A(s.activation, H[0:64, 19, :], H[0:64, AK, :], ACT.Copy)
        A(s.activation, H[0:64, 20, :], B[6][0:64, :], ACT.Copy)
        t = A(s.activation, H[64:P, 20, :], H[64:P, AK, :], ACT.Copy)
        B[5].free = B[6].free = [t]

        items = []

        def to_mix(tile, bank):
            return lambda tok: [A(s.activation, M[:, tile, :], bank[:, :], ACT.Copy, after=[tok])]

        for h in range(4):
            hr = slice(64 * (h % 2), 64 * (h % 2) + 64)
            for b in range(NTB):
                lo = max(0, b - 1)
                w_ = (b + 1 - lo) * P
                extra = [(ident, const("causal"), w_ - P, P)]
                if b:
                    extra.append((ident, const("band"), 0, P))
                items.append(dict(q=H[hr, AQ + h // 2, b * P:b * P + P], k=H[hr, 19 + h // 2, lo * P:(b + 1) * P],
                                  extra=extra, width=w_, sink=vec2("sinks", h, h + 1),
                                  v=[av[:, c, 64 * (h // 2):64 * (h // 2) + 64] for c in range(lo, b + 1)],
                                  out=B[6 + h // 2][hr, b * P:b * P + P], bank=B[6 + h // 2], start=True, stop=True))
            if h % 2:
                items[-1]["evac"] = to_mix(h // 2, B[6 + h // 2])
        items[0]["after"] = now()
        add, mul = const("cmp_add"), const("cmp_mul")
        for h in range(4):
            hr = slice(64 * (h % 2), 64 * (h % 2) + 64)
            for b in range(NTB):
                w_ = (b + 1) * P
                out = dict(out=B[6 + h // 2][hr, b * P:w_], bank=B[6 + h // 2])
                cols = slice(b * N_CMP, (b + 1) * N_CMP)
                gate = lambda n: sm[:, b, 32 + 4 * n + h:33 + 4 * n + h]
                items.append(dict(q=H[hr, BQ + h // 2, b * P:w_], k=kcmp[hr, :], width=N_CMP, gate=gate(0),
                                  extra=[(ident, add[:, cols], 0, N_CMP)], valid=mul[:, cols], v=[vcmp],
                                  start=True, stop=False, **out))
                causal = [(ident, const("causal"), b * P, P)]
                items.append(dict(q=H[hr, BQR + h // 2, b * P:w_], k=H[hr, KS2, 0:w_], width=w_, gate=gate(1),
                                  extra=causal, v=[vsw[:, c, 0:64] for c in range(b + 1)], start=False, stop=False,
                                  **out))
                items.append(dict(q=H[hr, BQR + h // 2, b * P:w_], k=H[hr, KW2, 0:w_], width=w_, gate=gate(2),
                                  extra=causal, v=[vsw[:, c, 64:128] for c in range(b + 1)], start=False, stop=True,
                                  **out))
            if h % 2:
                items[-1]["evac"] = to_mix(2 + h // 2, B[6 + h // 2])
        attention(items)

        SMC = COL[:, 128:256]
        beta, gcol, gc, gl, bege, gle = (SMC[:, z * 16:z * 16 + 16] for z in range(6))
        c4 = lambda ap: ap.rearrange("p (b h) -> p b h", b=NTB)
        t = A(s.activation, c4(beta), sm[:, :, 16:20], ACT.Sigmoid, after=now())
        x = c4(gcol)
        for b in range(NTB):
            V(v.tensor_tensor, x[:, b, :], sm[:, b, 12:16], vec2("dt_bias"), ALU.add)
        V(v.tensor_scalar, gcol, gcol, -1.0, None, ALU.mult)
        softplus_neg(gc, gcol, gl)
        t = A(s.activation, COL[:, 84:88], vec2("A_log"), ACT.Exp, after=[V.sem.token()])
        V.wait(t)
        for b in range(NTB):
            V(v.scalar_tensor_tensor, x[:, b, :], c4(gc)[:, b, :], -1.0, COL[:, 84:88], ALU.mult, ALU.mult)
        PE.wait(B[2].free, B[3].free, *now())
        pe.matmul(B[2][:, 0:16], const("tri"), gcol, start=True, stop=True)
        ins = pe.matmul(B[3][:, 0:16], const("one64"), gcol, start=True, stop=True)
        tok = PE.done(ins)
        V(v.tensor_copy, gc, B[2][:, 0:16], after=[tok])
        V(v.tensor_copy, gl, B[3][:, 0:16])
        B[2].free = B[3].free = [V.sem.token()]
        V(v.tensor_tensor, gle, gl, gc, ALU.subtract)
        t = A(s.activation, gle, gle, ACT.Exp, after=[V.sem.token()])
        t = A(s.activation, bege, gc, ACT.Exp)
        V(v.tensor_tensor, bege, bege, beta, ALU.mult, after=[t])
        V(v.tensor_scalar, gl, gc, -1.0, None, ALU.mult)
        ngc = gl
        V(v.memset, TMP[:, :, 0:3], 0.0)
        ready = now()
        for m in range(12):
            def evac(bank, tok, m=m):
                src = TMP[:, m % 2, :]
                t = A(s.activation, src[:, 3:3 + T], bank[:, :], ACT.Copy, after=[tok, V.sem.token()])
                V.wait(t)
                conv4(src, H[:, m, :], lambda j: vec2("conv_w", 12 * j + m, 12 * j + m + 1), None)
                t = A(s.activation, H[:, m, :], H[:, m, :], ACT.Silu, after=[V.sem.token()])
                return [t]
            gemm(u, KT, evac, after=ready)
        for m in range(4):
            gemm(u, KT, lambda bank, tok, m=m: [A(s.activation, H[:, 12 + m, :], bank[:, :], ACT.Silu, after=[tok])])
        QK, WT = 16, 20
        KBT, ATL, XM, XTM, PM, KBG, VBT, EG = range(24, 32)
        h_ = lambda t: H[:, t, :]
        glast = COL[:, 16:48]
        for h in range(GH):
            for src, scale in ((h, float(P) ** -0.5), (4 + h, 1.0)):
                t = A(s.activation, h_(KBT), h_(src), ACT.Square, after=[V.sem.token()] + pr.tensor_now())
                tok = matmuls(B[2][:, :], [(ones, h_(KBT))], after=[t], bank=B[2])
                inv_sqrt(B[2], tok, 1e-6, h_(EG))
                V(v.scalar_tensor_tensor, h_(src), h_(src), scale, h_(EG), ALU.mult, ALU.mult, after=[A.sem.token()])
            for n, src in enumerate((4 + h, 8 + h)):
                bank = B[4 + n]
                PE.wait(bank.free, *now())
                for b in range(NTB):
                    ins = pe.transpose(bank[:, b * P:b * P + P], H[:, src, b * P:b * P + P], ident)
                tok = PE.done(ins)
            for b in range(NTB):
                blk = slice(b * P, b * P + P)
                V(v.tensor_scalar, H[:, KBG, blk], B[4][:, blk], c4(bege)[:, b, h:h + 1], None, ALU.mult, after=[tok])
                V(v.tensor_scalar, H[:, VBT, blk], B[5][:, blk], c4(beta)[:, b, h:h + 1], None, ALU.mult)
            for b in range(NTB):
                blk = slice(b * P, b * P + P)
                PE.wait(B[2].free, B[3].free)
                pe.matmul(B[2][:, blk], c4(gcol)[:, b, h:h + 1].broadcast_to([P, P]), const("tri"), start=True, stop=True)
                ins = pe.matmul(B[3][:, blk], c4(beta)[:, b, h:h + 1].broadcast_to([P, P]), ident, start=True, stop=True)
            tok = PE.done(ins)
            V(v.tensor_tensor, h_(KBT), h_(4 + h), B[3][:, :], ALU.mult, after=[tok])
            for b in range(NTB):
                blk = slice(b * P, b * P + P)
                V(v.scalar_tensor_tensor, H[:, PM, blk], B[2][:, blk], c4(ngc)[:, b, h:h + 1], const("decay_mask"),
                  ALU.add, ALU.add)
            t = A(s.activation, h_(PM), h_(PM), ACT.Exp, after=[V.sem.token()])
            t2 = A(s.activation, h_(EG), B[2][:, :], ACT.Exp)
            B[2].free = B[3].free = [t2, V.sem.token()]
            V(v.tensor_copy, glast[:, 8 * h:8 * h + 8], h_(EG)[:, 63::64], after=[t2])
            PE.wait(B[2].free, B[3].free, *now())
            for b in range(NTB):
                blk = slice(b * P, b * P + P)
                pe.matmul(B[2][:, blk], H[:, 4 + h, blk], H[:, KBT, blk], start=True, stop=True)
                ins = pe.matmul(B[3][:, blk], H[:, 4 + h, blk], H[:, h, blk], start=True, stop=True)
            tok = PE.done(ins)
            V(v.tensor_tensor, h_(ATL), B[2][:, :], h_(PM), ALU.mult, after=[tok])
            V(v.tensor_tensor, h_(QK + h), B[3][:, :], h_(PM), ALU.mult, after=pr.tensor_now())
            B[2].free = B[3].free = [V.sem.token()]
            V(v.tensor_tensor, h_(h), h_(h), h_(EG), ALU.mult)
            for b in range(NTB):
                blk = slice(b * P, b * P + P)
                V(v.tensor_tensor, H[:, ATL, blk], H[:, ATL, blk], const("strict"), ALU.mult)
                V(v.tensor_scalar, H[:, 4 + h, blk], B[4][:, blk], c4(gle)[:, b, h:h + 1], None, ALU.mult)
            B[4].free = B[5].free = [V.sem.token()]
            lev = const("levels")
            for b in range(NTB):
                blk = slice(b * P, b * P + P)
                V(v.tensor_tensor, H[:, EG, blk], H[:, ATL, blk], lev[:, 0:P], ALU.mult)
                V(v.tensor_tensor, H[:, XTM, blk], ident, H[:, EG, blk], ALU.subtract)
            PE.wait(B[2].free, *now())
            for b in range(NTB):
                blk = slice(b * P, b * P + P)
                ins = pe.transpose(B[2][:, blk], H[:, XTM, blk], ident)
            tok = PE.done(ins)
            B[2].free = [V(v.tensor_copy, h_(XM), B[2][:, :], after=[tok])]
            for k in range(1, 6):
                for b in range(NTB):
                    blk = slice(b * P, b * P + P)
                    V(v.tensor_tensor, H[:, EG, blk], H[:, ATL, blk], lev[:, k * P:k * P + P], ALU.mult,
                      after=pr.tensor_now())
                PE.wait(B[2].free, B[3].free, *now())
                for b in range(NTB):
                    blk = slice(b * P, b * P + P)
                    ins = pe.matmul(B[2][:, blk], H[:, EG, blk], H[:, XM, blk], start=True, stop=True)
                tok = PE.done(ins)
                t = A(s.activation, h_(PM), B[2][:, :], ACT.Copy, after=[tok])
                B[2].free = [t]
                PE.wait(t)
                for b in range(NTB):
                    blk = slice(b * P, b * P + P)
                    ins = pe.matmul(B[3][:, blk], H[:, PM, blk], H[:, XTM, blk], start=True, stop=True)
                tok = PE.done(ins)
                if k < 5:
                    for b in range(NTB):
                        blk = slice(b * P, b * P + P)
                        ins = pe.matmul(B[2][:, blk], H[:, XTM, blk], H[:, PM, blk], start=True, stop=True)
                    tok = PE.done(ins)
                    V(v.tensor_tensor, h_(XM), h_(XM), B[2][:, :], ALU.subtract, after=[tok])
                t = V(v.tensor_tensor, h_(XTM), h_(XTM), B[3][:, :], ALU.subtract, after=[tok])
                B[2].free = B[3].free = [t]
            PE.wait(B[2].free, B[3].free, *now())
            for b in range(NTB):
                blk = slice(b * P, b * P + P)
                pe.matmul(B[2][:, blk], H[:, XTM, blk], H[:, VBT, blk], start=True, stop=True)
                ins = pe.matmul(B[3][:, blk], H[:, KBG, blk], H[:, XTM, blk], start=True, stop=True)
            tok = PE.done(ins)
            A(s.activation, h_(8 + h), B[2][:, :], ACT.Copy, after=[tok])
            t = A(s.activation, h_(WT + h), B[3][:, :], ACT.Copy)
            B[2].free = B[3].free = [t]
        ST = H[:, KBT, :].rearrange("p (h e) -> p h e", h=GH)
        VN = H[:, ATL, :].rearrange("p (h e) -> p h e", h=GH)
        V(v.memset, ST, 0.0, after=now() + pr.tensor_now())
        for c in range(8):
            b, o = c // 2, 64 * (c % 2)
            ck = slice(c * 64, c * 64 + 64)
            blk = slice(b * P, b * P + P)
            PE.wait(B[2].free, *now())
            for h in range(GH):
                ins = pe.matmul(B[2][o:o + 64, h * P:h * P + P], H[:, WT + h, ck], ST[:, h, :], start=True, stop=True)
            tok = PE.done(ins)
            for h in range(GH):
                t = V(v.tensor_tensor, VN[o:o + 64, h, :], H[o:o + 64, 8 + h, blk], B[2][o:o + 64, h * P:h * P + P],
                      ALU.subtract, after=[tok] + pr.tensor_now())
            B[2].free = [t]
            bank = B[4 + c % 2]
            PE.wait(bank.free, B[3].free, t)
            for h in range(GH):
                pe.matmul(bank[:, h * 64:h * 64 + 64], ST[:, h, :], H[:, h, ck], start=True, stop=False,
                          skip_group_check=True)
                pe.matmul(bank[:, h * 64:h * 64 + 64], VN[o:o + 64, h, :], H[o:o + 64, QK + h, ck], start=False,
                          stop=True, skip_group_check=True)
                ins = pe.matmul(B[3][:, h * P:h * P + P], H[o:o + 64, 4 + h, blk], VN[o:o + 64, h, :], start=True,
                                stop=True)
            tok = PE.done(ins)
            for h in range(GH):
                V(v.scalar_tensor_tensor, ST[:, h, :], ST[:, h, :], glast[:, 8 * h + c:8 * h + c + 1],
                  B[3][:, h * P:h * P + P], ALU.mult, ALU.add, after=[tok])
            B[3].free = [V.sem.token()]
            t = A(s.activation, M[:, 4:8, ck], bank[:, 0:256].rearrange("p (h t) -> p h t", h=GH), ACT.Copy, after=[tok])
            bank.free = [t]
        for h in range(GH):
            o = M[:, 4 + h, :]
            sq, rs = h_(XM), h_(XTM)
            t = A(s.activation, sq, o, ACT.Square, after=[V.sem.token()] + pr.tensor_now())
            tok = matmuls(B[2][:, :], [(ones, sq)], after=[t], bank=B[2])
            t = V(v.tensor_scalar, rs, B[2][:, :], 1.0 / P, 1e-6, ALU.mult, ALU.add, after=[tok])
            B[2].free = [t]
            t = A(s.activation, rs, rs, ACT.Sqrt, after=[t])
            V(v.reciprocal, rs, rs, after=[t])
            V(v.scalar_tensor_tensor, o, o, vec2("gdn_norm"), rs, ALU.mult, ALU.mult)
            V(v.tensor_tensor, o, o, h_(12 + h), ALU.mult)

        def add_gated(gate0):
            return lambda m: (lambda bank, tok: [V(v.scalar_tensor_tensor, X[:, m, :], bank[:, :],
                                                   mod[:, gate0 + m:gate0 + m + 1], X[:, m, :], ALU.mult, ALU.add,
                                                   after=[tok])])
        ready = now()
        for m in range(KT):
            gemm(mix, KT, add_gated(16)(m), after=ready)
        rms_norm_all(GF, mod[:, 24:32], u)

        def gate_up(m_ap):
            tmp = TMP[:, 1, 0:T]
            gemm(u, KT, lambda bank, tok: [A(s.activation, tmp, bank[:, :], ACT.Silu, after=[tok, V.sem.token()])],
                 after=[A.sem.token()])
            gemm(u, KT, lambda bank, tok: [V(v.tensor_tensor, m_ap, bank[:, :], tmp, ALU.mult,
                                             after=[tok, A.sem.token()])])
        with pr.loop("gate_up", FF2_T // 4) as i:
            for j in range(4):
                gate_up(H[:, bass.ds(i * 4 + j, 1), :].rearrange("p a t -> p (a t)"))
        for j in range(FF2_T // 4 * 4, FF2_T):
            gate_up(H[:, j, :])
        ready = now()
        for m in range(KT):
            gemm(lambda k: H[:, k, :], FF2_T, add_gated(40)(m), after=ready)

    rms_norm_all(vec1("final"), None, u)
    stored = pr.count("stored")
    for b in range(NTB):
        for half in range(2):
            bank = B[4 + half]
            PE.wait(bank.free, *now())
            for k in range(4):
                ins = pe.transpose(bank[:, k * P:k * P + P], U[:, 4 * half + k, b * P:b * P + P], ident)
            tok = PE.done(ins)
            t = A(s.activation, M[:, 2 * b + half, :], bank[:, :], ACT.Copy, after=[tok])
            bank.free = [t]
    A.wait(A.sem.token())
    A.done(s.dma_start(io["out"].rearrange("(b p) d -> p b d", p=P),
                       M[:, :, :].rearrange("p (b h) t -> p b (h t)", b=NTB)), stored, 16)
    A.wait(stored.token())
    assert pr.panel == n_panels, (pr.panel, n_panels)
    return pr.found


def free_sem(pr):
    return pr.used.handle


def kernel(**inputs):
    import concourse.bacc as bacc
    from concourse.bass_utils import run_bass_kernel_spmd

    i = {k: np.asarray(a) for k, a in inputs.items()}
    arrays = {
        "x": np.ascontiguousarray(i["x"][0]),
        "consts": constants(),
        "vec1": vectors1(i),
        "vec2": np.stack([vectors2(i, l) for l in range(L2)]),
        "stream": weight_stream(i),
    }

    def program(plan):
        nc = bacc.Bacc("TRN2", target_bir_lowering=False, num_devices=1)
        io = {k: nc.dram_tensor(k, a.shape, F32, kind="ExternalInput").ap() for k, a in arrays.items()}
        io["out"] = nc.dram_tensor("out", (T, D), F32, kind="ExternalOutput").ap()
        return nc, build(nc, io, arrays["stream"].shape[0], plan)

    _, plan = program({})
    nc, again = program(plan)
    assert again == plan
    r = run_bass_kernel_spmd(nc, [arrays], core_ids=[0])
    return r.results[0]["out"].reshape(1, T, D)
```

```python
import numpy as np
import concourse.bass as bass
from concourse import mybir
from concourse.alu_op_type import AluOpType as ALU

P = 128
D = 1024
T = 512
KT = D // P
NTB = T // P
RING = 4
BODY = 2 * RING
F32 = mybir.dt.float32
F32R = mybir.dt.float32r
I32 = mybir.dt.int32
ACT = mybir.ActivationFunctionType
AXX = mybir.AxisListType.X
NEG = -1e30

L1 = 2
RGW = 512
GLA_CH = 64
ALPHA = float((2 * L1) ** 0.25)
FF1 = 4096
FOX_H = 16
L2 = 2
FF2 = 2816
FF2_T = FF2 // P
N_CMP = T // 16 - 1
GH = 4
N_MAIN = 423
N_START = 16
GROUP = 8
N_ADA = 2 * L1 * 24 + L2 * 48



class Columns:

    def __init__(self, items):
        self.at, self.n = {}, 0
        for name, width in items:
            self.at[name] = (self.n, width)
            self.n += width


CONST = Columns([("ident", 128), ("ones", 128), ("mean", 128), ("one64", 128), ("mean64", 128), ("tri", 128),
                 ("rot", 128), ("causal", 128), ("band", 128), ("decay_mask", 128), ("strict", 128),
                 ("levels", 6 * 128), ("gla_mask", 64), ("chunk_reset", T), ("cos", T), ("sin", T),
                 ("cmp_add", NTB * N_CMP), ("cmp_mul", NTB * N_CMP)])
VEC1 = Columns([("c", 8), ("ada_b", N_ADA), ("ln_g", 32), ("ln_b", 32), ("conv_w", 16), ("conv_b", 4),
                ("rg_ba", 4), ("rg_bx", 4), ("rg_lam", 4), ("gla_b", 2), ("gla_g", 4), ("gla_up", 256),
                ("fox_bf", 1), ("fox_qg", 1), ("fox_kg", 1), ("mlp_b1", 64), ("mlp_b2", 16), ("c2", 8),
                ("final", 8)])
VEC2 = Columns([("norm_mix", 8), ("norm_ffn", 8), ("conv_w", 48), ("gdn_norm", 1), ("sinks", 4),
                ("A_log", 4), ("dt_bias", 4), ("pe_k", 16), ("pe_v", 16)])


def constants():
    out = np.zeros((P, CONST.n), np.float32)

    def put(name, a, rows=P):
        c, w = CONST.at[name]
        out[:rows, c:c + w] = np.asarray(a, np.float32).reshape(rows, w)

    r, c = np.arange(P)[:, None], np.arange(P)[None, :]
    same = r // 64 == c // 64
    put("ident", r == c)
    put("ones", np.ones((P, P)))
    put("mean", np.full((P, P), 1.0 / D))
    put("one64", same)
    put("mean64", same / 64.0)
    put("tri", same & (r <= c))
    rot = np.zeros((P, P))
    for h in (0, 64):
        for d in range(32):
            rot[h + 32 + d, h + d] = -1.0
            rot[h + d, h + 32 + d] = 1.0
    put("rot", rot)
    put("causal", np.where(c <= r, 0.0, NEG))
    put("band", np.where(c > r, 0.0, NEG))
    put("decay_mask", np.where(same & (r <= c), 0.0, NEG))
    put("strict", same & (r < c))
    put("levels", np.stack([((c >> k) & 1 == 1) & ((r >> k) & 1 == 0) & (r >> (k + 1) == c >> (k + 1))
                            for k in range(6)], 1))
    put("gla_mask", np.tile(np.triu(np.ones((64, 64))), (2, 1)))
    t = np.arange(T)
    put("chunk_reset", np.broadcast_to(t % 64 != 0, (P, T)))
    inv = (1.0 / (10000.0 ** (np.arange(0, 64, 2, dtype=np.float32) / 64))).astype(np.float32)
    ang = (t.astype(np.float32)[None, :] * inv[:, None]).astype(np.float32)
    put("cos", np.tile(np.cos(ang), (4, 1)))
    put("sin", np.tile(np.sin(ang), (4, 1)))
    ends = np.arange(N_CMP) * 16 + 31
    valid = ends[None, None, :] <= (np.arange(NTB)[None, :, None] * P + np.arange(P)[:, None, None])
    put("cmp_add", np.where(valid, 0.0, NEG))
    put("cmp_mul", valid)
    return out


def columns_of(v):
    v = np.asarray(v)
    return np.ascontiguousarray(v.reshape(-1, P).T)


def pack(layout, values):
    out = np.zeros((P, layout.n), np.float32)
    for name, (c, w) in layout.at.items():
        a = values[name]
        out[:a.shape[0], c:c + w] = a
    return out


def panels_of(w):
    k, n = w.shape
    pk, pn = -k % D, -n % P
    if pk or pn:
        w = np.pad(w, ((0, pk), (0, pn)))
    kg, m = w.shape[0] // D, w.shape[1] // P
    return w.reshape(kg, KT, P, m, P).transpose(3, 0, 2, 1, 4).reshape(m * kg, P, KT * P)


def weight_streams(i):
    main, ada = [], []
    for l in range(L1):
        for s in range(2):
            ada.append(panels_of(i["ada_w"][l, s]))
    for l in range(L2):
        ada.append(panels_of(i["ada_w_2"][l]))

    def add(w):
        main.append(panels_of(w))

    ev = i["ev_w_in"][0]
    add(ev[:, 0:RGW])
    rg = np.zeros((P, 8, P), np.float32)
    for g, w in enumerate((i["ev_rg_wa"][0], i["ev_rg_wx"][0])):
        for b in range(8):
            o = 64 * (b % 2)
            rg[o:o + 64, 4 * g + b // 2, o:o + 64] = w[b]
    main.append(rg.reshape(1, P, KT * P))
    add(ev[:, 2560:])
    add(ev[:, 1024:2048])
    add(ev[:, RGW:1024])
    add(ev[:, 2048:2560])
    add(i["ev_w_out"][0])
    add(i["mlp_w1"][0])
    add(i["mlp_w2"][0])
    od = i["od_w_in"][0]
    add(od[:, 4 * D:])
    for hp in range(KT):
        for s in range(4):
            add(od[:, s * D + hp * P:s * D + hp * P + P])
    add(i["od_w_out"][0])
    add(i["mlp_w1"][1])
    add(i["mlp_w2"][1])
    for l in range(L2):
        w = i["w_in_2"][l]
        add(w[:, 0:384])
        add(w[:, 512:768])
        for a, b in ((768, 768), (832, 832), (896, 1024)):
            add(np.concatenate([w[:, a:a + 64], w[:, b:b + 64]], 1))
        add(w[:, 384:512])
        add(np.concatenate([w[:, 960:1024], w[:, 1088:1152]], 1))
        add(np.concatenate([w[:, 1152:1164], w[:, 3212:3220]], 1))
        add(i["cmp_k_w1_2"][l])
        add(i["cmp_v_w1_2"][l])
        add(np.concatenate([i["cmp_k_w2_2"][l], i["cmp_v_w2_2"][l]], 1))
        add(w[:, 1164:3212])
        add(i["w_out_2"][l])
        gu = i["w_gate_up_2"][l]
        for m in range(FF2_T):
            add(gu[:, m * P:m * P + P])
            add(gu[:, FF2 + m * P:FF2 + m * P + P])
        add(i["w_down_2"][l])
    ada = np.concatenate(ada)
    rest = np.concatenate([ada[N_START:], np.zeros((2, P, KT * P), np.float32)])
    return np.concatenate([ada[:N_START]] + main), rest


def vectors1(i):
    two = lambda g: np.concatenate([g, g])[:, None]
    return pack(VEC1, {
        "c": columns_of(i["c"]), "ada_b": np.concatenate([columns_of(i["ada_b"]), columns_of(i["ada_b_2"])], 1),
        "ln_g": columns_of(i["ln_g"]),
        "ln_b": columns_of(i["ln_b"]), "conv_w": columns_of(i["ev_conv_w"]), "conv_b": columns_of(i["ev_conv_b"]),
        "rg_ba": columns_of(i["ev_rg_ba"]), "rg_bx": columns_of(i["ev_rg_bx"]), "rg_lam": columns_of(i["ev_rg_lam"]),
        "gla_b": columns_of(i["ev_gla_b_up"]), "gla_g": columns_of(i["ev_gla_norm_g"]), "gla_up": i["ev_gla_w_up"][0],
        "fox_bf": i["od_b_f"].reshape(FOX_H, 1), "fox_qg": two(i["od_q_norm_g"][0]), "fox_kg": two(i["od_k_norm_g"][0]),
        "mlp_b1": columns_of(i["mlp_b1"]), "mlp_b2": columns_of(i["mlp_b2"]), "c2": columns_of(i["c_2"]),
        "final": columns_of(i["final_norm_2"])})


def vectors2(i, l):
    rows = lambda v: np.broadcast_to(v[None, :], (P, v.shape[0]))
    return pack(VEC2, {
        "norm_mix": columns_of(i["norm_mix_2"][l]),
        "norm_ffn": columns_of(i["norm_ffn_2"][l]), "conv_w": columns_of(i["gdn_conv_w_2"][l]),
        "gdn_norm": columns_of(i["gdn_norm_2"][l]), "sinks": rows(i["attn_sinks_2"][l]),
        "A_log": rows(i["gdn_A_log_2"][l]), "dt_bias": rows(i["gdn_dt_bias_2"][l]),
        "pe_k": columns_of(i["cmp_pe_k_2"][l]), "pe_v": columns_of(i["cmp_pe_v_2"][l])})




class Count:

    def __init__(self, handle):
        self.handle, self.const, self.terms = handle, 0, ()

    def token(self):
        return (self, self.const, self.terms)


class Engine:

    def __init__(self, prog, eng, sem, chained):
        self.prog, self.eng, self.sem, self.chained, self.seen = prog, eng, sem, chained, {}

    def wait(self, *tokens):
        for t in tokens:
            if isinstance(t, list):
                self.wait(*t)
                continue
            sem, const, terms = t
            known = [x[0] for x in self.prog.loops]
            assert all(x[0] in known for x in terms), "a token of a loop that has ended"
            if const == 0 and not terms:
                continue
            old = self.seen.get(id(sem))
            if old is not None and old[1] == terms and old[0] >= const:
                continue
            self.seen[id(sem)] = (const, terms)
            value = const
            for loop, k in terms:
                if k:
                    value = loop.i * k + value
            self.eng.wait_ge(sem.handle, value)

    def done(self, ins, sem=None, by=1):
        sem = sem or self.sem
        ins.then_inc(sem.handle, by)
        sem.const += by
        return sem.token()

    def __call__(self, op, *args, after=(), **kw):
        if self.chained:
            self.wait(self.sem.token())
        self.wait(*after)
        return self.done(op(*args, **kw))


class Loop:
    i = None


class Program:
    def __init__(self, nc, plan):
        self.nc, self.plan, self.found, self.loops = nc, plan, {}, []
        self.sems = []
        self.V = Engine(self, nc.vector, self.count("vector_done"), True)
        self.A = Engine(self, nc.scalar, self.count("scalar_done"), True)
        self.G = Engine(self, nc.gpsimd, self.count("gpsimd_done"), True)
        self.PE = Engine(self, nc.tensor, self.count("tensor_done"), False)
        self.used = self.count("panels_used")
        self.landed = [self.count(f"panel_landed_{k}") for k in range(RING)]
        self.split = None
        self.panel = 0
        self.banks = [Bank(nc.alloc_psum_tensor(f"bank{k}", [P, 512], F32)) for k in range(8)]

    def count(self, name):
        c = Count(self.nc.alloc_semaphore(name))
        self.sems.append(c)
        return c

    def tensor_now(self):
        return [self.PE.sem.token(), self.used.token()]

    def engines_seen_clear(self):
        for e in (self.V, self.A, self.G, self.PE):
            e.seen = {}

    def loop(self, name, trips, fence=True):
        return LoopScope(self, name, trips, fence)

    def take(self):
        slot = self.panel % RING
        self.split = None
        self.PE.wait(self.landed[slot].token_after(16))
        return self.ring[:, slot, :].rearrange("p (k c) -> p k c", k=KT)

    def release(self, matmul):
        slot = self.panel % RING
        self.landed[slot].const += 16
        self.panel += 1
        return self.PE.done(matmul, self.used)


def _token_after(self, by):
    return (self, self.const + by, self.terms)


Count.token_after = _token_after


class Bank:

    def __init__(self, t):
        self.t, self.free = t, []

    def __getitem__(self, k):
        return self.t[k]


class LoopScope:

    def __init__(self, prog, name, trips, fence):
        self.prog, self.name, self.trips, self.fence = prog, name, trips, fence

    def __enter__(self):
        p = self.prog
        self.scope = p.nc.Fori(0, self.trips, engines=(mybir.EngineType.PE, mybir.EngineType.Activation,
                                                       mybir.EngineType.DVE))
        self.loop = Loop()
        self.loop.i = self.scope.__enter__()
        self.start = [c.const for c in p.sems]
        per = p.plan.get(self.name, [0] * len(p.sems))
        for c, k in zip(p.sems, per):
            c.terms = c.terms + ((self.loop, k),)
        p.loops.append((self.loop, self.name))
        self.first = p.panel
        p.engines_seen_clear()
        if self.fence:
            p.PE.wait(p.V.sem.token(), p.A.sem.token())
            p.split = None
            for b in p.banks:
                b.free = []
        else:
            step = {id(c): (self.loop, k) for c, k in zip(p.sems, per)}
            self.carry(lambda t: (t[0], t[1], t[2] + (step[id(t[0])],)))
        return self.loop.i

    def carry(self, move):
        def moved(t):
            return [moved(x) for x in t] if isinstance(t, list) else move(t)
        p = self.prog
        if p.split is not None:
            p.split = moved(p.split)
        for b in p.banks:
            b.free = moved(b.free)

    def __exit__(self, *e):
        p = self.prog
        per = [c.const - s for c, s in zip(p.sems, self.start)]
        p.found[self.name] = per
        for c, s, k in zip(p.sems, self.start, per):
            c.const = s + k * self.trips
            c.terms = c.terms[:-1]
        p.loops.pop()
        used = p.panel - self.first
        assert used % RING == 0
        p.panel = self.first + used * self.trips
        self.scope.__exit__(None, None, None)
        p.engines_seen_clear()
        if self.fence:
            p.split = None
            for b in p.banks:
                b.free = [p.V.sem.token(), p.A.sem.token()]
        else:
            self.carry(lambda t: (t[0], t[1] + t[2][-1][1] * (self.trips - 1), t[2][:-1]))




def build(nc, io, n_panels, plan):
    pr = Program(nc, plan)
    V, A, G, PE = pr.V, pr.A, pr.G, pr.PE
    v, s, g, pe = nc.vector, nc.scalar, nc.gpsimd, nc.tensor
    B = pr.banks

    def sb(name, shape, dt=F32):
        return nc.alloc_sbuf_tensor(name, shape, dt)

    def sb_alias(name, base_after, shape, dt):
        return nc.alloc_sbuf_tensor_at(name, shape, dt, offset=base_after - 4 * int(np.prod(shape[1:])))

    X = sb("residual", [P, KT, T])
    U = sb("mixer_in", [P, KT, T])
    UHI = sb_alias("mlp_in_high", nc.sbuf_base, [P, KT, T], F32R)
    M = sb("mixer_out", [P, KT, T])
    ULO = sb_alias("mlp_in_low", nc.sbuf_base, [P, KT, T], F32R)
    H = sb("hidden", [P, 32, T])
    ring = sb("weight_ring", [P, RING, KT * P])
    pr.ring = ring
    WHI = sb("weights_high", [P, 2, KT * P], F32R)
    WLO = sb("weights_low", [P, 2, KT * P], F32R)
    C = sb("constants", [P, CONST.n])
    V1 = sb("vectors1", [P, VEC1.n])
    V2 = sb("vectors2", [P, VEC2.n])
    MODS = sb("modulations", [P, N_ADA])
    MH = sb("modulation_of_layer", [P, 48])
    SC = sb("silu_c", [P, 2, 8])
    AW = sb("modulation_panels", [P, 2, KT * P])
    AP_ = sb("modulation_products", [P, KT * P])
    AR = sb("modulation_sums", [P, 2, GROUP * P])
    COL = sb("columns", [P, 256])
    PB = sb("probs", [P, 2, T])
    PT = sb("probs_T", [P, 2, T])
    TMP = sb("tmp", [P, 2, T + 3])

    def const(name, rows=P):
        c, w = CONST.at[name]
        return C[0:rows, c:c + w]

    def vec1(name, a=0, b=None, rows=P):
        c, w = VEC1.at[name]
        return V1[0:rows, c + a:c + (w if b is None else b)]

    def vec2(name, a=0, b=None):
        c, w = VEC2.at[name]
        return V2[:, c + a:c + (w if b is None else b)]

    ident, ones = const("ident"), const("ones")

    loads = pr.count("loads")
    A.done(s.dma_start(H[:, 0:8, :].rearrange("p (b h) t -> p b (h t)", b=NTB),
                       io["x"].rearrange("(b p) d -> p b d", p=P)), loads, 16)
    A.done(s.dma_start(C[:, :], io["consts"]), loads, 16)
    A.done(s.dma_start(V1[:, :], io["vec1"]), loads, 16)
    all_loads = loads.token()

    stream = nc.sync
    whole = n_panels // RING
    with stream.Fori(0, whole) as i:
        for k in range(RING):
            stream.wait_ge(free_sem(pr), i * RING + k + 1)
            stream.dma_start(ring[:, k, :], io["stream"][i * RING + k]).then_inc(pr.landed[k].handle, 16)
    for n in range(whole * RING, n_panels):
        stream.wait_ge(free_sem(pr), n + 1)
        stream.dma_start(ring[:, n % RING, :], io["stream"][n]).then_inc(pr.landed[n % RING].handle, 16)

    PE.wait(all_loads)
    pe.sem_inc(pr.used.handle, RING)
    pr.used.const = RING

    def matmuls(bank_ap, pairs, after=(), start=True, stop=True, last=True, bank=None):
        if bank is not None:
            PE.wait(bank.free)
        PE.wait(*after)
        n = len(pairs)
        for k, (lhsT, rhs) in enumerate(pairs):
            ins = pe.matmul(bank_ap, lhsT, rhs, start=start and k == 0, stop=stop and k == n - 1)
        return PE.done(ins) if last else None

    gemm_turn = [0]
    between = []

    def fill(n=1):
        for _ in range(n):
            if between:
                between.pop(0)()

    def gemm_bank():
        gemm_turn[0] += 1
        return B[gemm_turn[0] % 2]

    def gemm(rhs, ktiles, evac, ready=None):
        bank = gemm_bank()
        PE.wait(bank.free)
        k = 0
        while k < ktiles:
            w = pr.take()
            n = min(KT, ktiles - k)
            for j in range(n):
                if ready is not None:
                    PE.wait(ready[k + j])
                ins = pe.matmul(bank[:, :], w[:, j, :], rhs(k + j), start=(k + j == 0), stop=(k + j == ktiles - 1))
            k += n
            tok = pr.release(ins)
        bank.free = evac(bank, tok)
        fill()

    def split_panel():
        n = pr.panel
        z = n % 2
        free = (pr.used, pr.used.const - 1, pr.used.terms)
        t = A(s.activation, WHI[:, z, :], ring[:, n % RING, :], ACT.Copy,
              after=[pr.landed[n % RING].token_after(16), free])
        pr.split = V(v.tensor_tensor, WLO[:, z, :], ring[:, n % RING, :], WHI[:, z, :].bitcast(F32), ALU.subtract,
                     after=[t, free])

    def gemm_split(evac, ready=None):
        if pr.split is None:
            split_panel()
        bank = gemm_bank()
        PE.wait(bank.free, pr.split)
        z = pr.panel % 2
        for k in range(KT):
            if ready is not None:
                PE.wait(ready[k])
            cols = slice(k * P, k * P + P)
            for w, x in ((WHI, UHI), (WHI, ULO), (WLO, UHI)):
                ins = pe.matmul(bank[:, :], w[:, z, cols], x[:, k, :], start=(k == 0 and x is UHI and w is WHI),
                                stop=(k == KT - 1 and w is WLO))
        tok = pr.release(ins)
        split_panel()
        bank.free = evac(bank, tok)

    def gemm_tok(act, width, evac, ready=None):
        bank = gemm_bank()
        PE.wait(bank.free)
        if ready is not None:
            PE.wait(*ready)
        w = pr.take()
        for b in range(NTB):
            for j in range(KT):
                ins = pe.matmul(bank[:, b * P:b * P + width], act(j)[:, b * P:b * P + P], w[:, j, 0:width],
                                start=(j == 0), stop=(j == KT - 1))
        tok = pr.release(ins)
        bank.free = evac(bank, tok)
        fill()

    class Ada:

        def __init__(self):
            self.made = pr.count("modulation_groups_made")
            self.read = pr.count("modulation_groups_read")
            self.groups = 0

        def start(self, c):
            bank = B[7]
            for n in range(N_START):
                w = pr.take()
                for k in range(KT):
                    ins = pe.matmul(bank[:, n:n + 1], w[:, k, :], c[:, k:k + 1], start=(k == 0), stop=(k == KT - 1))
                tok = pr.release(ins)
            bank.free = [V(v.tensor_tensor, MODS[:, 0:N_START], bank[:, 0:N_START], vec1("ada_b", 0, N_START), ALU.add,
                           after=[tok])]

        def gpsimd_program(self):
            landed = [nc.alloc_semaphore(f"modulation_panel_landed_{z}") for z in range(2)]
            step = nc.alloc_semaphore("gpsimd_steps")
            G.wait(A.sem.token())
            for z in range(2):
                g.dma_start(AW[:, z, :], io["ada"][z]).then_inc(landed[z], 16)
            panels = 2 * GROUP
            at, stepped = 0, 0
            for trips, c in ((5, SC[:, 0, :]), (6, SC[:, 1, :])):
                cb = c.rearrange("p (k x) -> p k x", x=1).broadcast_to([P, KT, P])
                with g.Fori(0, trips) as i:
                    count = [0]

                    def own(ins):
                        count[0] += 1
                        ins.then_inc(step, 1)
                        g.wait_ge(step, i * (4 * panels) + (stepped + count[0]))
                    for n in range(panels):
                        slot = n % 2
                        half = n // GROUP
                        if n % GROUP == 0:
                            g.wait_ge(self.read.handle, i * 2 + (at // GROUP + half + READ_START - 1))
                        g.wait_ge(landed[slot], i * (16 * GROUP) + 16 * (at // 2 + n // 2 + 1))
                        own(g.tensor_tensor(AP_[:, :].rearrange("p (k c) -> p k c", k=KT),
                                            AW[:, slot, :].rearrange("p (k c) -> p k c", k=KT), cb, ALU.mult))
                        g.dma_start(AW[:, slot, :], io["ada"][i * panels + (at + n + 2)]).then_inc(landed[slot], 16)
                        own(g.tensor_tensor(AP_[:, 0:512], AP_[:, 0:512], AP_[:, 512:1024], ALU.add))
                        own(g.tensor_tensor(AP_[:, 0:256], AP_[:, 0:256], AP_[:, 256:512], ALU.add))
                        j = n % GROUP
                        own(g.tensor_tensor(AR[:, half, j * P:j * P + P], AP_[:, 0:128], AP_[:, 128:256], ALU.add))
                        if j == GROUP - 1:
                            g.sem_inc(self.made.handle, 1)
                at += panels * trips
                stepped += 4 * panels * trips
            for z in range(2):
                g.wait_ge(landed[z], 16 * (at // 2 + 1))

        def read_group(self):
            bank = B[7]
            half = self.groups % 2
            self.made.const += 1
            PE.wait(bank.free, self.made.token())
            for j in range(GROUP):
                ins = pe.matmul(bank[:, j:j + 1], AR[:, half, j * P:j * P + P], ones[:, 0:1], start=True, stop=True)
            tok = PE.done(ins, self.read)
            self.groups += 1
            at = self.at()
            t = V(v.tensor_tensor, MODS[:, bass.ds(at + N_START, GROUP)], bank[:, 0:GROUP],
                  V1[:, bass.ds(at + (N_START + VEC1.at["ada_b"][0]), GROUP)], ALU.add, after=[tok])
            bank.free = [t]

        def at(self):
            out = (self.made.const - 1) * GROUP
            for loop, k in self.made.terms:
                if k:
                    out = loop.i * (k * GROUP) + out
            return out

    ada = Ada()
    READ_START = 2
    pe.sem_inc(ada.read.handle, READ_START)
    ada.read.const = READ_START

    def plus_one(ap):
        return V(v.tensor_scalar, ap, ap, 1.0, None, ALU.add)

    def stage(n):
        return MODS[:, 24 * n:24 * n + 24]

    def modulate(mod, tiles=range(KT)):
        plus_one(mod[:, 8:16])
        t = V.sem.token()
        return [A(s.activation, U[:, k, :], X[:, k, :], ACT.Identity, bias=mod[:, k:k + 1], scale=mod[:, 8 + k:9 + k],
                  after=[t] + pr.tensor_now()) for k in tiles]

    def mean_step(bank, src, k, tok):
        if k == 0:
            PE.wait(bank.free)
        PE.wait(tok)
        ins = pe.matmul(bank[:, :], const("mean"), src, start=(k == 0), stop=(k == KT - 1), skip_group_check=True)
        return PE.done(ins)

    def inv_sqrt(bank, tok, eps, out):
        t = V(v.tensor_scalar, out, bank[:, :], eps, None, ALU.add, after=[tok, A.sem.token()])
        t2 = A(s.activation, out, out, ACT.Sqrt, after=[t])
        bank.free = [t]
        return V(v.reciprocal, out, out, after=[t2])

    R = TMP[:, 0, 0:T]

    STAGE = 16

    def split_high(k, tok):
        return A(s.activation, UHI[:, k, :], H[:, STAGE + k, :], ACT.Copy, after=[tok])

    def split_low(k, tok):
        return V(v.tensor_tensor, ULO[:, k, :], H[:, STAGE + k, :], UHI[:, k, :].bitcast(F32), ALU.subtract,
                 after=[tok])

    def layer_norm(mean_tok, gcol, bcol, mod, split=False):
        for k in range(KT):
            t = V(v.tensor_tensor, X[:, k, :], X[:, k, :], B[2][:, :], ALU.subtract, after=[mean_tok])
            t = A(s.activation, M[:, k, :], X[:, k, :], ACT.Square, after=[t] + (pr.tensor_now() if k == 0 else []))
            tok = mean_step(B[3], M[:, k, :], k, t)
        B[2].free = [V.sem.token()]
        if mod is not None:
            plus_one(mod[:, 8:16])
            sh = COL[:, 104:112]
            V(v.tensor_tensor, sh, bcol, mod[:, 8:16], ALU.mult)
            V(v.tensor_tensor, sh, sh, mod[:, 0:8], ALU.add)
        inv_sqrt(B[3], tok, 1e-5, R)
        out, high = [], []
        for k in range(KT):
            t = V(v.scalar_tensor_tensor, X[:, k, :], X[:, k, :], gcol[:, k:k + 1], R, ALU.mult, ALU.mult,
                  after=[A.sem.token()] if k == 0 else ())
            if mod is not None:
                dst = H[:, STAGE + k, :] if split else U[:, k, :]
                t = A(s.activation, dst, X[:, k, :], ACT.Identity, bias=sh[:, k:k + 1], scale=mod[:, 8 + k:9 + k],
                      after=[t])
                if split:
                    high.append(split_high(k, t))
                    if k:
                        out.append(split_low(k - 1, high[k - 1]))
                else:
                    out.append(t)
        if split:
            out.append(split_low(KT - 1, high[-1]))
        for k in range(KT):
            A(s.activation, X[:, k, :], X[:, k, :], ACT.Identity, bias=bcol[:, k:k + 1], after=[V.sem.token()])
        return out

    def square_step(m, tok):
        t = A(s.activation, H[:, 24 + m, :], X[:, m, :], ACT.Square, after=[tok])
        return mean_step(B[3], H[:, 24 + m, :], m, t)

    def rms_norm_all(ms_tok, gain, shift, split=False):
        inv_sqrt(B[3], ms_tok, 1e-6, R)
        out, high = [], []
        for k in range(KT):
            dst = H[:, STAGE + k, :] if split else U[:, k, :]
            t = V(v.scalar_tensor_tensor, dst, X[:, k, :], gain[:, k:k + 1], R, ALU.mult, ALU.mult,
                  after=pr.tensor_now() + ([A.sem.token()] if k == 0 else []))
            if shift is not None:
                t = A(s.activation, dst, dst, ACT.Identity, bias=shift[:, k:k + 1], after=[t])
            if split:
                high.append(split_high(k, t))
                if k:
                    out.append(split_low(k - 1, high[k - 1]))
            else:
                out.append(t)
        if split:
            out.append(split_low(KT - 1, high[-1]))
        return out

    def now():
        return [V.sem.token(), A.sem.token()]

    def softplus_neg(out, x, tmp, after=()):
        t = A(s.activation, tmp, x, ACT.Abs, after=list(after) + [V.sem.token()])
        A(s.activation, tmp, tmp, ACT.Exp, scale=-1.0)
        t = A(s.activation, tmp, tmp, ACT.Ln, bias=1.0)
        V(v.tensor_scalar, out, x, 0.0, None, ALU.min, after=[t])
        return V(v.tensor_tensor, out, tmp, out, ALU.subtract)

    def wide(a, n=4):
        return H[:, a:a + n, :].rearrange("p a t -> p (a t)")

    def attention(items, filler=lambda j: None):
        n = len(items)
        held = [None] * n

        def scores(j):
            it = items[j]
            bank = B[2 + j % 2]
            PE.wait(bank.free)
            PE.wait(*it.get("after", ()))
            w = it["width"]
            ins = pe.matmul(bank[:, 0:w], it["q"], it["k"], start=True, stop=True)
            for m, (lhsT, rhs, c, cw) in enumerate(it["extra"]):
                ins = pe.matmul(bank[:, c:c + cw], lhsT, rhs, start=False, stop=True, skip_group_check=True)
            tok = PE.done(ins)
            c = 8 * (j % 4)
            nm, tot, es = COL[:, c:c + 1], COL[:, c + 1:c + 2], COL[:, c + 2:c + 3]
            probs = PB[:, j % 2, 0:w]
            t = V(v.tensor_reduce, nm, bank[:, 0:w], AXX, ALU.max, negate=True, after=[tok, A.sem.token()])
            if it.get("sink") is not None:
                V(v.tensor_scalar, es, it["sink"], -1.0, None, ALU.mult)
                t = V(v.tensor_tensor, nm, nm, es, ALU.min)
            t = A(s.activation, probs, bank[:, 0:w], ACT.Exp, bias=nm, accum_out=tot,
                  after=[t] + ([held[j - 2]] if j >= 2 else pr.tensor_now()))
            bank.free = [t]
            if it.get("sink") is not None:
                t = A(s.activation, es, it["sink"], ACT.Exp, bias=nm)
                V(v.tensor_tensor, tot, tot, es, ALU.add, after=[t])
            V(v.reciprocal, tot, tot, after=[t])
            if it.get("gate") is not None:
                V(v.tensor_tensor, tot, tot, it["gate"], ALU.mult)
            if it.get("valid") is not None:
                t = V(v.scalar_tensor_tensor, probs, probs, tot, it["valid"], ALU.mult, ALU.mult)
            else:
                t = V(v.tensor_scalar, probs, probs, tot, None, ALU.mult)
            it["ready"] = t

        def turn(j):
            it = items[j]
            bank = B[4 + j % 2]
            w = it["width"]
            PE.wait(bank.free, it["ready"])
            chunks = [(c, min(P, w - c)) for c in range(0, w, P)]
            for c, cw in chunks:
                ins = pe.transpose(bank[0:cw, c:c + P], PB[:, j % 2, c:c + cw], ident)
            tok = PE.done(ins)
            held[j] = tok
            rows = min(P, w)
            cols = P * len(chunks)
            after = [tok] + ([items[j - 2]["used"]] if j >= 2 else pr.tensor_now())
            if j % 2:
                t = V(v.tensor_copy, PT[0:rows, j % 2, 0:cols], bank[0:rows, 0:cols], after=after)
            else:
                t = A(s.activation, PT[0:rows, j % 2, 0:cols], bank[0:rows, 0:cols], ACT.Copy, after=after)
            bank.free = [t]
            it["turned"] = t

        def product(j):
            it = items[j]
            if it["start"]:
                PE.wait(it["bank"].free)
            PE.wait(it["turned"])
            m = len(it["v"])
            for c, lhsT in enumerate(it["v"]):
                rows = min(P, it["width"])
                ins = pe.matmul(it["out"], lhsT, PT[0:rows, j % 2, c * P:c * P + P],
                                start=it["start"] and c == 0, stop=it["stop"] and c == m - 1, skip_group_check=True)
            it["used"] = PE.done(ins)
            if it.get("evac"):
                it["bank"].free = it["evac"](it["used"])

        for j in range(n + 2):
            if j < n:
                scores(j)
            if j < n:
                filler(j)
            if 1 <= j <= n:
                turn(j - 1)
            if j >= 2:
                product(j - 2)

    for k in range(KT):
        bank = B[2 + k % 2]
        PE.wait(bank.free, all_loads)
        for b in range(NTB):
            ins = pe.transpose(bank[:, b * P:b * P + P],
                               H[:, 2 * b + k // 4, (k % 4) * P:(k % 4) * P + P], ident)
        tok = PE.done(ins)
        bank.free = [A(s.activation, X[:, k, :], bank[:, :], ACT.Copy, after=[tok, all_loads])]
    V.wait(all_loads)
    A.wait(all_loads)
    A(s.activation, SC[:, 0, :], vec1("c"), ACT.Silu)
    A(s.activation, SC[:, 1, :], vec1("c2"), ACT.Silu)
    PE.wait(A.sem.token())
    ada.gpsimd_program()

    ada.start(SC[:, 0, :])
    ready = modulate(stage(0))
    u = lambda k: U[:, k, :]
    XR, YR, Q, K_, GG, VT = 0, 4, 8, 10, 12, 16
    RT, IT, AT_ = 20, 24, 28

    def conv4(src, tile, wcol, bias):
        V(v.tensor_scalar, tile, src[:, 0:T], wcol(0), bias, ALU.mult, ALU.add if bias is not None else ALU.bypass)
        for j in range(1, 4):
            t = V(v.scalar_tensor_tensor, tile, src[:, j:j + T], wcol(j), tile, ALU.mult, ALU.add)
        return t

    V(v.memset, TMP[:, :, 0:3], 0.0)
    LS = COL[:, 64:68]
    softplus_neg(LS, vec1("rg_lam"), COL[:, 68:72])
    V(v.tensor_scalar, LS, LS, -8.0, None, ALU.mult)
    for m in range(4):
        def evac(bank, tok, m=m):
            src = TMP[:, m % 2, :]
            t = A(s.activation, src[:, 3:3 + T], bank[:, :], ACT.Copy, after=[tok, V.sem.token()])
            V.wait(t)
            conv4(src, H[:, XR + m, :], lambda j: vec1("conv_w", 4 * j + m, 4 * j + m + 1), vec1("conv_b", m, m + 1))
            return [t]
        gemm(u, KT, evac, ready)
    w = pr.take()
    PE.wait(V.sem.token())
    for half in range(2):
        for m in range(4):
            bank = B[2 + m]
            PE.wait(bank.free)
            ins = pe.matmul(bank[:, :], w[:, 4 * half + m, :], H[:, XR + m, :], start=True, stop=True)
            tok = pr.release(ins) if (half, m) == (1, 3) else PE.done(ins)
            bank.free = [A(s.activation, H[:, (RT, IT)[half] + m, :], bank[:, :], ACT.Sigmoid,
                           bias=vec1(("rg_ba", "rg_bx")[half], m, m + 1), after=[tok])]
    r, i_, a, xr, yr = wide(RT), wide(IT), wide(AT_), wide(XR), wide(YR)
    th = M[:, 4:8, :].rearrange("p a t -> p (a t)")
    rgo = M[:, 0:4, :].rearrange("p a t -> p (a t)")

    def rg_1():
        V(v.tensor_tensor, i_, i_, xr, ALU.mult, after=[A.sem.token()])

    def rg_2():
        for m in range(4):
            A(s.activation, H[:, AT_ + m, :], H[:, RT + m, :], ACT.Exp, scale=LS[:, m:m + 1], after=[V.sem.token()])

    def rg_3():
        for m in range(4):
            A(s.activation, M[:, 4 + m, :], H[:, RT + m, :], ACT.Tanh, scale=LS[:, m:m + 1])

    def rg_4():
        V(v.tensor_scalar, r, th, -1.0, 1.0, ALU.mult, ALU.add, after=[A.sem.token()])
        V(v.reciprocal, r, r)

    def rg_5():
        V(v.tensor_tensor, th, th, r, ALU.mult)

    def rg_6():
        A(s.activation, th, th, ACT.Sqrt, scale=-2.0, after=[V.sem.token()])

    def rg_7():
        V(v.tensor_tensor, i_, i_, th, ALU.mult, after=[A.sem.token()])

    def rg_8():
        for m in range(4):
            V(v.tensor_tensor_scan, M[:, m, :], H[:, AT_ + m, :], H[:, IT + m, :], 0.0, ALU.mult, ALU.add)

    def rg_9():
        A(s.activation, th, yr, ACT.Square, after=[V.sem.token()])

    def rg_10():
        V(v.tensor_scalar, th, th, 0.044715, 1.0, ALU.mult, ALU.add, after=[A.sem.token()])
        V(v.tensor_tensor, th, th, yr, ALU.mult)

    def rg_11():
        A(s.activation, th, th, ACT.Sigmoid, scale=float(2.0 * np.sqrt(2.0 / np.pi)), after=[V.sem.token()])

    def rg_12():
        V(v.tensor_tensor, th, th, yr, ALU.mult, after=[A.sem.token()])
        V(v.tensor_tensor, rgo, rgo, th, ALU.mult)

    ZL = TMP[0:16, 0, 0:T]
    EB, QD, KD, KE, T1, KET = 20, 22, 24, 26, 28, 30

    def gla_1(m):
        tok = matmuls(B[2 + m][:, :], [(vec1("gla_up", m * P, m * P + P, rows=16), ZL)], after=now(), bank=B[2 + m])
        x = H[:, QD + m, :]
        t = A(s.activation, x, B[2 + m][:, :], ACT.Identity, bias=vec1("gla_b", m, m + 1), after=[tok, V.sem.token()])
        B[2 + m].free = [t]
        softplus_neg(H[:, KD + m, :], x, H[:, KE + m, :])

    def gla_2(m):
        la, bc, eb, t1 = (H[:, z + m, :] for z in (KD, KE, EB, T1))
        V(v.tensor_scalar, la, la, -1.0 / 16.0, None, ALU.mult)
        V(v.tensor_tensor_scan, bc, const("chunk_reset"), la, 0.0, ALU.mult, ALU.add)
        A(s.activation, eb, bc, ACT.Exp, after=[V.sem.token()])
        A(s.activation, t1, bc, ACT.Exp, scale=-1.0)

    def gla_3(m):
        qd, kd, bc, eb, t1 = (H[:, z + m, :] for z in (QD, KD, KE, EB, T1))
        V(v.tensor_tensor, qd, H[:, Q + m, :], eb, ALU.mult, after=[A.sem.token()])
        V(v.tensor_tensor, kd, H[:, K_ + m, :], t1, ALU.mult)
        bc3 = bc.rearrange("p (c t) -> p c t", t=GLA_CH)
        t3 = t1.rearrange("p (c t) -> p c t", t=GLA_CH)
        V(v.tensor_tensor, t3, bc3[:, :, GLA_CH - 1:GLA_CH].broadcast_to([P, 8, GLA_CH]), bc3, ALU.subtract)
        t = A(s.activation, t1, t1, ACT.Exp, after=[V.sem.token()])
        V(v.tensor_tensor, bc, H[:, K_ + m, :], t1, ALU.mult, after=[t])

    ket = H[:, KET:KET + 2, :].rearrange("p (b x) t -> p b (x t)", b=1)[:, 0, :].rearrange("p (b k) -> p b k", b=NTB)

    def gla_4(m):
        bank = B[4 + m]
        PE.wait(bank.free, *now())
        for b in range(NTB):
            ins = pe.transpose(bank[:, b * P:b * P + P], H[:, KE + m, b * P:b * P + P], ident)
        tok = PE.done(ins)
        bank.free = [A(s.activation, ket[:, :, m * P:m * P + P], bank[:, :].rearrange("p (b c) -> p b c", b=NTB),
                       ACT.Copy, after=[tok])]

    steps = [rg_1, rg_2, rg_3, rg_4, rg_5, rg_6, rg_7, lambda: (rg_8(), ada.read_group()),
             lambda: gla_1(0), lambda: gla_1(1), lambda: (gla_2(0), gla_2(1)), lambda: gla_3(0), lambda: gla_3(1),
             rg_9, rg_10, rg_11, lambda: (rg_12(), ada.read_group())]
    between += steps
    gemm(u, KT, lambda bank, tok: [A(s.activation, ZL, bank[0:16, :], ACT.Copy, after=[tok, V.sem.token()])])
    for m in range(2):
        gemm(u, KT, lambda bank, tok, m=m: [A(s.activation, H[:, Q + m, :], bank[:, :], ACT.Copy, scale=0.125, after=[tok])])
    for m in range(2):
        gemm(u, KT, lambda bank, tok, m=m: [A(s.activation, H[:, K_ + m, :], bank[:, :], ACT.Copy, after=[tok])])
    vt = H[:, VT:VT + 4, :]
    for m in range(4):
        gemm_tok(u, P, lambda bank, tok, m=m: [A(s.activation, vt[:, :, m * P:m * P + P],
                 bank[:, :].rearrange("p (b c) -> p b c", b=NTB), ACT.Copy, after=[tok])])
    for m in range(4):
        gemm(u, KT, lambda bank, tok, m=m: [A(s.activation, H[:, YR + m, :], bank[:, :], ACT.Copy, after=[tok])])
    for m in range(4):
        gemm(u, KT, lambda bank, tok, m=m: [A(s.activation, H[:, GG + m, :], bank[:, :], ACT.Silu, after=[tok])])
    fill(len(between))
    for m in range(2):
        gla_4(m)
    att = [H[:, XR + z, :] for z in range(2)]
    masked = []
    zero = V(v.memset, H[:, XR:XR + 2, :], 0.0, after=now() + pr.tensor_now())
    PE.wait(B[4].free, B[5].free, *now())
    chunk = lambda c: slice(c * 64, c * 64 + 64)
    for h in range(4):
        hp, ho = h // 2, 64 * (h % 2)
        for c in range(8):
            o, col = 64 * (c % 2), (c // 2) * P + hp * 64
            ins = pe.matmul(B[4 + h % 2][o:o + 64, col:col + 64], H[ho:ho + 64, KD + hp, chunk(c)],
                            H[ho:ho + 64, QD + hp, chunk(c)], start=True, stop=True)
    t_att = PE.done(ins)
    PE.wait(B[2].free, B[3].free, B[6].free, B[7].free)
    kv_bank = lambda c: B[(2, 3, 6, 7)[2 * (c % 2) + c // 4]]
    kv_col = lambda c, hp: ((c // 2) % 2) * 256 + hp * P
    for c in range(8):
        o, b = 64 * (c % 2), c // 2
        for h in range(4):
            hp, ho = h // 2, 64 * (h % 2)
            col = kv_col(c, hp)
            ins = pe.matmul(kv_bank(c)[ho:ho + 64, col:col + P], ket[o:o + 64, b, h * 64:h * 64 + 64],
                            vt[o:o + 64, b, h * P:h * P + P], start=True, stop=True)
    t_kv = PE.done(ins)
    mask = const("gla_mask").bitcast(I32)
    mask8 = mask.rearrange("p (a t) -> p a t", a=1).broadcast_to([P, 8, 64])
    for z in range(2):
        t = V(v.copy_predicated, att[z].rearrange("p (n t) -> p n t", n=8), mask8,
              B[4 + z][:, :].rearrange("p (n t) -> p n t", n=8), after=[t_att])
    B[4].free = B[5].free = [t]
    ST = H[:, AT_:AT_ + 4, :].rearrange("p a (c x) -> p (a c) x", c=2).rearrange("p c (m v) -> p c m v", m=2)
    V(v.memset, ST[:, 0, :, :], 0.0, after=[t_kv])
    for c in range(7):
        for hp in range(2):
            col = kv_col(c, hp)
            t_st = V(v.scalar_tensor_tensor, ST[:, c + 1, hp, :], ST[:, c, hp, :],
                     H[:, EB + hp, c * 64 + 63:c * 64 + 64], kv_bank(c)[:, col:col + P], ALU.mult, ALU.add)
    for z in (2, 3, 6, 7):
        B[z].free = [t_st]
    OG = [Q, Q + 1, K_, K_ + 1]
    o_tok = []
    for hp in range(2):
        banks = (B[0], B[1], B[2], B[3]) if hp == 0 else (B[4], B[5], B[6], B[7])
        PE.wait(*[z.free for z in banks], t_st)
        for e in range(2):
            h, ho = 2 * hp + e, 64 * e
            for c in range(8):
                o, b = 64 * (c % 2), c // 2
                pe.matmul(banks[c % 2][:, e * 256 + b * 64:e * 256 + b * 64 + 64], vt[o:o + 64, b, h * P:h * P + P],
                          att[e][o:o + 64, b * P + hp * 64:b * P + hp * 64 + 64], start=True, stop=True)
                ins = pe.matmul(banks[2 + e][:, chunk(c)], ST[ho:ho + 64, c, hp, :], H[ho:ho + 64, QD + hp, chunk(c)],
                                start=True, stop=True)
        tok = PE.done(ins)
        for e in range(2):
            dst = H[:, OG[2 * hp + e], :].rearrange("p (b o t) -> p b o t", o=2, t=64)
            for o in range(2):
                A(s.activation, dst[:, :, o, :],
                  banks[o][:, e * 256:e * 256 + 256].rearrange("p (b t) -> p b t", b=NTB), ACT.Copy, after=[tok])
            t = V(v.tensor_tensor, H[:, OG[2 * hp + e], :], H[:, OG[2 * hp + e], :], banks[2 + e][:, :], ALU.add,
                  after=[A.sem.token()])
        for z in banks:
            z.free = [t]
    oo, sq, rs = wide(Q), wide(RT), wide(IT)
    A(s.activation, sq, oo, ACT.Square, after=[V.sem.token()] + pr.tensor_now())

    def head_norm(src_tile, o_all, sq0, rs0, gain, out):
        for h in range(4):
            tok = matmuls(B[2 + h][:, :], [(ones, H[:, sq0 + h, :])], after=[A.sem.token()], bank=B[2 + h])
            B[2 + h].free = [V(v.tensor_scalar, H[:, rs0 + h, :], B[2 + h][:, :], 1.0 / P, 1e-6, ALU.mult, ALU.add,
                               after=[tok])]
        t = A(s.activation, wide(rs0), wide(rs0), ACT.Sqrt, after=[V.sem.token()])
        V.wait(t)
        for h in range(4):
            V(v.reciprocal, H[:, rs0 + h, :], H[:, rs0 + h, :])
            V(v.scalar_tensor_tensor, src_tile(h), src_tile(h), gain(h), H[:, rs0 + h, :], ALU.mult, ALU.mult)
            out(h)

    mix_tok = [A.sem.token()] * KT

    def gla_out(h):
        mix_tok[4 + h] = V(v.tensor_tensor, M[:, 4 + h, :], H[:, OG[h], :], H[:, GG + h, :], ALU.mult)

    mix_tok[0:4] = [V.sem.token()] * 4
    head_norm(lambda h: H[:, OG[h], :], oo, RT, IT, lambda h: vec1("gla_g", h, h + 1), gla_out)

    def add_residual(mod, bias=None):
        def evac_of(m):
            def evac(bank, tok):
                tmp = TMP[:, m % 2, 0:T]
                gcol = mod[:, 16 + m:17 + m]
                if bias is None:
                    t = A(s.activation, tmp, bank[:, :], ACT.Copy, scale=gcol, after=[tok, V.sem.token()])
                else:
                    t = A(s.activation, tmp, bank[:, :], ACT.Identity, scale=gcol, bias=bias[:, m:m + 1],
                          after=[tok, V.sem.token()])
                V(v.scalar_tensor_tensor, X[:, m, :], X[:, m, :], ALPHA, tmp, ALU.mult, ALU.add, after=[t])
                return [t]
            return evac
        return evac_of

    def output_gemm(src, ktiles, evac, step, ready=None):
        prev = None
        for m in range(KT):
            gemm(src, ktiles, evac(m), ready)
            if prev is not None:
                step(m - 1, prev)
            prev = V.sem.token()
        return step(KT - 1, prev)

    def project(mod, ready=None):
        plus_one(mod[:, 16:24])
        return output_gemm(mix, KT, add_residual(mod), lambda m, tok: mean_step(B[2], X[:, m, :], m, tok), ready)

    mix = lambda k: M[:, k, :]

    def mlp(l, mod, ready, early, middle, late):
        b1 = VEC1.at["mlp_b1"][0] + 32 * l

        def up(i, j, ready=None):
            def evac(bank, tok):
                h = H[:, bass.ds(i * BODY + j, 1), :].rearrange("p a t -> p (a t)")
                t = A(s.activation, h, bank[:, :], ACT.Relu, bias=V1[:, bass.ds(i * BODY + (b1 + j), 1)], after=[tok])
                V(v.tensor_tensor, h, h, h, ALU.mult, after=[t])
                return [t]
            gemm_split(evac, ready)

        for j in range(BODY):
            up(0, j, ready)
            if j in early:
                ada.read_group()
        with pr.loop(f"mlp_up{l}", FF1 // D - 1, fence=False) as i:
            for j in range(BODY):
                up(i + 1, j)
        gb = COL[:, 72:80]
        plus_one(mod[:, 16:24])
        V(v.tensor_tensor, gb, mod[:, 16:24], vec1("mlp_b2", 8 * l, 8 * l + 8), ALU.mult)
        for _ in range(middle):
            ada.read_group()
        PE.wait(*now())

        def step(m, tok):
            if m in late:
                ada.read_group()
            return mean_step(B[2], X[:, m, :], m, tok)
        return output_gemm(lambda k: H[:, k, :], FF1 // P, add_residual(mod, gb), step)

    ada.read_group()
    tok = project(stage(0), mix_tok)
    ready = layer_norm(tok, vec1("ln_g", 0, 8), vec1("ln_b", 0, 8), stage(1), split=True)
    tok = mlp(0, stage(1), ready, (2, 4), 2, (0, 2, 4, 6))
    ready = layer_norm(tok, vec1("ln_g", 8, 16), vec1("ln_b", 8, 16), stage(2))

    NF = H[0:FOX_H, 31, :]

    def evac_f(bank, tok):
        z, tmp = TMP[0:FOX_H, 0, 0:T], TMP[0:FOX_H, 1, 0:T]
        t = A(s.activation, z, bank[0:FOX_H, :], ACT.Identity, bias=vec1("fox_bf", rows=FOX_H), after=[tok, V.sem.token()])
        softplus_neg(H[0:FOX_H, 30, :], z, tmp)
        V(v.tensor_tensor_scan, NF, const("ones", FOX_H)[:, 0:1].broadcast_to([FOX_H, T]), H[0:FOX_H, 30, :], 0.0,
          ALU.mult, ALU.add)
        return [t]
    gemm(u, KT, evac_f, ready)
    PE.wait(*now())
    QG = COL[:, 80:81]
    V(v.tensor_scalar, QG, vec1("fox_qg"), 0.125, None, ALU.mult)

    def fox_tiles(e):
        return tuple(H[:, 4 * e + z, :] for z in range(4))

    def fox_projections(e):
        q, k_, gt, vt_ = fox_tiles(e)
        vtok = vt_.rearrange("p (b c) -> p b c", b=NTB)
        sq, rs = H[:, 8, :], H[:, 9, :]

        def plain(dst, func, view=lambda z: z):
            return lambda bank, tok: [A(s.activation, dst, view(bank[:, :]), func,
                                        after=[tok, V.sem.token()] + pr.tensor_now())]

        def norm(gain, dst):
            def step():
                t = A(s.activation, sq, dst, ACT.Square, after=pr.tensor_now())
                tok = matmuls(B[1][:, :], [(const("mean64"), sq)], after=[t], bank=B[1])
                inv_sqrt(B[1], tok, 1e-6, rs)
                V(v.scalar_tensor_tensor, dst, dst, gain, rs, ALU.mult, ALU.mult)
            return step
        return [lambda: gemm(u, KT, plain(q, ACT.Copy)), norm(QG, q),
                lambda: gemm(u, KT, plain(k_, ACT.Copy)), norm(vec1("fox_kg"), k_),
                lambda: gemm_tok(u, P, plain(vtok, ACT.Copy, lambda z: z.rearrange("p (b c) -> p b c", b=NTB))),
                lambda: gemm(u, KT, plain(gt, ACT.Sigmoid))]

    def fox_attention(pair, e, steps):
        q, k_, gt, vt_ = fox_tiles(e)
        vtok = vt_.rearrange("p (b c) -> p b c", b=NTB)
        sel = H[0:FOX_H, 10 + e, 0:2 * P]
        c0 = CONST.at["ident"][0]
        V(v.tensor_copy, sel.rearrange("p (a c) -> p a c", a=2),
          C[0:FOX_H, bass.ds(pair * 2 + c0, 2)].rearrange("p (a x) -> p a x", x=1).broadcast_to([FOX_H, 2, P]),
          after=pr.tensor_now())
        items = []
        for hd in range(2):
            hr = slice(64 * hd, 64 * hd + 64)
            for b in range(NTB):
                w_ = (b + 1) * P
                items.append(dict(
                    q=q[hr, b * P:w_], k=k_[hr, 0:w_], width=w_,
                    extra=[(sel[:, hd * P:hd * P + P], NF[:, 0:w_], 0, w_), (ident, const("causal"), b * P, P)],
                    v=[vtok[:, c, hr] for c in range(b + 1)], out=B[6][hr, b * P:w_], bank=B[6],
                    start=True, stop=True))
        items[0]["after"] = now()

        def evac(tok):
            o = M[:, bass.ds(pair, 1), :].rearrange("p a t -> p (a t)")
            return [V(v.tensor_tensor, o, B[6][:, :], gt, ALU.mult, after=[tok, A.sem.token()])]
        items[-1]["evac"] = evac
        todo = list(steps)

        def filler(j):
            if j == 4:
                ada.read_group()
            if todo:
                todo.pop(0)()
        attention(items, filler)
        assert not todo

    for f in fox_projections(0):
        f()
    with pr.loop("fox", KT // 2 - 1) as i:
        fox_attention(i * 2, 0, fox_projections(1))
        fox_attention(i * 2 + 1, 1, fox_projections(0))
    for e in range(2):
        fox_attention(KT - 2 + e, e, fox_projections(1) if e == 0 else [])
    tok = project(stage(2), [now()] * KT)
    ready = layer_norm(tok, vec1("ln_g", 16, 24), vec1("ln_b", 16, 24), stage(3), split=True)
    tok = mlp(1, stage(3), ready, (3,), 1, (3,))
    layer_norm(tok, vec1("ln_g", 24, 32), vec1("ln_b", 24, 32), None)

    mod = MH
    V.wait(A.sem.token())
    with pr.loop("hybrid", L2) as l:
        A.wait(V.sem.token(), *pr.tensor_now())
        tok = A.done(s.dma_start(V2[:, :], io["vec2"][l]), loads, 16)
        V(v.tensor_copy, MH[:, :], MODS[:, bass.ds(l * 48 + (N_ADA - 96), 48)], after=[tok, A.sem.token()])
        A.wait(tok)
        GM, GF = COL[:, 96:104], COL[:, 104:112]
        plus_one(mod[:, 8:16])
        plus_one(mod[:, 32:40])
        V(v.tensor_tensor, GM, mod[:, 8:16], vec2("norm_mix"), ALU.mult)
        V(v.tensor_tensor, GF, mod[:, 32:40], vec2("norm_ffn"), ALU.mult)
        for m in range(KT):
            tok = square_step(m, V.sem.token())
        ready = rms_norm_all(tok, GM, mod[:, 0:8])
        AK, KC, VC, KSW, XK, HID = 0, 1, 2, 3, 4, 6
        AQ, BQ, BQR, AV, VSW, SM, CMP, KS2, KW2, AK2 = 16, 18, 20, 22, 23, 24, 25, 26, 27, 28

        def rope(bank, tok, dst, scale, raw=None):
            x = raw if raw is not None else TMP[:, 0, 0:T]
            t = A(s.activation, x, bank[:, :], ACT.Copy, scale=scale, after=[tok, V.sem.token()] + pr.tensor_now())
            tok2 = matmuls(B[2][:, :], [(const("rot"), x)], after=[t], bank=B[2])
            V(v.tensor_tensor, TMP[:, 1, 0:T], B[2][:, :], const("sin"), ALU.mult, after=[tok2])
            B[2].free = [V.sem.token()]
            V(v.tensor_tensor, dst, x, const("cos"), ALU.mult)
            V(v.tensor_tensor, dst, dst, TMP[:, 1, 0:T], ALU.add)
            return [t]

        for m in range(2):
            gemm(u, KT, lambda bank, tok, m=m: rope(bank, tok, H[:, AQ + m, :], 0.125), ready)
        gemm(u, KT, lambda bank, tok: rope(bank, tok, H[:, AK, :], 1.0))
        for m in range(2):
            gemm(u, KT, lambda bank, tok, m=m: rope(bank, tok, H[:, BQR + m, :], 0.125, raw=H[:, BQ + m, :]))
        for dst in (KC, VC):
            def evac(bank, tok, dst=dst):
                A(s.activation, H[0:64, dst, :], bank[0:64, :], ACT.Copy, after=[tok])
                V(v.memset, H[64:P, dst, T - 1:T], 0.0, after=[A.sem.token()])
                t = A(s.activation, H[64:P, dst, 0:T - 1], bank[64:P, 1:T], ACT.Copy, after=[V.sem.token()])
                return [t]
            gemm(u, KT, evac)
        gemm(u, KT, lambda bank, tok: rope(bank, tok, H[:, KSW, :], 1.0))
        r4 = lambda ap: ap.rearrange("p (b c) -> p b c", b=NTB)
        av, vsw, sm = r4(H[:, AV, :]), r4(H[:, VSW, :]), r4(H[:, SM, :])
        for dst in (av, vsw):
            gemm_tok(u, P, lambda bank, tok, dst=dst: [A(s.activation, dst, r4(bank[:, :]), ACT.Copy, after=[tok])])
        gemm_tok(u, 20, lambda bank, tok: [A(s.activation, sm[:, :, 0:20], r4(bank[:, :])[:, :, 0:20], ACT.Copy,
                                             after=[tok])])
        A(s.activation, sm[:, :, 32:44], sm[:, :, 0:12], ACT.Sigmoid)
        xw = lambda ap: ap.rearrange("p (j n) -> p j n", j=16)
        for which, (src, pos) in enumerate(((KC, "pe_k"), (VC, "pe_v"))):
            x = H[:, XK + which, 0:16 * N_CMP]
            base = H[:, src, :]
            for jp in range(16):
                V(v.tensor_scalar, x[:, jp * N_CMP:(jp + 1) * N_CMP], base[:, 2 * jp:2 * jp + 16 * (N_CMP - 1) + 1:16],
                  vec2(pos, jp, jp + 1), None, ALU.add, after=[A.sem.token()])
        hid = H[:, HID, 0:4 * 32].rearrange("p (w m n) -> p w m n", w=2, m=2)
        for which in range(2):
            x = xw(H[:, XK + which, 0:16 * N_CMP])
            for m in range(2):
                bank = B[2 + m]
                PE.wait(bank.free, V.sem.token())
                for kg in range(2):
                    w = pr.take()
                    for j in range(KT):
                        ins = pe.matmul(bank[:, 0:N_CMP], w[:, j, :], x[:, kg * KT + j, :], start=(kg + j == 0),
                                        stop=(kg == 1 and j == KT - 1))
                    tok = pr.release(ins)
                bank.free = [A(s.activation, hid[:, which, m, 0:N_CMP], bank[:, 0:N_CMP], ACT.Silu, after=[tok])]
        w = pr.take()
        PE.wait(B[2].free, B[3].free, *now())
        for m in range(2):
            pe.matmul(B[2][0:64, 0:N_CMP], w[:, m, 0:64], hid[:, 0, m, 0:N_CMP], start=(m == 0), stop=(m == 1))
        for m in range(2):
            pe.matmul(B[4][64:P, 0:N_CMP], w[:, m, 0:64], hid[:, 0, m, 0:N_CMP], start=(m == 0), stop=(m == 1))
        for m in range(2):
            ins = pe.matmul(B[3][0:N_CMP, 0:64], hid[:, 1, m, 0:N_CMP], w[:, m, 64:128], start=(m == 0), stop=(m == 1))
        tok = pr.release(ins)
        kcmp, vcmp = H[:, CMP, 0:N_CMP], H[0:N_CMP, CMP, 64:128]
        A(s.activation, H[0:64, CMP, 0:N_CMP], B[2][0:64, 0:N_CMP], ACT.Copy, after=[tok])
        A(s.activation, H[64:P, CMP, 0:N_CMP], B[4][64:P, 0:N_CMP], ACT.Copy)
        t = A(s.activation, vcmp, B[3][0:N_CMP, 0:64], ACT.Copy)
        B[2].free = B[3].free = B[4].free = [t]
        PE.wait(B[3].free, *now())
        pe.matmul(B[3][64:P, :], ident[:, 0:64], H[:, KSW, :], start=True, stop=True)
        ins = pe.matmul(B[4][0:64, :], ident[:, 64:P], H[:, KSW, :], start=True, stop=True)
        tok = PE.done(ins)
        A(s.activation, H[64:P, KS2, :], B[3][64:P, :], ACT.Copy, after=[tok])
        A(s.activation, H[0:64, KS2, :], H[0:64, KSW, :], ACT.Copy)
        A(s.activation, H[0:64, KW2, :], B[4][0:64, :], ACT.Copy)
        t = A(s.activation, H[64:P, KW2, :], H[64:P, KSW, :], ACT.Copy)
        B[3].free = B[4].free = [t]
        PE.wait(B[5].free, B[6].free, *now())
        pe.matmul(B[5][64:P, :], ident[:, 0:64], H[:, AK, :], start=True, stop=True)
        ins = pe.matmul(B[6][0:64, :], ident[:, 64:P], H[:, AK, :], start=True, stop=True)
        tok = PE.done(ins)
        A(s.activation, H[64:P, AK2, :], B[5][64:P, :], ACT.Copy, after=[tok])
        A(s.activation, H[0:64, AK2, :], H[0:64, AK, :], ACT.Copy)
        A(s.activation, H[0:64, AK2 + 1, :], B[6][0:64, :], ACT.Copy)
        t = A(s.activation, H[64:P, AK2 + 1, :], H[64:P, AK, :], ACT.Copy)
        B[5].free = B[6].free = [t]

        items = []

        def to_mix(tile, bank):
            return lambda tok: [A(s.activation, M[:, tile, :], bank[:, :], ACT.Copy, after=[tok])]

        for h in range(4):
            hr = slice(64 * (h % 2), 64 * (h % 2) + 64)
            for b in range(NTB):
                lo = max(0, b - 1)
                w_ = (b + 1 - lo) * P
                extra = [(ident, const("causal"), w_ - P, P)]
                if b:
                    extra.append((ident, const("band"), 0, P))
                items.append(dict(q=H[hr, AQ + h // 2, b * P:b * P + P], k=H[hr, AK2 + h // 2, lo * P:(b + 1) * P],
                                  extra=extra, width=w_, sink=vec2("sinks", h, h + 1),
                                  v=[av[:, c, 64 * (h // 2):64 * (h // 2) + 64] for c in range(lo, b + 1)],
                                  out=B[6 + h // 2][hr, b * P:b * P + P], bank=B[6 + h // 2], start=True, stop=True))
            if h % 2:
                items[-1]["evac"] = to_mix(h // 2, B[6 + h // 2])
        items[0]["after"] = now()
        add, mul = const("cmp_add"), const("cmp_mul")
        for h in range(4):
            hr = slice(64 * (h % 2), 64 * (h % 2) + 64)
            for b in range(NTB):
                w_ = (b + 1) * P
                out = dict(out=B[6 + h // 2][hr, b * P:w_], bank=B[6 + h // 2])
                cols = slice(b * N_CMP, (b + 1) * N_CMP)
                gate = lambda n: sm[:, b, 32 + 4 * n + h:33 + 4 * n + h]
                items.append(dict(q=H[hr, BQ + h // 2, b * P:w_], k=kcmp[hr, :], width=N_CMP, gate=gate(0),
                                  extra=[(ident, add[:, cols], 0, N_CMP)], valid=mul[:, cols], v=[vcmp],
                                  start=True, stop=False, **out))
                causal = [(ident, const("causal"), b * P, P)]
                items.append(dict(q=H[hr, BQR + h // 2, b * P:w_], k=H[hr, KS2, 0:w_], width=w_, gate=gate(1),
                                  extra=causal, v=[vsw[:, c, 0:64] for c in range(b + 1)], start=False, stop=False,
                                  **out))
                items.append(dict(q=H[hr, BQR + h // 2, b * P:w_], k=H[hr, KW2, 0:w_], width=w_, gate=gate(2),
                                  extra=causal, v=[vsw[:, c, 64:128] for c in range(b + 1)], start=False, stop=True,
                                  **out))
            if h % 2:
                items[-1]["evac"] = to_mix(2 + h // 2, B[6 + h // 2])

        V(v.memset, TMP[:, :, 0:3], 0.0, after=[A.sem.token()])

        def conv_tile(m):
            def evac(bank, tok):
                src = TMP[:, m % 2, :]
                t = A(s.activation, src[:, 3:3 + T], bank[:, :], ACT.Copy, after=[tok, V.sem.token()])
                V.wait(t)
                conv4(src, H[:, m, :], lambda j: vec2("conv_w", 12 * j + m, 12 * j + m + 1), None)
                A(s.activation, H[:, m, :], H[:, m, :], ACT.Silu, after=[V.sem.token()])
                return [t]
            return lambda: gemm(u, KT, evac)

        def z_tile(m):
            return lambda: gemm(u, KT, lambda bank, tok: [A(s.activation, H[:, 12 + m, :], bank[:, :], ACT.Silu,
                                                            after=[tok])])
        todo = [conv_tile(m) for m in range(12)] + [z_tile(m) for m in range(4)]
        V.wait(*pr.tensor_now())
        attention(items, lambda j: todo.pop(0)() if todo and j % 3 == 0 else None)
        for f in todo:
            f()

        SMC = COL[:, 128:256]
        beta, gcol, gc, gl, bege, gle = (SMC[:, z * 16:z * 16 + 16] for z in range(6))
        c4 = lambda ap: ap.rearrange("p (b h) -> p b h", b=NTB)
        A(s.activation, c4(beta), sm[:, :, 16:20], ACT.Sigmoid, after=now())
        x = c4(gcol)
        for b in range(NTB):
            V(v.tensor_tensor, x[:, b, :], sm[:, b, 12:16], vec2("dt_bias"), ALU.add)
        V(v.tensor_scalar, gcol, gcol, -1.0, None, ALU.mult)
        softplus_neg(gc, gcol, gl)
        t = A(s.activation, COL[:, 84:88], vec2("A_log"), ACT.Exp, after=[V.sem.token()])
        V.wait(t)
        for b in range(NTB):
            V(v.scalar_tensor_tensor, x[:, b, :], c4(gc)[:, b, :], -1.0, COL[:, 84:88], ALU.mult, ALU.mult)
        PE.wait(B[2].free, B[3].free, *now())
        pe.matmul(B[2][:, 0:16], const("tri"), gcol, start=True, stop=True)
        ins = pe.matmul(B[3][:, 0:16], const("one64"), gcol, start=True, stop=True)
        tok = PE.done(ins)
        V(v.tensor_copy, gc, B[2][:, 0:16], after=[tok])
        V(v.tensor_copy, gl, B[3][:, 0:16])
        B[2].free = B[3].free = [V.sem.token()]
        V(v.tensor_tensor, gle, gl, gc, ALU.subtract)
        A(s.activation, gle, gle, ACT.Exp, after=[V.sem.token()])
        t = A(s.activation, bege, gc, ACT.Exp)
        V(v.tensor_tensor, bege, bege, beta, ALU.mult, after=[t])
        V(v.tensor_scalar, gl, gc, -1.0, None, ALU.mult)
        ngc = gl
        A(s.activation, U[:, 0:8, :].rearrange("p a t -> p (a t)"), wide(0, 8), ACT.Square,
          after=[V.sem.token()] + pr.tensor_now())
        sq_tok = A.sem.token()
        NR = lambda n: H[:, 24 + n, :]
        for n in range(8):
            bank = B[2 + n % 4]
            tok = matmuls(bank[:, :], [(ones, U[:, n, :])], after=[sq_tok], bank=bank)
            bank.free = [V(v.tensor_scalar, NR(n), bank[:, :], 1e-6, None, ALU.add, after=[tok])]
        for z in range(2):
            t = A(s.activation, wide(24 + 4 * z), wide(24 + 4 * z), ACT.Sqrt, after=[V.sem.token()])
            V(v.reciprocal, wide(24 + 4 * z), wide(24 + 4 * z), after=[t])
            V(v.scalar_tensor_tensor, wide(4 * z), wide(4 * z), (float(P) ** -0.5, 1.0)[z], wide(24 + 4 * z),
              ALU.mult, ALU.mult)
        QK, WT = 16, 20
        UT, KDEC = 4, 8
        KBT, ATL, XM, XTM, PM, KBG, VBT, EG = range(8)
        glast = COL[:, 16:48]
        blk = lambda b: slice(b * P, b * P + P)
        v4 = lambda ap: ap.rearrange("p (b c) -> p b c", b=NTB)
        over = lambda ap: ap.rearrange("p (a c) -> p a c", a=1).broadcast_to([P, NTB, P])
        lev = const("levels")
        for pair in range(2):
            hs = (2 * pair, 2 * pair + 1)
            W = [lambda n: H[:, 24 + n, :], lambda n: U[:, n, :]]
            col = lambda a, h: c4(a)[:, :, h:h + 1].broadcast_to([P, NTB, P])
            level_mask = lambda e, k: M[:, 4 + 2 * e + k % 2, :]
            start = now()
            t_tok, t_rows = [0, 0], [0, 0]
            for e, h in enumerate(hs):
                for n, src in enumerate((4 + h, 8 + h)):
                    bank = B[2 + 3 * e + n]
                    PE.wait(bank.free, *start)
                    for b in range(NTB):
                        ins = pe.transpose(bank[:, blk(b)], H[:, src, blk(b)], ident)
                    t_tok[e] = PE.done(ins)
                PE.wait(B[4 + 3 * e].free, B[e].free)
                for b in range(NTB):
                    pe.matmul(B[4 + 3 * e][:, blk(b)], c4(gcol)[:, b, h:h + 1].broadcast_to([P, P]), const("tri"),
                              start=True, stop=True)
                    ins = pe.matmul(B[e][:, blk(b)], c4(beta)[:, b, h:h + 1].broadcast_to([P, P]), ident,
                                    start=True, stop=True)
                t_rows[e] = PE.done(ins)
            t_kb, t_dec = [0, 0], [0, 0]
            for e, h in enumerate(hs):
                w = W[e]
                for b in range(NTB):
                    V(v.scalar_tensor_tensor, w(PM)[:, blk(b)], B[4 + 3 * e][:, blk(b)], c4(ngc)[:, b, h:h + 1],
                      const("decay_mask"), ALU.add, ALU.add, after=[t_rows[e], A.sem.token()] + pr.tensor_now())
                A(s.activation, w(PM), w(PM), ACT.Exp, after=[V.sem.token()])
                t_dec[e] = A(s.activation, w(EG), B[4 + 3 * e][:, :], ACT.Exp, after=pr.tensor_now())
                B[4 + 3 * e].free = [t_dec[e]]
                t_kb[e] = V(v.tensor_tensor, w(KBT), H[:, 4 + h, :], B[e][:, :], ALU.mult)
                B[e].free = [t_kb[e]]
                V(v.tensor_tensor, v4(w(KBG)), v4(B[2 + 3 * e][:, :]), col(bege, h), ALU.mult)
                V(v.tensor_tensor, v4(w(VBT)), v4(B[3 + 3 * e][:, :]), col(beta, h), ALU.mult)
                t = V(v.tensor_tensor, v4(H[:, KDEC + h, :]), v4(B[2 + 3 * e][:, :]), col(gle, h), ALU.mult)
                B[2 + 3 * e].free = B[3 + 3 * e].free = [t]
            for e, h in enumerate(hs):
                w = W[e]
                PE.wait(B[2 + 3 * e].free, B[3 + 3 * e].free, t_kb[e])
                for b in range(NTB):
                    pe.matmul(B[2 + 3 * e][:, blk(b)], H[:, 4 + h, blk(b)], w(KBT)[:, blk(b)], start=True, stop=True)
                    ins = pe.matmul(B[3 + 3 * e][:, blk(b)], H[:, 4 + h, blk(b)], H[:, h, blk(b)], start=True, stop=True)
                t_kk = PE.done(ins)
                V(v.tensor_tensor, w(ATL), B[2 + 3 * e][:, :], w(PM), ALU.mult, after=[t_kk, t_dec[e]])
                t = V(v.tensor_tensor, H[:, QK + h, :], B[3 + 3 * e][:, :], w(PM), ALU.mult)
                B[2 + 3 * e].free = B[3 + 3 * e].free = [t]
                V(v.tensor_copy, glast[:, 8 * h:8 * h + 8], w(EG)[:, 63::64])
                V(v.tensor_tensor, v4(w(XM)), v4(w(ATL)), over(lev[:, 0:P]), ALU.mult)
                t = V(v.tensor_tensor, v4(w(XTM)), over(ident), v4(w(XM)), ALU.subtract)
                bank = B[4 + 3 * e]
                PE.wait(bank.free, t)
                for b in range(NTB):
                    ins = pe.transpose(bank[:, blk(b)], w(XTM)[:, blk(b)], ident)
                tok = PE.done(ins)
                V(v.tensor_tensor, H[:, h, :], H[:, h, :], w(EG), ALU.mult)
                bank.free = [A(s.activation, w(XM), bank[:, :], ACT.Copy, after=[tok, t])]
            t_xm = [A.sem.token()] * 2
            t_mask = [0, 0]
            atl_ready = V.sem.token()
            t_used = [pr.tensor_now()] * 2
            for e in range(2):
                t_mask[e] = V(v.tensor_tensor, v4(level_mask(e, 1)), v4(W[e](ATL)), over(lev[:, P:2 * P]), ALU.mult,
                              after=[atl_ready, A.sem.token()] + t_used[e])
            for k in range(1, 6):
                t_p, t_pc = [0, 0], [0, 0]
                for e in range(2):
                    w = W[e]
                    bank = B[2 + 3 * e]
                    PE.wait(bank.free, t_mask[e], t_xm[e])
                    for b in range(NTB):
                        ins = pe.matmul(bank[:, blk(b)], level_mask(e, k)[:, blk(b)], w(XM)[:, blk(b)], start=True, stop=True)
                    t_p[e] = PE.done(ins)
                    if k < 5:
                        t_mask[e] = V(v.tensor_tensor, v4(level_mask(e, k + 1)), v4(w(ATL)),
                                      over(lev[:, (k + 1) * P:(k + 2) * P]), ALU.mult, after=[t_p[e]])
                    t_pc[e] = A(s.activation, w(PM), bank[:, :], ACT.Copy, after=[t_p[e], V.sem.token()])
                    bank.free = [t_pc[e]]
                t_xm2 = [0, 0]
                for e in range(2):
                    w = W[e]
                    PE.wait(B[3 + 3 * e].free, B[4 + 3 * e].free, t_pc[e])
                    if k < 5:
                        for b in range(NTB):
                            ins = pe.matmul(B[4 + 3 * e][:, blk(b)], w(XTM)[:, blk(b)], w(PM)[:, blk(b)], start=True, stop=True)
                        t_q = PE.done(ins)
                    for b in range(NTB):
                        ins = pe.matmul(B[3 + 3 * e][:, blk(b)], w(PM)[:, blk(b)], w(XTM)[:, blk(b)], start=True, stop=True)
                    t_qt = PE.done(ins)
                    if k < 5:
                        t_xm2[e] = V(v.tensor_tensor, w(XM), w(XM), B[4 + 3 * e][:, :], ALU.subtract, after=[t_q, t_xm[e]])
                        B[4 + 3 * e].free = [t_xm2[e]]
                    t_xt = V(v.tensor_tensor, w(XTM), w(XTM), B[3 + 3 * e][:, :], ALU.subtract, after=[t_qt])
                    B[3 + 3 * e].free = [t_xt]
                    if k == 5:
                        t_xm2[e] = t_xt
                t_xm = t_xm2
            for e, h in enumerate(hs):
                w = W[e]
                PE.wait(B[2 + 3 * e].free, B[3 + 3 * e].free, t_xm[e])
                for b in range(NTB):
                    pe.matmul(B[2 + 3 * e][:, blk(b)], w(XTM)[:, blk(b)], w(VBT)[:, blk(b)], start=True, stop=True)
                    ins = pe.matmul(B[3 + 3 * e][:, blk(b)], w(KBG)[:, blk(b)], w(XTM)[:, blk(b)], start=True, stop=True)
                tok = PE.done(ins)
                A(s.activation, H[:, UT + h, :], B[2 + 3 * e][:, :], ACT.Copy, after=[tok])
                t = A(s.activation, H[:, WT + h, :], B[3 + 3 * e][:, :], ACT.Copy)
                B[2 + 3 * e].free = B[3 + 3 * e].free = [t]
        ST2 = H[:, 24, :].rearrange("p (h e) -> p h e", h=GH)
        VN = H[:, 25, :].rearrange("p (h e) -> p h e", h=GH)
        t_st = [V(v.memset, ST2, 0.0, after=now() + pr.tensor_now())]
        PE.wait(*now())
        t_read = pr.tensor_now()
        for c in range(8):
            b, o = c // 2, 64 * (c % 2)
            ck = slice(c * 64, c * 64 + 64)
            bw, bo, bs = B[2 + c % 2], B[4 + c % 2], B[6 + c % 2]
            PE.wait(bw.free, t_st)
            for h in range(GH):
                ins = pe.matmul(bw[o:o + 64, h * P:h * P + P], H[:, WT + h, ck], ST2[:, h, :], start=True, stop=True)
            tok = PE.done(ins)
            t_vn = V(v.tensor_tensor, VN[o:o + 64, :, :], H[o:o + 64, UT:UT + GH, blk(b)],
                     bw[o:o + 64, :].rearrange("p (h e) -> p h e", h=GH), ALU.subtract, after=[tok] + t_read)
            bw.free = [t_vn]
            PE.wait(bo.free, bs.free, t_vn)
            for h in range(GH):
                ins = pe.matmul(bs[:, h * P:h * P + P], H[o:o + 64, KDEC + h, blk(b)], VN[o:o + 64, h, :], start=True,
                                stop=True)
            t_kv = PE.done(ins)
            for h in range(GH):
                pe.matmul(bo[:, h * 64:h * 64 + 64], ST2[:, h, :], H[:, h, ck], start=True, stop=False,
                          skip_group_check=True)
                ins = pe.matmul(bo[:, h * 64:h * 64 + 64], VN[o:o + 64, h, :], H[o:o + 64, QK + h, ck], start=False,
                                stop=True, skip_group_check=True)
            t_o = PE.done(ins)
            t_read = [t_o]
            for h in range(GH):
                t = V(v.scalar_tensor_tensor, ST2[:, h, :], ST2[:, h, :], glast[:, 8 * h + c:8 * h + c + 1],
                      bs[:, h * P:h * P + P], ALU.mult, ALU.add, after=[t_kv, t_o])
            t_st = [t]
            bs.free = [t]
            bo.free = [A(s.activation, M[:, 4:8, ck], bo[:, 0:256].rearrange("p (h t) -> p h t", h=GH), ACT.Copy,
                         after=[t_o, V.sem.token()])]
        mo = M[:, 4:8, :].rearrange("p a t -> p (a t)")
        A(s.activation, wide(24), mo, ACT.Square, after=[V.sem.token()] + pr.tensor_now())
        mix_tok[0:4] = [A.sem.token()] * 4

        def gdn_out(h):
            mix_tok[4 + h] = V(v.tensor_tensor, M[:, 4 + h, :], M[:, 4 + h, :], H[:, 12 + h, :], ALU.mult)
        head_norm(lambda h: M[:, 4 + h, :], mo, 24, 28, lambda h: vec2("gdn_norm"), gdn_out)

        def add_gated(gate0):
            return lambda m: (lambda bank, tok: [V(v.scalar_tensor_tensor, X[:, m, :], bank[:, :],
                                                   mod[:, gate0 + m:gate0 + m + 1], X[:, m, :], ALU.mult, ALU.add,
                                                   after=[tok])])
        tok = output_gemm(mix, KT, add_gated(16), square_step, mix_tok)
        ready = rms_norm_all(tok, GF, mod[:, 24:32], split=True)
        turn = [0]

        def gate_up(m_ap, ready=None):
            turn[0] ^= 1
            tmp = H[:, 30 + turn[0], :]
            gemm_split(lambda bank, tok: [A(s.activation, tmp, bank[:, :], ACT.Silu, after=[tok, V.sem.token()])],
                       ready)
            gemm_split(lambda bank, tok: [V(v.tensor_tensor, m_ap, bank[:, :], tmp, ALU.mult,
                                            after=[tok, A.sem.token()])])
        first = FF2_T % 4 + 4
        for j in range(first):
            gate_up(H[:, j, :], ready)
        with pr.loop("gate_up", (FF2_T - first) // 4, fence=False) as i:
            for j in range(4):
                gate_up(H[:, bass.ds(i * 4 + (first + j), 1), :].rearrange("p a t -> p (a t)"))
        PE.wait(*now())
        output_gemm(lambda k: H[:, k, :], FF2_T, add_gated(40), lambda m, tok: tok)

    for m in range(KT):
        tok = square_step(m, V.sem.token())
    rms_norm_all(tok, vec1("final"), None)
    stored = pr.count("stored")
    for b in range(NTB):
        for half in range(2):
            bank = B[4 + half]
            PE.wait(bank.free, *now())
            for k in range(4):
                ins = pe.transpose(bank[:, k * P:k * P + P], U[:, 4 * half + k, b * P:b * P + P], ident)
            tok = PE.done(ins)
            t = A(s.activation, M[:, 2 * b + half, :], bank[:, :], ACT.Copy, after=[tok])
            bank.free = [t]
    A.wait(A.sem.token())
    A.done(s.dma_start(io["out"].rearrange("(b p) d -> p b d", p=P),
                       M[:, :, :].rearrange("p (b h) t -> p b (h t)", b=NTB)), stored, 16)
    A.wait(stored.token())
    assert pr.panel == n_panels, (pr.panel, n_panels)
    assert ada.made.const * GROUP + N_START == N_ADA
    return pr.found


def free_sem(pr):
    return pr.used.handle


def kernel(**inputs):
    import concourse.bacc as bacc
    from concourse.bass_utils import run_bass_kernel_spmd

    i = {k: np.asarray(a) for k, a in inputs.items()}
    arrays = {
        "x": np.ascontiguousarray(i["x"][0]),
        "consts": constants(),
        "vec1": vectors1(i),
        "vec2": np.stack([vectors2(i, l) for l in range(L2)]),
    }
    arrays["stream"], arrays["ada"] = weight_streams(i)

    def program(plan):
        nc = bacc.Bacc("TRN2", target_bir_lowering=False, num_devices=1)
        io = {k: nc.dram_tensor(k, a.shape, F32, kind="ExternalInput").ap() for k, a in arrays.items()}
        io["out"] = nc.dram_tensor("out", (T, D), F32, kind="ExternalOutput").ap()
        return nc, build(nc, io, N_START + N_MAIN, plan)

    _, plan = program({})
    nc, again = program(plan)
    assert again == plan
    r = run_bass_kernel_spmd(nc, [arrays], core_ids=[0])
    return r.results[0]["out"].reshape(1, T, D)
```

```python
import numpy as np
import concourse.bass as bass
from concourse import mybir
from concourse.alu_op_type import AluOpType as ALU

P = 128
D = 1024
T = 512
KT = D // P
NTB = T // P
RING = 4
BODY = RING
F32 = mybir.dt.float32
F32R = mybir.dt.float32r
I32 = mybir.dt.int32
ACT = mybir.ActivationFunctionType
AXX = mybir.AxisListType.X
NEG = -1e30

L1 = 2
RGW = 512
GLA_CH = 64
ALPHA = float((2 * L1) ** 0.25)
FF1 = 4096
FOX_H = 16
L2 = 2
FF2 = 2816
FF2_T = FF2 // P
HALF = 16
N_CMP = T // 16 - 1
GH = 4
N_MAIN = 423
N_START = 16
GROUP = 8
N_ADA = 2 * L1 * 24 + L2 * 48



class Columns:

    def __init__(self, items):
        self.at, self.n = {}, 0
        for name, width in items:
            self.at[name] = (self.n, width)
            self.n += width


CONST = Columns([("ident", 128), ("ones", 128), ("mean", 128), ("one64", 128), ("mean64", 128), ("tri", 128),
                 ("rot", 128), ("causal", 128), ("band", 128), ("decay_mask", 128), ("strict", 128),
                 ("levels", 6 * 128), ("gla_mask", 64), ("chunk_reset", T), ("cos", T), ("sin", T),
                 ("cmp_add", NTB * N_CMP), ("cmp_mul", NTB * N_CMP), ("eps", 2)])
VEC1 = Columns([("c", 8), ("ada_b", N_ADA), ("ln_g", 32), ("ln_b", 32), ("conv_w", 16), ("conv_b", 4),
                ("rg_ba", 4), ("rg_bx", 4), ("rg_lam", 4), ("gla_b", 2), ("gla_g", 4), ("gla_up", 256),
                ("fox_bf", 1), ("fox_qg", 1), ("fox_kg", 1), ("mlp_b1", 64), ("mlp_b2", 16), ("c2", 8),
                ("final", 8)])
VEC2 = Columns([("norm_mix", 8), ("norm_ffn", 8), ("conv_w", 48), ("gdn_norm", 1), ("sinks", 4),
                ("A_log", 4), ("dt_bias", 4), ("pe_k", 16), ("pe_v", 16)])


def constants():
    out = np.zeros((P, CONST.n), np.float32)

    def put(name, a, rows=P):
        c, w = CONST.at[name]
        out[:rows, c:c + w] = np.asarray(a, np.float32).reshape(rows, w)

    r, c = np.arange(P)[:, None], np.arange(P)[None, :]
    same = r // 64 == c // 64
    put("ident", r == c)
    put("ones", np.ones((P, P)))
    put("mean", np.full((P, P), 1.0 / D))
    put("one64", same)
    put("mean64", same / 64.0)
    put("tri", same & (r <= c))
    rot = np.zeros((P, P))
    for h in (0, 64):
        for d in range(32):
            rot[h + 32 + d, h + d] = -1.0
            rot[h + d, h + 32 + d] = 1.0
    put("rot", rot)
    put("causal", np.where(c <= r, 0.0, NEG))
    put("band", np.where(c > r, 0.0, NEG))
    put("decay_mask", np.where(same & (r <= c), 0.0, NEG))
    put("strict", same & (r < c))
    put("levels", np.stack([((c >> k) & 1 == 1) & ((r >> k) & 1 == 0) & (r >> (k + 1) == c >> (k + 1))
                            for k in range(6)], 1))
    put("gla_mask", np.tile(np.triu(np.ones((64, 64))), (2, 1)))
    t = np.arange(T)
    put("chunk_reset", np.broadcast_to(t % 64 != 0, (P, T)))
    inv = (1.0 / (10000.0 ** (np.arange(0, 64, 2, dtype=np.float32) / 64))).astype(np.float32)
    ang = (t.astype(np.float32)[None, :] * inv[:, None]).astype(np.float32)
    put("cos", np.tile(np.cos(ang), (4, 1)))
    put("sin", np.tile(np.sin(ang), (4, 1)))
    ends = np.arange(N_CMP) * 16 + 31
    valid = ends[None, None, :] <= (np.arange(NTB)[None, :, None] * P + np.arange(P)[:, None, None])
    put("cmp_add", np.where(valid, 0.0, NEG))
    put("cmp_mul", valid)
    put("eps", np.tile(np.float32([1e-5, 1e-6]), (P, 1)))
    return out


def columns_of(v):
    v = np.asarray(v)
    return np.ascontiguousarray(v.reshape(-1, P).T)


def pack(layout, values):
    out = np.zeros((P, layout.n), np.float32)
    for name, (c, w) in layout.at.items():
        a = values[name]
        out[:a.shape[0], c:c + w] = a
    return out


def panels_of(w):
    k, n = w.shape
    pk, pn = -k % D, -n % P
    if pk or pn:
        w = np.pad(w, ((0, pk), (0, pn)))
    kg, m = w.shape[0] // D, w.shape[1] // P
    return w.reshape(kg, KT, P, m, P).transpose(3, 0, 2, 1, 4).reshape(m * kg, P, KT * P)


def weight_streams(i):
    main, ada = [], []
    for l in range(L1):
        for s in range(2):
            ada.append(panels_of(i["ada_w"][l, s]))
    for l in range(L2):
        ada.append(panels_of(i["ada_w_2"][l]))

    def add(w):
        main.append(panels_of(w))

    def add_mlp(l):
        for a in range(0, FF1, HALF * P):
            add(i["mlp_w1"][l][:, a:a + HALF * P])
            add(i["mlp_w2"][l][a:a + HALF * P])

    ev = i["ev_w_in"][0]
    add(ev[:, 0:RGW])
    rg = np.zeros((P, 8, P), np.float32)
    for g, w in enumerate((i["ev_rg_wa"][0], i["ev_rg_wx"][0])):
        for b in range(8):
            o = 64 * (b % 2)
            rg[o:o + 64, 4 * g + b // 2, o:o + 64] = w[b]
    main.append(rg.reshape(1, P, KT * P))
    add(ev[:, 2560:])
    add(ev[:, 1024:2048])
    add(ev[:, RGW:1024])
    add(ev[:, 2048:2560])
    add(i["ev_w_out"][0])
    add_mlp(0)
    od = i["od_w_in"][0]
    add(od[:, 4 * D:])
    for hp in range(KT):
        for s in range(4):
            add(od[:, s * D + hp * P:s * D + hp * P + P])
    add(i["od_w_out"][0])
    add_mlp(1)
    for l in range(L2):
        w = i["w_in_2"][l]
        add(w[:, 0:384])
        add(w[:, 512:768])
        for a, b in ((768, 768), (832, 832), (896, 1024)):
            add(np.concatenate([w[:, a:a + 64], w[:, b:b + 64]], 1))
        add(w[:, 384:512])
        add(np.concatenate([w[:, 960:1024], w[:, 1088:1152]], 1))
        add(np.concatenate([w[:, 1152:1164], w[:, 3212:3220]], 1))
        add(w[:, 2188:2956])
        add(i["cmp_k_w1_2"][l])
        add(i["cmp_v_w1_2"][l])
        add(w[:, 2956:3084])
        add(np.concatenate([i["cmp_k_w2_2"][l], i["cmp_v_w2_2"][l]], 1))
        add(w[:, 3084:3212])
        add(w[:, 1164:2188])
        add(i["w_out_2"][l])
        gu = i["w_gate_up_2"][l]
        for a in range(0, FF2_T, HALF):
            for m in range(a, min(a + HALF, FF2_T)):
                add(gu[:, m * P:m * P + P])
                add(gu[:, FF2 + m * P:FF2 + m * P + P])
            add(i["w_down_2"][l][a * P:(a + HALF) * P])
    ada = np.concatenate(ada)
    rest = np.concatenate([ada[N_START:], np.zeros((2, P, KT * P), np.float32)])
    return np.concatenate([ada[:N_START]] + main), rest


def vectors1(i):
    two = lambda g: np.concatenate([g, g])[:, None]
    return pack(VEC1, {
        "c": columns_of(i["c"]), "ada_b": np.concatenate([columns_of(i["ada_b"]), columns_of(i["ada_b_2"])], 1),
        "ln_g": columns_of(i["ln_g"]),
        "ln_b": columns_of(i["ln_b"]), "conv_w": columns_of(i["ev_conv_w"]), "conv_b": columns_of(i["ev_conv_b"]),
        "rg_ba": columns_of(i["ev_rg_ba"]), "rg_bx": columns_of(i["ev_rg_bx"]), "rg_lam": columns_of(i["ev_rg_lam"]),
        "gla_b": columns_of(i["ev_gla_b_up"]), "gla_g": columns_of(i["ev_gla_norm_g"]), "gla_up": i["ev_gla_w_up"][0],
        "fox_bf": i["od_b_f"].reshape(FOX_H, 1), "fox_qg": two(i["od_q_norm_g"][0]), "fox_kg": two(i["od_k_norm_g"][0]),
        "mlp_b1": columns_of(i["mlp_b1"]), "mlp_b2": columns_of(i["mlp_b2"]), "c2": columns_of(i["c_2"]),
        "final": columns_of(i["final_norm_2"])})


def vectors2(i, l):
    rows = lambda v: np.broadcast_to(v[None, :], (P, v.shape[0]))
    return pack(VEC2, {
        "norm_mix": columns_of(i["norm_mix_2"][l]),
        "norm_ffn": columns_of(i["norm_ffn_2"][l]), "conv_w": columns_of(i["gdn_conv_w_2"][l]),
        "gdn_norm": columns_of(i["gdn_norm_2"][l]), "sinks": rows(i["attn_sinks_2"][l]),
        "A_log": rows(i["gdn_A_log_2"][l]), "dt_bias": rows(i["gdn_dt_bias_2"][l]),
        "pe_k": columns_of(i["cmp_pe_k_2"][l]), "pe_v": columns_of(i["cmp_pe_v_2"][l])})




class Count:

    def __init__(self, handle):
        self.handle, self.const, self.terms = handle, 0, ()

    def token(self):
        return (self, self.const, self.terms)


class Engine:

    def __init__(self, prog, eng, sem, chained):
        self.prog, self.eng, self.sem, self.chained, self.seen = prog, eng, sem, chained, {}

    def wait(self, *tokens):
        for t in tokens:
            if isinstance(t, list):
                self.wait(*t)
                continue
            sem, const, terms = t
            known = [x[0] for x in self.prog.loops]
            assert all(x[0] in known for x in terms), "a token of a loop that has ended"
            if const == 0 and not terms:
                continue
            old = self.seen.get(id(sem))
            if old is not None and old[1] == terms and old[0] >= const:
                continue
            self.seen[id(sem)] = (const, terms)
            value = const
            for loop, k in terms:
                if k:
                    value = loop.i * k + value
            self.eng.wait_ge(sem.handle, value)

    def done(self, ins, sem=None, by=1):
        sem = sem or self.sem
        ins.then_inc(sem.handle, by)
        sem.const += by
        return sem.token()

    def __call__(self, op, *args, after=(), **kw):
        if self.chained:
            self.wait(self.sem.token())
        self.wait(*after)
        return self.done(op(*args, **kw))


class Loop:
    i = None


class Program:
    def __init__(self, nc, plan):
        self.nc, self.plan, self.found, self.loops = nc, plan, {}, []
        self.sems = []
        self.V = Engine(self, nc.vector, self.count("vector_done"), True)
        self.A = Engine(self, nc.scalar, self.count("scalar_done"), True)
        self.G = Engine(self, nc.gpsimd, self.count("gpsimd_done"), True)
        self.PE = Engine(self, nc.tensor, self.count("tensor_done"), False)
        self.used = self.count("panels_used")
        self.landed = [self.count(f"panel_landed_{k}") for k in range(RING)]
        self.split = None
        self.hidden = []
        self.panel = 0
        self.banks = [Bank(nc.alloc_psum_tensor(f"bank{k}", [P, 512], F32)) for k in range(8)]

    def count(self, name):
        c = Count(self.nc.alloc_semaphore(name))
        self.sems.append(c)
        return c

    def tensor_now(self):
        return [self.PE.sem.token(), self.used.token()]

    def engines_seen_clear(self):
        for e in (self.V, self.A, self.G, self.PE):
            e.seen = {}

    def loop(self, name, trips, fence=True):
        return LoopScope(self, name, trips, fence)

    def take(self):
        slot = self.panel % RING
        self.split = None
        self.PE.wait(self.landed[slot].token_after(16))
        return self.ring[:, slot, :].rearrange("p (k c) -> p k c", k=KT)

    def release(self, matmul):
        slot = self.panel % RING
        self.landed[slot].const += 16
        self.panel += 1
        return self.PE.done(matmul, self.used)


def _token_after(self, by):
    return (self, self.const + by, self.terms)


Count.token_after = _token_after


class Bank:

    def __init__(self, t):
        self.t, self.free = t, []

    def __getitem__(self, k):
        return self.t[k]


class LoopScope:

    def __init__(self, prog, name, trips, fence):
        self.prog, self.name, self.trips, self.fence = prog, name, trips, fence

    def __enter__(self):
        p = self.prog
        self.scope = p.nc.Fori(0, self.trips, engines=(mybir.EngineType.PE, mybir.EngineType.Activation,
                                                       mybir.EngineType.DVE))
        self.loop = Loop()
        self.loop.i = self.scope.__enter__()
        self.start = [c.const for c in p.sems]
        per = p.plan.get(self.name, [0] * len(p.sems))
        for c, k in zip(p.sems, per):
            c.terms = c.terms + ((self.loop, k),)
        p.loops.append((self.loop, self.name))
        self.first = p.panel
        p.engines_seen_clear()
        if self.fence:
            p.PE.wait(p.V.sem.token(), p.A.sem.token())
            p.split = None
            for b in p.banks:
                b.free = []
        else:
            step = {id(c): (self.loop, k) for c, k in zip(p.sems, per)}
            self.carry(lambda t: (t[0], t[1], t[2] + (step[id(t[0])],)))
        return self.loop.i

    def carry(self, move):
        def moved(t):
            return [moved(x) for x in t] if isinstance(t, list) else move(t)
        p = self.prog
        if p.split is not None:
            p.split = moved(p.split)
        p.hidden = moved(p.hidden)
        for b in p.banks:
            b.free = moved(b.free)

    def __exit__(self, *e):
        p = self.prog
        per = [c.const - s for c, s in zip(p.sems, self.start)]
        p.found[self.name] = per
        for c, s, k in zip(p.sems, self.start, per):
            c.const = s + k * self.trips
            c.terms = c.terms[:-1]
        p.loops.pop()
        used = p.panel - self.first
        assert used % RING == 0
        p.panel = self.first + used * self.trips
        self.scope.__exit__(None, None, None)
        p.engines_seen_clear()
        if self.fence:
            p.split = None
            for b in p.banks:
                b.free = [p.V.sem.token(), p.A.sem.token()]
        else:
            self.carry(lambda t: (t[0], t[1] + t[2][-1][1] * (self.trips - 1), t[2][:-1]))




def build(nc, io, n_panels, plan):
    pr = Program(nc, plan)
    V, A, G, PE = pr.V, pr.A, pr.G, pr.PE
    v, s, g, pe = nc.vector, nc.scalar, nc.gpsimd, nc.tensor
    B = pr.banks

    def sb(name, shape, dt=F32):
        return nc.alloc_sbuf_tensor(name, shape, dt)

    def sb_alias(name, base_after, shape, dt):
        return nc.alloc_sbuf_tensor_at(name, shape, dt, offset=base_after - 4 * int(np.prod(shape[1:])))

    X = sb("residual", [P, KT, T])
    U = sb("mixer_in", [P, KT, T])
    UHI = sb_alias("mlp_in_high", nc.sbuf_base, [P, KT, T], F32R)
    M = sb("mixer_out", [P, KT, T])
    ULO = sb_alias("mlp_in_low", nc.sbuf_base, [P, KT, T], F32R)
    H = sb("hidden", [P, 32, T])
    HSPLIT = sb_alias("hidden_split", nc.sbuf_base, [P, 2, HALF, T], F32R)
    ring = sb("weight_ring", [P, RING, KT * P])
    pr.ring = ring
    WHI = sb("weights_high", [P, 2, KT * P], F32R)
    WLO = sb("weights_low", [P, 2, KT * P], F32R)
    C = sb("constants", [P, CONST.n])
    V1 = sb("vectors1", [P, VEC1.n])
    V2 = sb("vectors2", [P, VEC2.n])
    MODS = sb("modulations", [P, N_ADA])
    MH = sb("modulation_of_layer", [P, 48])
    SC = sb("silu_c", [P, 2, 8])
    AW = sb("modulation_panels", [P, 2, KT * P])
    AP_ = sb("modulation_products", [P, KT * P])
    AR = sb("modulation_sums", [P, 2, GROUP * P])
    COL = sb("columns", [P, 256])
    PB = sb("probs", [P, 3, T])
    PT = sb("probs_T", [P, 2, T])
    TMP = sb("tmp", [P, 2, T + 3])

    def const(name, rows=P):
        c, w = CONST.at[name]
        return C[0:rows, c:c + w]

    def vec1(name, a=0, b=None, rows=P):
        c, w = VEC1.at[name]
        return V1[0:rows, c + a:c + (w if b is None else b)]

    def vec2(name, a=0, b=None):
        c, w = VEC2.at[name]
        return V2[:, c + a:c + (w if b is None else b)]

    ident, ones = const("ident"), const("ones")

    loads = pr.count("loads")
    A.done(s.dma_start(H[:, 0:8, :].rearrange("p (b h) t -> p b (h t)", b=NTB),
                       io["x"].rearrange("(b p) d -> p b d", p=P)), loads, 16)
    A.done(s.dma_start(C[:, :], io["consts"]), loads, 16)
    A.done(s.dma_start(V1[:, :], io["vec1"]), loads, 16)
    all_loads = loads.token()

    stream = nc.sync
    whole = n_panels // RING
    with stream.Fori(0, whole) as i:
        for k in range(RING):
            stream.wait_ge(pr.used.handle, i * RING + k + 1)
            stream.dma_start(ring[:, k, :], io["stream"][i * RING + k]).then_inc(pr.landed[k].handle, 16)
    for n in range(whole * RING, n_panels):
        stream.wait_ge(pr.used.handle, n + 1)
        stream.dma_start(ring[:, n % RING, :], io["stream"][n]).then_inc(pr.landed[n % RING].handle, 16)

    PE.wait(all_loads)
    pe.sem_inc(pr.used.handle, RING)
    pr.used.const = RING

    def matmuls(bank_ap, pairs, after=(), start=True, stop=True, last=True, bank=None):
        if bank is not None:
            PE.wait(bank.free)
        PE.wait(*after)
        n = len(pairs)
        for k, (lhsT, rhs) in enumerate(pairs):
            ins = pe.matmul(bank_ap, lhsT, rhs, start=start and k == 0, stop=stop and k == n - 1)
        return PE.done(ins) if last else None

    gemm_turn = [0]
    between = []

    def fill(n=1):
        for _ in range(n):
            if between:
                between.pop(0)()

    def gemm_bank():
        gemm_turn[0] += 1
        return B[gemm_turn[0] % 2]

    def gemm(rhs, ktiles, evac, ready=None):
        bank = gemm_bank()
        PE.wait(bank.free)
        k = 0
        while k < ktiles:
            w = pr.take()
            n = min(KT, ktiles - k)
            for j in range(n):
                if ready is not None:
                    PE.wait(ready[k + j])
                ins = pe.matmul(bank[:, :], w[:, j, :], rhs(k + j), start=(k + j == 0), stop=(k + j == ktiles - 1))
            k += n
            tok = pr.release(ins)
        bank.free = evac(bank, tok)
        fill()

    def split_panel():
        n = pr.panel
        z = n % 2
        free = (pr.used, pr.used.const - 1, pr.used.terms)
        t = A(s.activation, WHI[:, z, :], ring[:, n % RING, :], ACT.Copy,
              after=[pr.landed[n % RING].token_after(16), free])
        pr.split = V(v.tensor_tensor, WLO[:, z, :], ring[:, n % RING, :], WHI[:, z, :].bitcast(F32), ALU.subtract,
                     after=[t, free])

    def gemm_split(x, ktiles, evac, ready=None, ahead=True):
        bank = gemm_bank()
        PE.wait(bank.free)
        k = 0
        while k < ktiles:
            if pr.split is None:
                split_panel()
            PE.wait(pr.split)
            z = pr.panel % 2
            n = min(KT, ktiles - k)
            for j in range(n):
                if ready is not None:
                    PE.wait(ready[k + j])
                cols = slice(j * P, j * P + P)
                high, low = x(k + j)
                pe.matmul(bank[:, :], WHI[:, z, cols], high, start=(k + j == 0), stop=False)
                pe.matmul(bank[:, :], WHI[:, z, cols], low, start=False, stop=False)
                ins = pe.matmul(bank[:, :], WLO[:, z, cols], high, start=False, stop=(k + j == ktiles - 1))
            k += n
            tok = pr.release(ins)
            pr.split = None
            if ahead or k < ktiles:
                split_panel()
        bank.free = evac(bank, tok)

    u_split = lambda k: (UHI[:, k, :], ULO[:, k, :])
    h_split = lambda k: (HSPLIT[:, 0, k, :], HSPLIT[:, 1, k, :])

    def split_hidden(at, full, tok):
        high, low = (HSPLIT[:, z, bass.ds(at, 1), :].rearrange("p a t -> p (a t)") for z in range(2))
        t = A(s.activation, high, full, ACT.Copy, after=[tok])
        t = V(v.tensor_tensor, low, full, high.bitcast(F32), ALU.subtract, after=[t])
        pr.hidden = [pr.hidden[-1] if pr.hidden else t, t]

    def hidden_ready(n):
        return [pr.hidden[0]] * (n - 1) + [pr.hidden[1]]

    def gemm_tok(act, width, evac, ready=None):
        bank = gemm_bank()
        PE.wait(bank.free)
        if ready is not None:
            PE.wait(*ready)
        w = pr.take()
        for b in range(NTB):
            for j in range(KT):
                ins = pe.matmul(bank[:, b * P:b * P + width], act(j)[:, b * P:b * P + P], w[:, j, 0:width],
                                start=(j == 0), stop=(j == KT - 1))
        tok = pr.release(ins)
        bank.free = evac(bank, tok)
        fill()

    class Ada:

        def __init__(self):
            self.made = pr.count("modulation_groups_made")
            self.read = pr.count("modulation_groups_read")
            self.groups = 0

        def start(self, c):
            bank = B[7]
            for n in range(N_START):
                w = pr.take()
                for k in range(KT):
                    ins = pe.matmul(bank[:, n:n + 1], w[:, k, :], c[:, k:k + 1], start=(k == 0), stop=(k == KT - 1))
                tok = pr.release(ins)
            bank.free = [V(v.tensor_tensor, MODS[:, 0:N_START], bank[:, 0:N_START], vec1("ada_b", 0, N_START), ALU.add,
                           after=[tok])]

        def gpsimd_program(self):
            landed = [nc.alloc_semaphore(f"modulation_panel_landed_{z}") for z in range(2)]
            step = nc.alloc_semaphore("gpsimd_steps")
            G.wait(A.sem.token())
            for z in range(2):
                g.dma_start(AW[:, z, :], io["ada"][z]).then_inc(landed[z], 16)
            panels = 2 * GROUP
            at, stepped = 0, 0
            for trips, c in ((5, SC[:, 0, :]), (6, SC[:, 1, :])):
                cb = c.rearrange("p (k x) -> p k x", x=1).broadcast_to([P, KT, P])
                with g.Fori(0, trips) as i:
                    count = [0]

                    def own(ins):
                        count[0] += 1
                        ins.then_inc(step, 1)
                        g.wait_ge(step, i * (4 * panels) + (stepped + count[0]))
                    for n in range(panels):
                        slot = n % 2
                        half = n // GROUP
                        if n % GROUP == 0:
                            g.wait_ge(self.read.handle, i * 2 + (at // GROUP + half + READ_START - 1))
                        g.wait_ge(landed[slot], i * (16 * GROUP) + 16 * (at // 2 + n // 2 + 1))
                        own(g.tensor_tensor(AP_[:, :].rearrange("p (k c) -> p k c", k=KT),
                                            AW[:, slot, :].rearrange("p (k c) -> p k c", k=KT), cb, ALU.mult))
                        g.dma_start(AW[:, slot, :], io["ada"][i * panels + (at + n + 2)]).then_inc(landed[slot], 16)
                        own(g.tensor_tensor(AP_[:, 0:512], AP_[:, 0:512], AP_[:, 512:1024], ALU.add))
                        own(g.tensor_tensor(AP_[:, 0:256], AP_[:, 0:256], AP_[:, 256:512], ALU.add))
                        j = n % GROUP
                        own(g.tensor_tensor(AR[:, half, j * P:j * P + P], AP_[:, 0:128], AP_[:, 128:256], ALU.add))
                        if j == GROUP - 1:
                            g.sem_inc(self.made.handle, 1)
                at += panels * trips
                stepped += 4 * panels * trips
            for z in range(2):
                g.wait_ge(landed[z], 16 * (at // 2 + 1))

        def read_group(self):
            bank = B[7]
            half = self.groups % 2
            self.made.const += 1
            PE.wait(bank.free, self.made.token())
            for j in range(GROUP):
                ins = pe.matmul(bank[:, j:j + 1], AR[:, half, j * P:j * P + P], ones[:, 0:1], start=True, stop=True)
            tok = PE.done(ins, self.read)
            self.groups += 1
            at = self.at()
            t = V(v.tensor_tensor, MODS[:, bass.ds(at + N_START, GROUP)], bank[:, 0:GROUP],
                  V1[:, bass.ds(at + (N_START + VEC1.at["ada_b"][0]), GROUP)], ALU.add, after=[tok])
            bank.free = [t]

        def at(self):
            out = (self.made.const - 1) * GROUP
            for loop, k in self.made.terms:
                if k:
                    out = loop.i * (k * GROUP) + out
            return out

    ada = Ada()
    READ_START = 2
    pe.sem_inc(ada.read.handle, READ_START)
    ada.read.const = READ_START

    def plus_one(ap):
        return V(v.tensor_scalar, ap, ap, 1.0, None, ALU.add)

    def stage(n):
        return MODS[:, 24 * n:24 * n + 24]

    def modulate(mod, tiles=range(KT)):
        plus_one(mod[:, 8:16])
        t = V.sem.token()
        return [A(s.activation, U[:, k, :], X[:, k, :], ACT.Identity, bias=mod[:, k:k + 1], scale=mod[:, 8 + k:9 + k],
                  after=[t] + pr.tensor_now()) for k in tiles]

    def mean_step(bank, src, k, tok):
        if k == 0:
            PE.wait(bank.free)
        PE.wait(tok)
        ins = pe.matmul(bank[:, :], const("mean"), src, start=(k == 0), stop=(k == KT - 1), skip_group_check=True)
        return PE.done(ins)

    EPS = {1e-5: const("eps")[:, 0:1], 1e-6: const("eps")[:, 1:2]}

    def inv_sqrt(bank, tok, eps, out, scale=1.0):
        t = A(s.activation, out, bank[:, :], ACT.Ln, bias=EPS[eps], scale=scale, after=[tok, V.sem.token()])
        bank.free = [t]
        t = A(s.activation, out, out, ACT.Exp, scale=-0.5)
        V.wait(t)
        return t

    R = TMP[:, 0, 0:T]

    STAGE = 16

    def split_high(k, tok):
        return A(s.activation, UHI[:, k, :], H[:, STAGE + k, :], ACT.Copy, after=[tok])

    def split_low(k, tok):
        return V(v.tensor_tensor, ULO[:, k, :], H[:, STAGE + k, :], UHI[:, k, :].bitcast(F32), ALU.subtract,
                 after=[tok])

    def layer_norm(mean_tok, gcol, bcol, mod, split=False):
        for k in range(KT):
            t = V(v.tensor_tensor, X[:, k, :], X[:, k, :], B[2][:, :], ALU.subtract, after=[mean_tok])
            t = A(s.activation, M[:, k, :], X[:, k, :], ACT.Square, after=[t] + (pr.tensor_now() if k == 0 else []))
            tok = mean_step(B[3], M[:, k, :], k, t)
        B[2].free = [V.sem.token()]
        if mod is not None:
            plus_one(mod[:, 8:16])
            sh = COL[:, 104:112]
            V(v.tensor_tensor, sh, bcol, mod[:, 8:16], ALU.mult)
            V(v.tensor_tensor, sh, sh, mod[:, 0:8], ALU.add)
        inv_sqrt(B[3], tok, 1e-5, R)
        out, high = [], []
        for k in range(KT):
            t = V(v.scalar_tensor_tensor, X[:, k, :], X[:, k, :], gcol[:, k:k + 1], R, ALU.mult, ALU.mult,
                  after=[A.sem.token()] if k == 0 else ())
            if mod is not None:
                dst = H[:, STAGE + k, :] if split else U[:, k, :]
                t = A(s.activation, dst, X[:, k, :], ACT.Identity, bias=sh[:, k:k + 1], scale=mod[:, 8 + k:9 + k],
                      after=[t])
                if split:
                    high.append(split_high(k, t))
                    if k:
                        out.append(split_low(k - 1, high[k - 1]))
                else:
                    out.append(t)
        if split:
            out.append(split_low(KT - 1, high[-1]))
        for k in range(KT):
            A(s.activation, X[:, k, :], X[:, k, :], ACT.Identity, bias=bcol[:, k:k + 1], after=[V.sem.token()])
        return out

    def square_step(m, tok):
        t = A(s.activation, H[:, 24 + m, :], X[:, m, :], ACT.Square, after=[tok])
        return mean_step(B[3], H[:, 24 + m, :], m, t)

    def rms_norm_all(ms_tok, gain, shift, split=False):
        inv_sqrt(B[3], ms_tok, 1e-6, R)
        out, high = [], []
        for k in range(KT):
            dst = H[:, STAGE + k, :] if split else U[:, k, :]
            t = V(v.scalar_tensor_tensor, dst, X[:, k, :], gain[:, k:k + 1], R, ALU.mult, ALU.mult,
                  after=pr.tensor_now() + ([A.sem.token()] if k == 0 else []))
            if shift is not None:
                t = A(s.activation, dst, dst, ACT.Identity, bias=shift[:, k:k + 1], after=[t])
            if split:
                high.append(split_high(k, t))
                if k:
                    out.append(split_low(k - 1, high[k - 1]))
            else:
                out.append(t)
        if split:
            out.append(split_low(KT - 1, high[-1]))
        return out

    def now():
        return [V.sem.token(), A.sem.token()]

    def softplus_neg(out, x, tmp, after=()):
        t = A(s.activation, tmp, x, ACT.Abs, after=list(after) + [V.sem.token()])
        A(s.activation, tmp, tmp, ACT.Exp, scale=-1.0)
        t = A(s.activation, tmp, tmp, ACT.Ln, bias=1.0)
        V(v.tensor_scalar, out, x, 0.0, None, ALU.min, after=[t])
        return V(v.tensor_tensor, out, tmp, out, ALU.subtract)

    def wide(a, n=4):
        return H[:, a:a + n, :].rearrange("p a t -> p (a t)")

    def attention(items, filler=lambda j: None):
        n = len(items)
        held = [None] * n

        def scores(j):
            it = items[j]
            bank = B[2 + j % 2]
            PE.wait(bank.free)
            PE.wait(*it.get("after", ()))
            w = it["width"]
            ins = pe.matmul(bank[:, 0:w], it["q"], it["k"], start=True, stop=True)
            for m, (lhsT, rhs, c, cw) in enumerate(it["extra"]):
                ins = pe.matmul(bank[:, c:c + cw], lhsT, rhs, start=False, stop=True, skip_group_check=True)
            tok = PE.done(ins)
            c = 8 * (j % 4)
            nm, tot, es = COL[:, c:c + 1], COL[:, c + 1:c + 2], COL[:, c + 2:c + 3]
            probs = PB[:, j % 3, 0:w]
            t = V(v.tensor_reduce, nm, bank[:, 0:w], AXX, ALU.max, negate=True, after=[tok, A.sem.token()])
            if it.get("sink") is not None:
                V(v.tensor_scalar, es, it["sink"], -1.0, None, ALU.mult)
                t = V(v.tensor_tensor, nm, nm, es, ALU.min)
            t = A(s.activation, probs, bank[:, 0:w], ACT.Exp, bias=nm, accum_out=tot,
                  after=[t] + ([held[j - 3]] if j >= 3 else pr.tensor_now()))
            bank.free = [t]
            if it.get("sink") is not None:
                t = A(s.activation, es, it["sink"], ACT.Exp, bias=nm)
            it["exp"] = t

        def probabilities(j):
            it = items[j]
            c = 8 * (j % 4)
            tot, es = COL[:, c + 1:c + 2], COL[:, c + 2:c + 3]
            probs = PB[:, j % 3, 0:it["width"]]
            t = it["exp"]
            if it.get("sink") is not None:
                V(v.tensor_tensor, tot, tot, es, ALU.add, after=[t])
            V(v.reciprocal, tot, tot, after=[t])
            if it.get("gate") is not None:
                V(v.tensor_tensor, tot, tot, it["gate"], ALU.mult)
            if it.get("valid") is not None:
                t = V(v.scalar_tensor_tensor, probs, probs, tot, it["valid"], ALU.mult, ALU.mult)
            else:
                t = V(v.tensor_scalar, probs, probs, tot, None, ALU.mult)
            it["ready"] = t

        def turn(j):
            it = items[j]
            bank = B[4 + j % 2]
            w = it["width"]
            PE.wait(bank.free, it["ready"])
            chunks = [(c, min(P, w - c)) for c in range(0, w, P)]
            for c, cw in chunks:
                ins = pe.transpose(bank[0:cw, c:c + P], PB[:, j % 3, c:c + cw], ident)
            tok = PE.done(ins)
            held[j] = tok
            rows = min(P, w)
            cols = P * len(chunks)
            after = [tok] + ([items[j - 2]["used"]] if j >= 2 else pr.tensor_now())
            if j % 2:
                t = V(v.tensor_copy, PT[0:rows, j % 2, 0:cols], bank[0:rows, 0:cols], after=after)
            else:
                t = A(s.activation, PT[0:rows, j % 2, 0:cols], bank[0:rows, 0:cols], ACT.Copy, after=after)
            bank.free = [t]
            it["turned"] = t

        def product(j):
            it = items[j]
            if it["start"]:
                PE.wait(it["bank"].free)
            PE.wait(it["turned"])
            m = len(it["v"])
            for c, lhsT in enumerate(it["v"]):
                rows = min(P, it["width"])
                ins = pe.matmul(it["out"], lhsT, PT[0:rows, j % 2, c * P:c * P + P],
                                start=it["start"] and c == 0, stop=it["stop"] and c == m - 1, skip_group_check=True)
            it["used"] = PE.done(ins)
            if it.get("evac"):
                it["bank"].free = it["evac"](it["used"])

        for j in range(n + 3):
            if j < n:
                scores(j)
            if 1 <= j <= n:
                probabilities(j - 1)
            filler(j)
            if 2 <= j <= n + 1:
                turn(j - 2)
            if j >= 3:
                product(j - 3)

    for k in range(KT):
        bank = B[2 + k % 2]
        PE.wait(bank.free, all_loads)
        for b in range(NTB):
            ins = pe.transpose(bank[:, b * P:b * P + P],
                               H[:, 2 * b + k // 4, (k % 4) * P:(k % 4) * P + P], ident)
        tok = PE.done(ins)
        bank.free = [A(s.activation, X[:, k, :], bank[:, :], ACT.Copy, after=[tok, all_loads])]
    V.wait(all_loads)
    A.wait(all_loads)
    A(s.activation, SC[:, 0, :], vec1("c"), ACT.Silu)
    A(s.activation, SC[:, 1, :], vec1("c2"), ACT.Silu)
    PE.wait(A.sem.token())
    ada.gpsimd_program()

    ada.start(SC[:, 0, :])
    ready = modulate(stage(0))
    u = lambda k: U[:, k, :]
    XR, YR, Q, K_, GG, VT = 0, 4, 8, 10, 12, 16
    RT, IT, AT_ = 20, 24, 28

    def conv4(src, tile, wcol, bias):
        V(v.tensor_scalar, tile, src[:, 0:T], wcol(0), bias, ALU.mult, ALU.add if bias is not None else ALU.bypass)
        for j in range(1, 4):
            t = V(v.scalar_tensor_tensor, tile, src[:, j:j + T], wcol(j), tile, ALU.mult, ALU.add)
        return t

    V(v.memset, TMP[:, :, 0:3], 0.0)
    LS = COL[:, 64:68]
    softplus_neg(LS, vec1("rg_lam"), COL[:, 68:72])
    V(v.tensor_scalar, LS, LS, -8.0, None, ALU.mult)
    for m in range(4):
        def evac(bank, tok, m=m):
            src = TMP[:, m % 2, :]
            t = A(s.activation, src[:, 3:3 + T], bank[:, :], ACT.Copy, after=[tok, V.sem.token()])
            V.wait(t)
            conv4(src, H[:, XR + m, :], lambda j: vec1("conv_w", 4 * j + m, 4 * j + m + 1), vec1("conv_b", m, m + 1))
            return [t]
        gemm(u, KT, evac, ready)
    w = pr.take()
    PE.wait(V.sem.token())
    for half in range(2):
        for m in range(4):
            bank = B[2 + m]
            PE.wait(bank.free)
            ins = pe.matmul(bank[:, :], w[:, 4 * half + m, :], H[:, XR + m, :], start=True, stop=True)
            tok = pr.release(ins) if (half, m) == (1, 3) else PE.done(ins)
            bank.free = [A(s.activation, H[:, (RT, IT)[half] + m, :], bank[:, :], ACT.Sigmoid,
                           bias=vec1(("rg_ba", "rg_bx")[half], m, m + 1), after=[tok])]
    r, i_, a, xr, yr = wide(RT), wide(IT), wide(AT_), wide(XR), wide(YR)
    th = M[:, 4:8, :].rearrange("p a t -> p (a t)")
    rgo = M[:, 0:4, :].rearrange("p a t -> p (a t)")

    def rg_1():
        V(v.tensor_tensor, i_, i_, xr, ALU.mult, after=[A.sem.token()])

    def rg_2():
        for m in range(4):
            A(s.activation, H[:, AT_ + m, :], H[:, RT + m, :], ACT.Exp, scale=LS[:, m:m + 1], after=[V.sem.token()])

    def rg_3():
        for m in range(4):
            A(s.activation, M[:, 4 + m, :], H[:, RT + m, :], ACT.Tanh, scale=LS[:, m:m + 1])

    def rg_4():
        V(v.tensor_scalar, r, th, -1.0, 1.0, ALU.mult, ALU.add, after=[A.sem.token()])
        V(v.reciprocal, r, r)

    def rg_5():
        V(v.tensor_tensor, th, th, r, ALU.mult)

    def rg_6():
        A(s.activation, th, th, ACT.Sqrt, scale=-2.0, after=[V.sem.token()])

    def rg_7():
        V(v.tensor_tensor, i_, i_, th, ALU.mult, after=[A.sem.token()])

    def rg_8():
        for m in range(4):
            V(v.tensor_tensor_scan, M[:, m, :], H[:, AT_ + m, :], H[:, IT + m, :], 0.0, ALU.mult, ALU.add)

    def rg_9():
        A(s.activation, th, yr, ACT.Square, after=[V.sem.token()])

    def rg_10():
        V(v.tensor_scalar, th, th, 0.044715, 1.0, ALU.mult, ALU.add, after=[A.sem.token()])
        V(v.tensor_tensor, th, th, yr, ALU.mult)

    def rg_11():
        A(s.activation, th, th, ACT.Sigmoid, scale=float(2.0 * np.sqrt(2.0 / np.pi)), after=[V.sem.token()])

    def rg_12():
        V(v.tensor_tensor, th, th, yr, ALU.mult, after=[A.sem.token()])
        V(v.tensor_tensor, rgo, rgo, th, ALU.mult)

    ZL = TMP[0:16, 0, 0:T]
    EB, QD, KD, KE, T1, KET = 20, 22, 24, 26, 28, 30

    def gla_1(m):
        tok = matmuls(B[2 + m][:, :], [(vec1("gla_up", m * P, m * P + P, rows=16), ZL)], after=now(), bank=B[2 + m])
        x = H[:, QD + m, :]
        t = A(s.activation, x, B[2 + m][:, :], ACT.Identity, bias=vec1("gla_b", m, m + 1), after=[tok, V.sem.token()])
        B[2 + m].free = [t]
        softplus_neg(H[:, KD + m, :], x, H[:, KE + m, :])

    def gla_2(m):
        la, bc, eb, t1 = (H[:, z + m, :] for z in (KD, KE, EB, T1))
        V(v.tensor_scalar, la, la, -1.0 / 16.0, None, ALU.mult)
        V(v.tensor_tensor_scan, bc, const("chunk_reset"), la, 0.0, ALU.mult, ALU.add)
        A(s.activation, eb, bc, ACT.Exp, after=[V.sem.token()])
        A(s.activation, t1, bc, ACT.Exp, scale=-1.0)

    def gla_3(m):
        qd, kd, bc, eb, t1 = (H[:, z + m, :] for z in (QD, KD, KE, EB, T1))
        V(v.tensor_tensor, qd, H[:, Q + m, :], eb, ALU.mult, after=[A.sem.token()])
        V(v.tensor_tensor, kd, H[:, K_ + m, :], t1, ALU.mult)
        bc3 = bc.rearrange("p (c t) -> p c t", t=GLA_CH)
        t3 = t1.rearrange("p (c t) -> p c t", t=GLA_CH)
        V(v.tensor_tensor, t3, bc3[:, :, GLA_CH - 1:GLA_CH].broadcast_to([P, 8, GLA_CH]), bc3, ALU.subtract)
        t = A(s.activation, t1, t1, ACT.Exp, after=[V.sem.token()])
        V(v.tensor_tensor, bc, H[:, K_ + m, :], t1, ALU.mult, after=[t])

    ket = H[:, KET:KET + 2, :].rearrange("p (b x) t -> p b (x t)", b=1)[:, 0, :].rearrange("p (b k) -> p b k", b=NTB)

    def gla_4(m):
        bank = B[4 + m]
        PE.wait(bank.free, *now())
        for b in range(NTB):
            ins = pe.transpose(bank[:, b * P:b * P + P], H[:, KE + m, b * P:b * P + P], ident)
        tok = PE.done(ins)
        bank.free = [A(s.activation, ket[:, :, m * P:m * P + P], bank[:, :].rearrange("p (b c) -> p b c", b=NTB),
                       ACT.Copy, after=[tok])]

    steps = [rg_1, rg_2, rg_3, rg_4, rg_5, rg_6, rg_7, lambda: (rg_8(), ada.read_group()),
             lambda: gla_1(0), lambda: gla_1(1), lambda: (gla_2(0), gla_2(1)), lambda: gla_3(0), lambda: gla_3(1),
             rg_9, rg_10, rg_11, lambda: (rg_12(), ada.read_group())]
    between += steps
    gemm(u, KT, lambda bank, tok: [A(s.activation, ZL, bank[0:16, :], ACT.Copy, after=[tok, V.sem.token()])])
    for m in range(2):
        gemm(u, KT, lambda bank, tok, m=m: [A(s.activation, H[:, Q + m, :], bank[:, :], ACT.Copy, scale=0.125, after=[tok])])
    for m in range(2):
        gemm(u, KT, lambda bank, tok, m=m: [A(s.activation, H[:, K_ + m, :], bank[:, :], ACT.Copy, after=[tok])])
    vt = H[:, VT:VT + 4, :]
    for m in range(4):
        gemm_tok(u, P, lambda bank, tok, m=m: [A(s.activation, vt[:, :, m * P:m * P + P],
                 bank[:, :].rearrange("p (b c) -> p b c", b=NTB), ACT.Copy, after=[tok])])
    for m in range(4):
        gemm(u, KT, lambda bank, tok, m=m: [A(s.activation, H[:, YR + m, :], bank[:, :], ACT.Copy, after=[tok])])
    for m in range(4):
        gemm(u, KT, lambda bank, tok, m=m: [A(s.activation, H[:, GG + m, :], bank[:, :], ACT.Silu, after=[tok])])
    fill(len(between))
    for m in range(2):
        gla_4(m)
    att = [H[:, XR + z, :] for z in range(2)]
    masked = []
    zero = V(v.memset, H[:, XR:XR + 2, :], 0.0, after=now() + pr.tensor_now())
    PE.wait(B[4].free, B[5].free, *now())
    chunk = lambda c: slice(c * 64, c * 64 + 64)
    for h in range(4):
        hp, ho = h // 2, 64 * (h % 2)
        for c in range(8):
            o, col = 64 * (c % 2), (c // 2) * P + hp * 64
            ins = pe.matmul(B[4 + h % 2][o:o + 64, col:col + 64], H[ho:ho + 64, KD + hp, chunk(c)],
                            H[ho:ho + 64, QD + hp, chunk(c)], start=True, stop=True)
    t_att = PE.done(ins)
    PE.wait(B[2].free, B[3].free, B[6].free, B[7].free)
    kv_bank = lambda c: B[(2, 3, 6, 7)[2 * (c % 2) + c // 4]]
    kv_col = lambda c, hp: ((c // 2) % 2) * 256 + hp * P
    for c in range(8):
        o, b = 64 * (c % 2), c // 2
        for h in range(4):
            hp, ho = h // 2, 64 * (h % 2)
            col = kv_col(c, hp)
            ins = pe.matmul(kv_bank(c)[ho:ho + 64, col:col + P], ket[o:o + 64, b, h * 64:h * 64 + 64],
                            vt[o:o + 64, b, h * P:h * P + P], start=True, stop=True)
    t_kv = PE.done(ins)
    mask = const("gla_mask").bitcast(I32)
    mask8 = mask.rearrange("p (a t) -> p a t", a=1).broadcast_to([P, 8, 64])
    for z in range(2):
        t = V(v.copy_predicated, att[z].rearrange("p (n t) -> p n t", n=8), mask8,
              B[4 + z][:, :].rearrange("p (n t) -> p n t", n=8), after=[t_att])
    B[4].free = B[5].free = [t]
    ST = H[:, AT_:AT_ + 4, :].rearrange("p a (c x) -> p (a c) x", c=2).rearrange("p c (m v) -> p c m v", m=2)
    V(v.memset, ST[:, 0, :, :], 0.0, after=[t_kv])
    for c in range(7):
        for hp in range(2):
            col = kv_col(c, hp)
            t_st = V(v.scalar_tensor_tensor, ST[:, c + 1, hp, :], ST[:, c, hp, :],
                     H[:, EB + hp, c * 64 + 63:c * 64 + 64], kv_bank(c)[:, col:col + P], ALU.mult, ALU.add)
    for z in (2, 3, 6, 7):
        B[z].free = [t_st]
    OG = [Q, Q + 1, K_, K_ + 1]
    o_tok = []
    for hp in range(2):
        banks = (B[0], B[1], B[2], B[3]) if hp == 0 else (B[4], B[5], B[6], B[7])
        PE.wait(*[z.free for z in banks], t_st)
        for z in range(2):
            o = 64 * z
            for e in range(2):
                h = 2 * hp + e
                for b in range(NTB):
                    pe.matmul(banks[z][:, e * 256 + b * 64:e * 256 + b * 64 + 64], vt[o:o + 64, b, h * P:h * P + P],
                              att[e][o:o + 64, b * P + hp * 64:b * P + hp * 64 + 64], start=True, stop=True)
        for e in range(2):
            ho = 64 * e
            for c in range(8):
                ins = pe.matmul(banks[2 + e][:, chunk(c)], ST[ho:ho + 64, c, hp, :], H[ho:ho + 64, QD + hp, chunk(c)],
                                start=True, stop=True)
        tok = PE.done(ins)
        for e in range(2):
            dst = H[:, OG[2 * hp + e], :].rearrange("p (b o t) -> p b o t", o=2, t=64)
            for o in range(2):
                A(s.activation, dst[:, :, o, :],
                  banks[o][:, e * 256:e * 256 + 256].rearrange("p (b t) -> p b t", b=NTB), ACT.Copy, after=[tok])
            t = V(v.tensor_tensor, H[:, OG[2 * hp + e], :], H[:, OG[2 * hp + e], :], banks[2 + e][:, :], ALU.add,
                  after=[A.sem.token()])
        for z in banks:
            z.free = [t]
    oo, sq, rs = wide(Q), wide(RT), wide(IT)
    A(s.activation, sq, oo, ACT.Square, after=[V.sem.token()] + pr.tensor_now())

    def head_norm(src_tile, o_all, sq0, rs0, gain, out):
        after = [A.sem.token()]
        toks = [matmuls(B[2 + h][:, :], [(ones, H[:, sq0 + h, :])], after=after, bank=B[2 + h]) for h in range(4)]
        for h in range(4):
            inv_sqrt(B[2 + h], toks[h], 1e-6, H[:, rs0 + h, :], scale=1.0 / P)
            V(v.scalar_tensor_tensor, src_tile(h), src_tile(h), gain(h), H[:, rs0 + h, :], ALU.mult, ALU.mult)
            out(h)

    mix_tok = [A.sem.token()] * KT

    def gla_out(h):
        mix_tok[4 + h] = V(v.tensor_tensor, M[:, 4 + h, :], H[:, OG[h], :], H[:, GG + h, :], ALU.mult)

    mix_tok[0:4] = [V.sem.token()] * 4
    head_norm(lambda h: H[:, OG[h], :], oo, RT, IT, lambda h: vec1("gla_g", h, h + 1), gla_out)

    def add_residual(mod, bias=None):
        def evac_of(m):
            def evac(bank, tok):
                tmp = TMP[:, m % 2, 0:T]
                gcol = mod[:, 16 + m:17 + m]
                if bias is None:
                    t = A(s.activation, tmp, bank[:, :], ACT.Copy, scale=gcol, after=[tok, V.sem.token()])
                else:
                    t = A(s.activation, tmp, bank[:, :], ACT.Identity, scale=gcol, bias=bias[:, m:m + 1],
                          after=[tok, V.sem.token()])
                V(v.scalar_tensor_tensor, X[:, m, :], X[:, m, :], ALPHA, tmp, ALU.mult, ALU.add, after=[t])
                return [t]
            return evac
        return evac_of

    def output_gemm(tile, evac, step=None):
        prev = None
        for m in range(KT):
            tile(m, evac(m))
            if prev is not None and step:
                step(m - 1, prev)
            prev = V.sem.token()
        return step(KT - 1, prev) if step else prev

    def mix_tile(ready=None):
        return lambda m, evac: gemm(mix, KT, evac, ready)

    def down_tile(n, last):
        ready = hidden_ready(n)
        return lambda m, evac: gemm_split(h_split, n, evac, ready if m == 0 else None, ahead=m < KT - 1 or not last)

    def add_gated(gcol):
        return lambda m: (lambda bank, tok: [V(v.scalar_tensor_tensor, X[:, m, :], bank[:, :], gcol[:, m:m + 1],
                                               X[:, m, :], ALU.mult, ALU.add, after=[tok])])

    def project(mod, ready=None):
        plus_one(mod[:, 16:24])
        return output_gemm(mix_tile(ready), add_residual(mod), lambda m, tok: mean_step(B[2], X[:, m, :], m, tok))

    mix = lambda k: M[:, k, :]

    def mlp(l, mod, ready, early, late):
        b1 = VEC1.at["mlp_b1"][0] + 32 * l

        def up(half, i, j, ready=None):
            def evac(bank, tok):
                h = TMP[:, j % 2, 0:T]
                t_relu = A(s.activation, h, bank[:, :], ACT.Relu, bias=V1[:, bass.ds(i * BODY + (b1 + HALF * half + j), 1)],
                           after=[tok, V.sem.token()])
                split_hidden(i * BODY + j, h, V(v.tensor_tensor, h, h, h, ALU.mult, after=[t_relu]))
                return [t_relu]
            gemm_split(u_split, KT, evac, ready)

        gb = COL[:, 72:80]
        for half in range(2):
            for j in range(BODY):
                up(half, 0, j, ready if half == 0 else None)
                if j in early[half]:
                    ada.read_group()
            with pr.loop(f"mlp_up{l}_{half}", HALF // BODY - 1, fence=False) as i:
                for j in range(BODY):
                    up(half, i + 1, j)
            if half == 0:
                plus_one(mod[:, 16:24])
                V(v.tensor_tensor, gb, mod[:, 16:24], vec1("mlp_b2", 8 * l, 8 * l + 8), ALU.mult)

            def step(m, tok, half=half):
                if m in late[half]:
                    ada.read_group()
                return mean_step(B[2], X[:, m, :], m, tok) if half else None
            tok = output_gemm(down_tile(HALF, half == 1), add_gated(mod[:, 16:24]) if half else add_residual(mod, gb),
                              step)
        return tok

    ada.read_group()
    tok = project(stage(0), mix_tok)
    ready = layer_norm(tok, vec1("ln_g", 0, 8), vec1("ln_b", 0, 8), stage(1), split=True)
    tok = mlp(0, stage(1), ready, ((1,), (1,)), ((2, 5), (2, 5)))
    ready = layer_norm(tok, vec1("ln_g", 8, 16), vec1("ln_b", 8, 16), stage(2))

    NF = H[0:FOX_H, 31, :]

    def evac_f(bank, tok):
        z, tmp = TMP[0:FOX_H, 0, 0:T], TMP[0:FOX_H, 1, 0:T]
        t = A(s.activation, z, bank[0:FOX_H, :], ACT.Identity, bias=vec1("fox_bf", rows=FOX_H), after=[tok, V.sem.token()])
        softplus_neg(H[0:FOX_H, 30, :], z, tmp)
        V(v.tensor_tensor_scan, NF, const("ones", FOX_H)[:, 0:1].broadcast_to([FOX_H, T]), H[0:FOX_H, 30, :], 0.0,
          ALU.mult, ALU.add)
        return [t]
    gemm(u, KT, evac_f, ready)
    PE.wait(*now())
    QG = COL[:, 80:81]
    V(v.tensor_scalar, QG, vec1("fox_qg"), 0.125, None, ALU.mult)

    def fox_tiles(e):
        return tuple(H[:, 4 * e + z, :] for z in range(4))

    def fox_projections(e):
        q, k_, gt, vt_ = fox_tiles(e)
        vtok = vt_.rearrange("p (b c) -> p b c", b=NTB)
        sq, rs = H[:, 8, :], H[:, 9, :]

        def plain(dst, func, view=lambda z: z):
            return lambda bank, tok: [A(s.activation, dst, view(bank[:, :]), func,
                                        after=[tok, V.sem.token()] + pr.tensor_now())]

        def square(src):
            return lambda: A(s.activation, sq, src, ACT.Square, after=[V.sem.token()] + pr.tensor_now())

        def norm(gain, dst):
            def step():
                tok = matmuls(B[1][:, :], [(const("mean64"), sq)], after=[A.sem.token()], bank=B[1])
                inv_sqrt(B[1], tok, 1e-6, rs)
                V(v.scalar_tensor_tensor, dst, dst, gain, rs, ALU.mult, ALU.mult)
            return step
        return {0: lambda: gemm(u, KT, plain(q, ACT.Copy)), 1: square(q), 2: norm(QG, q),
                3: lambda: gemm(u, KT, plain(k_, ACT.Copy)), 4: square(k_), 5: norm(vec1("fox_kg"), k_),
                7: lambda: gemm_tok(u, P, plain(vtok, ACT.Copy, lambda z: z.rearrange("p (b c) -> p b c", b=NTB))),
                9: lambda: gemm(u, KT, plain(gt, ACT.Sigmoid))}

    def fox_attention(pair, e, steps):
        q, k_, gt, vt_ = fox_tiles(e)
        vtok = vt_.rearrange("p (b c) -> p b c", b=NTB)
        sel = H[0:FOX_H, 10 + e, 0:2 * P]
        c0 = CONST.at["ident"][0]
        V(v.tensor_copy, sel.rearrange("p (a c) -> p a c", a=2),
          C[0:FOX_H, bass.ds(pair * 2 + c0, 2)].rearrange("p (a x) -> p a x", x=1).broadcast_to([FOX_H, 2, P]),
          after=pr.tensor_now())
        items = []
        for hd in range(2):
            hr = slice(64 * hd, 64 * hd + 64)
            for b in range(NTB):
                w_ = (b + 1) * P
                items.append(dict(
                    q=q[hr, b * P:w_], k=k_[hr, 0:w_], width=w_,
                    extra=[(sel[:, hd * P:hd * P + P], NF[:, 0:w_], 0, w_), (ident, const("causal"), b * P, P)],
                    v=[vtok[:, c, hr] for c in range(b + 1)], out=B[6][hr, b * P:w_], bank=B[6],
                    start=True, stop=True))
        items[0]["after"] = now()

        def evac(tok):
            o = M[:, bass.ds(pair, 1), :].rearrange("p a t -> p (a t)")
            return [V(v.tensor_tensor, o, B[6][:, :], gt, ALU.mult, after=[tok, A.sem.token()])]
        items[-1]["evac"] = evac

        def filler(j):
            if j == 4:
                ada.read_group()
            if j in steps:
                steps[j]()
        attention(items, filler)

    for f in fox_projections(0).values():
        f()
    with pr.loop("fox", KT // 2 - 1) as i:
        fox_attention(i * 2, 0, fox_projections(1))
        fox_attention(i * 2 + 1, 1, fox_projections(0))
    for e in range(2):
        fox_attention(KT - 2 + e, e, fox_projections(1) if e == 0 else {})
    tok = project(stage(2), [now()] * KT)
    ready = layer_norm(tok, vec1("ln_g", 16, 24), vec1("ln_b", 16, 24), stage(3), split=True)
    tok = mlp(1, stage(3), ready, ((1,), (1,)), ((2, 5), (2,)))
    layer_norm(tok, vec1("ln_g", 24, 32), vec1("ln_b", 24, 32), None)

    mod = MH
    V.wait(A.sem.token())
    for m in range(KT):
        square_step(m, V.sem.token())
    with pr.loop("hybrid", L2) as l:
        A.wait(V.sem.token(), *pr.tensor_now())
        tok = A.done(s.dma_start(V2[:, :], io["vec2"][l]), loads, 16)
        V(v.tensor_copy, MH[:, :], MODS[:, bass.ds(l * 48 + (N_ADA - 96), 48)], after=[tok, A.sem.token()])
        A.wait(tok)
        GM, GF = COL[:, 96:104], COL[:, 104:112]
        plus_one(mod[:, 8:16])
        plus_one(mod[:, 32:40])
        V(v.tensor_tensor, GM, mod[:, 8:16], vec2("norm_mix"), ALU.mult)
        V(v.tensor_tensor, GF, mod[:, 32:40], vec2("norm_ffn"), ALU.mult)
        ready = rms_norm_all(pr.tensor_now(), GM, mod[:, 0:8])
        AK, KC, VC, KSW, XK, HID = 0, 1, 2, 3, 4, 6
        AQ, BQ, BQR, AV, VSW, SM, CMP, KS2, KW2, AK2 = 16, 18, 20, 22, 23, 24, 25, 26, 27, 28

        def rope(bank, tok, dst, scale, raw=None):
            x = raw if raw is not None else TMP[:, 0, 0:T]
            t = A(s.activation, x, bank[:, :], ACT.Copy, scale=scale, after=[tok, V.sem.token()] + pr.tensor_now())
            tok2 = matmuls(B[2][:, :], [(const("rot"), x)], after=[t], bank=B[2])
            V(v.tensor_tensor, TMP[:, 1, 0:T], B[2][:, :], const("sin"), ALU.mult, after=[tok2])
            B[2].free = [V.sem.token()]
            V(v.tensor_tensor, dst, x, const("cos"), ALU.mult)
            V(v.tensor_tensor, dst, dst, TMP[:, 1, 0:T], ALU.add)
            return [t]

        for m in range(2):
            gemm(u, KT, lambda bank, tok, m=m: rope(bank, tok, H[:, AQ + m, :], 0.125), ready)
        gemm(u, KT, lambda bank, tok: rope(bank, tok, H[:, AK, :], 1.0))
        ak_tok = V.sem.token()
        for m in range(2):
            gemm(u, KT, lambda bank, tok, m=m: rope(bank, tok, H[:, BQR + m, :], 0.125, raw=H[:, BQ + m, :]))
        for dst in (KC, VC):
            def evac(bank, tok, dst=dst):
                A(s.activation, H[0:64, dst, :], bank[0:64, :], ACT.Copy, after=[tok])
                V(v.memset, H[64:P, dst, T - 1:T], 0.0, after=[A.sem.token()])
                t = A(s.activation, H[64:P, dst, 0:T - 1], bank[64:P, 1:T], ACT.Copy, after=[V.sem.token()])
                return [t]
            gemm(u, KT, evac)
        gemm(u, KT, lambda bank, tok: rope(bank, tok, H[:, KSW, :], 1.0))
        ks_tok = V.sem.token()
        r4 = lambda ap: ap.rearrange("p (b c) -> p b c", b=NTB)
        av, vsw, sm = r4(H[:, AV, :]), r4(H[:, VSW, :]), r4(H[:, SM, :])
        for dst in (av, vsw):
            gemm_tok(u, P, lambda bank, tok, dst=dst: [A(s.activation, dst, r4(bank[:, :]), ACT.Copy, after=[tok])])
        gemm_tok(u, 20, lambda bank, tok: [A(s.activation, sm[:, :, 0:20], r4(bank[:, :])[:, :, 0:20], ACT.Copy,
                                             after=[tok])])
        V(v.memset, TMP[:, :, 0:3], 0.0, after=[A.sem.token()])

        def conv_tile(m):
            def evac(bank, tok):
                src = TMP[:, m % 2, :]
                t = A(s.activation, src[:, 3:3 + T], bank[:, :], ACT.Copy, after=[tok, V.sem.token()])
                V.wait(t)
                conv4(src, H[:, m, :], lambda j: vec2("conv_w", 12 * j + m, 12 * j + m + 1), None)
                A(s.activation, H[:, m, :], H[:, m, :], ACT.Silu, after=[V.sem.token()])
                return [t]
            return lambda: gemm(u, KT, evac)

        def z_tile(m):
            return lambda: gemm(u, KT, lambda bank, tok: [A(s.activation, H[:, 12 + m, :], bank[:, :], ACT.Silu,
                                                            after=[tok])])

        SMC = COL[:, 128:256]
        beta, gcol, gc, gl, bege, gle = (SMC[:, z * 16:z * 16 + 16] for z in range(6))
        ngc = gl
        c4 = lambda ap: ap.rearrange("p (b h) -> p b h", b=NTB)

        def gate_columns():
            A(s.activation, sm[:, :, 32:44], sm[:, :, 0:12], ACT.Sigmoid)
            A(s.activation, c4(beta), sm[:, :, 16:20], ACT.Sigmoid, after=[V.sem.token()])
            x = c4(gcol)
            for b in range(NTB):
                V(v.tensor_tensor, x[:, b, :], sm[:, b, 12:16], vec2("dt_bias"), ALU.add, after=[A.sem.token()])
            V(v.tensor_scalar, gcol, gcol, -1.0, None, ALU.mult)
            softplus_neg(gc, gcol, gl)
            t = A(s.activation, COL[:, 84:88], vec2("A_log"), ACT.Exp, after=[V.sem.token()])
            V.wait(t)
            for b in range(NTB):
                g_tok[0] = V(v.scalar_tensor_tensor, x[:, b, :], c4(gc)[:, b, :], -1.0, COL[:, 84:88], ALU.mult, ALU.mult)
        g_tok = [0]

        def decay_columns():
            PE.wait(B[2].free, B[3].free, g_tok[0])
            pe.matmul(B[2][:, 0:16], const("tri"), gcol, start=True, stop=True)
            ins = pe.matmul(B[3][:, 0:16], const("one64"), gcol, start=True, stop=True)
            tok = PE.done(ins)
            V(v.tensor_copy, gc, B[2][:, 0:16], after=[tok])
            V(v.tensor_copy, gl, B[3][:, 0:16])
            B[2].free = B[3].free = [V.sem.token()]
            V(v.tensor_tensor, gle, gl, gc, ALU.subtract)
            A(s.activation, gle, gle, ACT.Exp, after=[V.sem.token()])
            t = A(s.activation, bege, gc, ACT.Exp)
            V(v.tensor_tensor, bege, bege, beta, ALU.mult, after=[t])
            V(v.tensor_scalar, gl, gc, -1.0, None, ALU.mult)

        xw = lambda ap: ap.rearrange("p (j n) -> p j n", j=16)

        def windows(which, src, pos):
            x = H[:, XK + which, 0:16 * N_CMP]
            base = H[:, src, :]
            for jp in range(16):
                V(v.tensor_scalar, x[:, jp * N_CMP:(jp + 1) * N_CMP], base[:, 2 * jp:2 * jp + 16 * (N_CMP - 1) + 1:16],
                  vec2(pos, jp, jp + 1), None, ALU.add, after=[A.sem.token()])
            window_tok[which] = V.sem.token()
        window_tok = [0, 0]

        def swap_halves(src, low, high, banks, tok):
            b0, b1 = banks
            PE.wait(b0.free, b1.free, tok)
            pe.matmul(b0[64:P, :], ident[:, 0:64], H[:, src, :], start=True, stop=True)
            ins = pe.matmul(b1[0:64, :], ident[:, 64:P], H[:, src, :], start=True, stop=True)
            tok = PE.done(ins)
            A(s.activation, H[64:P, low, :], b0[64:P, :], ACT.Copy, after=[tok])
            A(s.activation, H[0:64, low, :], H[0:64, src, :], ACT.Copy)
            A(s.activation, H[0:64, high, :], b1[0:64, :], ACT.Copy)
            t = A(s.activation, H[64:P, high, :], H[64:P, src, :], ACT.Copy)
            b0.free = b1.free = [t]

        between.extend([lambda: windows(0, KC, "pe_k"), lambda: windows(1, VC, "pe_v"), gate_columns,
                        lambda: swap_halves(KSW, KS2, KW2, (B[3], B[4]), ks_tok),
                        decay_columns,
                        lambda: swap_halves(AK, AK2, AK2 + 1, (B[5], B[6]), ak_tok)])
        for m in (8, 9, 10, 11):
            conv_tile(m)()
        for m in range(2):
            z_tile(m)()
        hid = H[:, HID, 0:4 * 32].rearrange("p (w m n) -> p w m n", w=2, m=2)
        for which in range(2):
            x = xw(H[:, XK + which, 0:16 * N_CMP])
            for m in range(2):
                bank = B[2 + m]
                PE.wait(bank.free, window_tok[which])
                for kg in range(2):
                    w = pr.take()
                    for j in range(KT):
                        ins = pe.matmul(bank[:, 0:N_CMP], w[:, j, :], x[:, kg * KT + j, :], start=(kg + j == 0),
                                        stop=(kg == 1 and j == KT - 1))
                    tok = pr.release(ins)
                hid_tok = A(s.activation, hid[:, which, m, 0:N_CMP], bank[:, 0:N_CMP], ACT.Silu, after=[tok])
                bank.free = [hid_tok]
        z_tile(2)()
        w = pr.take()
        PE.wait(B[2].free, B[3].free, B[4].free, hid_tok)
        for m in range(2):
            pe.matmul(B[2][0:64, 0:N_CMP], w[:, m, 0:64], hid[:, 0, m, 0:N_CMP], start=(m == 0), stop=(m == 1))
        for m in range(2):
            pe.matmul(B[4][64:P, 0:N_CMP], w[:, m, 0:64], hid[:, 0, m, 0:N_CMP], start=(m == 0), stop=(m == 1))
        for m in range(2):
            ins = pe.matmul(B[3][0:N_CMP, 0:64], hid[:, 1, m, 0:N_CMP], w[:, m, 64:128], start=(m == 0), stop=(m == 1))
        tok = pr.release(ins)
        kcmp, vcmp = H[:, CMP, 0:N_CMP], H[0:N_CMP, CMP, 64:128]
        A(s.activation, H[0:64, CMP, 0:N_CMP], B[2][0:64, 0:N_CMP], ACT.Copy, after=[tok])
        A(s.activation, H[64:P, CMP, 0:N_CMP], B[4][64:P, 0:N_CMP], ACT.Copy)
        t = A(s.activation, vcmp, B[3][0:N_CMP, 0:64], ACT.Copy)
        B[2].free = B[3].free = B[4].free = [t]
        z_tile(3)()

        items = []

        def to_mix(tile, bank):
            return lambda tok: [A(s.activation, M[:, tile, :], bank[:, :], ACT.Copy, after=[tok])]

        for h in range(4):
            hr = slice(64 * (h % 2), 64 * (h % 2) + 64)
            for b in range(NTB):
                lo = max(0, b - 1)
                w_ = (b + 1 - lo) * P
                extra = [(ident, const("causal"), w_ - P, P)]
                if b:
                    extra.append((ident, const("band"), 0, P))
                items.append(dict(q=H[hr, AQ + h // 2, b * P:b * P + P], k=H[hr, AK2 + h // 2, lo * P:(b + 1) * P],
                                  extra=extra, width=w_, sink=vec2("sinks", h, h + 1),
                                  v=[av[:, c, 64 * (h // 2):64 * (h // 2) + 64] for c in range(lo, b + 1)],
                                  out=B[6 + h // 2][hr, b * P:b * P + P], bank=B[6 + h // 2], start=True, stop=True))
            if h % 2:
                items[-1]["evac"] = to_mix(h // 2, B[6 + h // 2])
        items[0]["after"] = now()
        add, mul = const("cmp_add"), const("cmp_mul")
        for h in range(4):
            hr = slice(64 * (h % 2), 64 * (h % 2) + 64)
            for b in range(NTB):
                w_ = (b + 1) * P
                out = dict(out=B[6 + h // 2][hr, b * P:w_], bank=B[6 + h // 2])
                cols = slice(b * N_CMP, (b + 1) * N_CMP)
                gate = lambda n: sm[:, b, 32 + 4 * n + h:33 + 4 * n + h]
                items.append(dict(q=H[hr, BQ + h // 2, b * P:w_], k=kcmp[hr, :], width=N_CMP, gate=gate(0),
                                  extra=[(ident, add[:, cols], 0, N_CMP)], valid=mul[:, cols], v=[vcmp],
                                  start=True, stop=False, **out))
                causal = [(ident, const("causal"), b * P, P)]
                items.append(dict(q=H[hr, BQR + h // 2, b * P:w_], k=H[hr, KS2, 0:w_], width=w_, gate=gate(1),
                                  extra=causal, v=[vsw[:, c, 0:64] for c in range(b + 1)], start=False, stop=False,
                                  **out))
                items.append(dict(q=H[hr, BQR + h // 2, b * P:w_], k=H[hr, KW2, 0:w_], width=w_, gate=gate(2),
                                  extra=causal, v=[vsw[:, c, 64:128] for c in range(b + 1)], start=False, stop=True,
                                  **out))
            if h % 2:
                items[-1]["evac"] = to_mix(2 + h // 2, B[6 + h // 2])

        def square(m):
            A(s.activation, H[:, 30, :], H[:, m, :], ACT.Square, after=[V.sem.token()] + pr.tensor_now())

        def l2_norm(m):
            bank = gemm_bank()
            tok = matmuls(bank[:, :], [(ones, H[:, 30, :])], after=[A.sem.token()], bank=bank)
            inv_sqrt(bank, tok, 1e-6, H[:, 31, :])
            V(v.scalar_tensor_tensor, H[:, m, :], H[:, m, :], 1.0 if m >= GH else float(P) ** -0.5, H[:, 31, :],
              ALU.mult, ALU.mult)
        todo = [conv_tile(0)]
        for m in range(7):
            todo += [lambda m=m: (square(m), conv_tile(m + 1)()), lambda m=m: l2_norm(m)]
        todo += [lambda: square(7), lambda: l2_norm(7)]
        n_todo, n_items = len(todo), len(items)
        V.wait(*pr.tensor_now())
        attention(items, lambda j: todo.pop(0)() if todo and j * n_todo % n_items < n_todo else None)
        assert not todo

        QK, WT = 16, 20
        UT, KDEC = 4, 8
        KBT, ATL, XM, XTM, PM, KBG, VBT, EG = range(8)
        glast = COL[:, 16:48]
        blk = lambda b: slice(b * P, b * P + P)
        v4 = lambda ap: ap.rearrange("p (b c) -> p b c", b=NTB)
        over = lambda ap: ap.rearrange("p (a c) -> p a c", a=1).broadcast_to([P, NTB, P])
        lev = const("levels")
        for pair in range(2):
            hs = (2 * pair, 2 * pair + 1)
            W = [lambda n: H[:, 24 + n, :], lambda n: U[:, n, :]]
            col = lambda a, h: c4(a)[:, :, h:h + 1].broadcast_to([P, NTB, P])
            level_mask = lambda e, k: M[:, 4 + 2 * e + k % 2, :]
            start = now()
            t_tok, t_rows = [0, 0], [0, 0]
            for e, h in enumerate(hs):
                for n, src in enumerate((4 + h, 8 + h)):
                    bank = B[2 + 3 * e + n]
                    PE.wait(bank.free, *start)
                    for b in range(NTB):
                        ins = pe.transpose(bank[:, blk(b)], H[:, src, blk(b)], ident)
                    t_tok[e] = PE.done(ins)
                PE.wait(B[4 + 3 * e].free, B[e].free)
                for b in range(NTB):
                    pe.matmul(B[4 + 3 * e][:, blk(b)], c4(gcol)[:, b, h:h + 1].broadcast_to([P, P]), const("tri"),
                              start=True, stop=True)
                    ins = pe.matmul(B[e][:, blk(b)], c4(beta)[:, b, h:h + 1].broadcast_to([P, P]), ident,
                                    start=True, stop=True)
                t_rows[e] = PE.done(ins)
            t_kb, t_dec = [0, 0], [0, 0]
            for e, h in enumerate(hs):
                w = W[e]
                for b in range(NTB):
                    V(v.scalar_tensor_tensor, w(PM)[:, blk(b)], B[4 + 3 * e][:, blk(b)], c4(ngc)[:, b, h:h + 1],
                      const("decay_mask"), ALU.add, ALU.add, after=[t_rows[e], A.sem.token()] + pr.tensor_now())
                A(s.activation, w(PM), w(PM), ACT.Exp, after=[V.sem.token()])
                t_dec[e] = A(s.activation, w(EG), B[4 + 3 * e][:, :], ACT.Exp, after=pr.tensor_now())
                B[4 + 3 * e].free = [t_dec[e]]
                t_kb[e] = V(v.tensor_tensor, w(KBT), H[:, 4 + h, :], B[e][:, :], ALU.mult)
                B[e].free = [t_kb[e]]
                V(v.tensor_tensor, v4(w(KBG)), v4(B[2 + 3 * e][:, :]), col(bege, h), ALU.mult)
                for dst, bank, scale in ((w(VBT), B[3 + 3 * e], beta), (H[:, KDEC + h, :], B[2 + 3 * e], gle)):
                    for b in range(NTB):
                        t = A(s.activation, dst[:, blk(b)], bank[:, blk(b)], ACT.Copy, scale=c4(scale)[:, b, h:h + 1],
                              after=[V.sem.token()])
                B[2 + 3 * e].free = B[3 + 3 * e].free = [V.sem.token(), t]
            for e, h in enumerate(hs):
                w = W[e]
                PE.wait(B[2 + 3 * e].free, B[3 + 3 * e].free, t_kb[e])
                for b in range(NTB):
                    pe.matmul(B[2 + 3 * e][:, blk(b)], H[:, 4 + h, blk(b)], w(KBT)[:, blk(b)], start=True, stop=True)
                    ins = pe.matmul(B[3 + 3 * e][:, blk(b)], H[:, 4 + h, blk(b)], H[:, h, blk(b)], start=True, stop=True)
                t_kk = PE.done(ins)
                V(v.tensor_tensor, w(ATL), B[2 + 3 * e][:, :], w(PM), ALU.mult, after=[t_kk, t_dec[e]])
                t = V(v.tensor_tensor, H[:, QK + h, :], B[3 + 3 * e][:, :], w(PM), ALU.mult)
                B[2 + 3 * e].free = B[3 + 3 * e].free = [t]
                V(v.tensor_copy, glast[:, 8 * h:8 * h + 8], w(EG)[:, 63::64])
                V(v.tensor_tensor, v4(w(XM)), v4(w(ATL)), over(lev[:, 0:P]), ALU.mult)
                t = V(v.tensor_tensor, v4(w(XTM)), over(ident), v4(w(XM)), ALU.subtract)
                bank = B[4 + 3 * e]
                PE.wait(bank.free, t)
                for b in range(NTB):
                    ins = pe.transpose(bank[:, blk(b)], w(XTM)[:, blk(b)], ident)
                tok = PE.done(ins)
                V(v.tensor_tensor, H[:, h, :], H[:, h, :], w(EG), ALU.mult)
                bank.free = [A(s.activation, w(XM), bank[:, :], ACT.Copy, after=[tok, t])]
            t_xm = [A.sem.token()] * 2
            t_mask = [0, 0]
            atl_ready = V.sem.token()
            t_used = [pr.tensor_now()] * 2
            for e in range(2):
                t_mask[e] = V(v.tensor_tensor, v4(level_mask(e, 1)), v4(W[e](ATL)), over(lev[:, P:2 * P]), ALU.mult,
                              after=[atl_ready, A.sem.token()] + t_used[e])
            for k in range(1, 6):
                t_p, t_pc = [0, 0], [0, 0]
                for e in range(2):
                    w = W[e]
                    bank = B[2 + 3 * e]
                    PE.wait(bank.free, t_mask[e], t_xm[e])
                    for b in range(NTB):
                        ins = pe.matmul(bank[:, blk(b)], level_mask(e, k)[:, blk(b)], w(XM)[:, blk(b)], start=True, stop=True)
                    t_p[e] = PE.done(ins)
                    if k < 5:
                        t_mask[e] = V(v.tensor_tensor, v4(level_mask(e, k + 1)), v4(w(ATL)),
                                      over(lev[:, (k + 1) * P:(k + 2) * P]), ALU.mult, after=[t_p[e]])
                    t_pc[e] = A(s.activation, w(PM), bank[:, :], ACT.Copy, after=[t_p[e], V.sem.token()])
                    bank.free = [t_pc[e]]
                t_xm2 = [0, 0]
                for e in range(2):
                    w = W[e]
                    PE.wait(B[3 + 3 * e].free, B[4 + 3 * e].free, t_pc[e])
                    if k < 5:
                        for b in range(NTB):
                            ins = pe.matmul(B[4 + 3 * e][:, blk(b)], w(XTM)[:, blk(b)], w(PM)[:, blk(b)], start=True, stop=True)
                        t_q = PE.done(ins)
                    for b in range(NTB):
                        ins = pe.matmul(B[3 + 3 * e][:, blk(b)], w(PM)[:, blk(b)], w(XTM)[:, blk(b)], start=True, stop=True)
                    t_qt = PE.done(ins)
                    if k < 5:
                        t_xm2[e] = V(v.tensor_tensor, w(XM), w(XM), B[4 + 3 * e][:, :], ALU.subtract, after=[t_q, t_xm[e]])
                        B[4 + 3 * e].free = [t_xm2[e]]
                    t_xt = V(v.tensor_tensor, w(XTM), w(XTM), B[3 + 3 * e][:, :], ALU.subtract, after=[t_qt])
                    B[3 + 3 * e].free = [t_xt]
                    if k == 5:
                        t_xm2[e] = t_xt
                t_xm = t_xm2
            for e, h in enumerate(hs):
                w = W[e]
                PE.wait(B[2 + 3 * e].free, B[3 + 3 * e].free, t_xm[e])
                for b in range(NTB):
                    pe.matmul(B[2 + 3 * e][:, blk(b)], w(XTM)[:, blk(b)], w(VBT)[:, blk(b)], start=True, stop=True)
                    ins = pe.matmul(B[3 + 3 * e][:, blk(b)], w(KBG)[:, blk(b)], w(XTM)[:, blk(b)], start=True, stop=True)
                tok = PE.done(ins)
                A(s.activation, H[:, UT + h, :], B[2 + 3 * e][:, :], ACT.Copy, after=[tok])
                t = A(s.activation, H[:, WT + h, :], B[3 + 3 * e][:, :], ACT.Copy)
                B[2 + 3 * e].free = B[3 + 3 * e].free = [t]
        heads = lambda n: H[:, n, :].rearrange("p (h e) -> p h e", h=GH)
        state = (heads(24), heads(26))
        v_new = (heads(25), heads(27))
        decay = glast.rearrange("p (h c) -> p h c", h=GH)
        t_st = [V(v.memset, state[0], 0.0, after=now() + pr.tensor_now())]
        PE.wait(*now())
        for c in range(8):
            b, o = c // 2, 64 * (c % 2)
            ck = slice(c * 64, c * 64 + 64)
            bw, bo, bs = B[2 + c % 2], B[4 + c % 2], B[6 + c % 2]
            ST2, VN, after_c = state[c % 2], v_new[c % 2], state[(c + 1) % 2]
            PE.wait(bw.free, t_st)
            for h in range(GH):
                ins = pe.matmul(bw[o:o + 64, h * P:h * P + P], H[:, WT + h, ck], ST2[:, h, :], start=True, stop=True)
            tok = PE.done(ins)
            t_vn = V(v.tensor_tensor, VN[o:o + 64, :, :], H[o:o + 64, UT:UT + GH, blk(b)],
                     bw[o:o + 64, :].rearrange("p (h e) -> p h e", h=GH), ALU.subtract, after=[tok])
            bw.free = [t_vn]
            PE.wait(bo.free)
            for h in range(GH):
                pe.matmul(bo[:, h * 64:h * 64 + 64], ST2[:, h, :], H[:, h, ck], start=(h == 0), stop=False,
                          skip_group_check=True)
            PE.wait(bs.free, t_vn)
            if c < 7:
                for h in range(GH):
                    ins = pe.matmul(bs[:, h * P:h * P + P], H[o:o + 64, KDEC + h, blk(b)], VN[o:o + 64, h, :],
                                    start=True, stop=True)
                t_kv = PE.done(ins)
                V(v.tensor_tensor, after_c, ST2, decay[:, :, c:c + 1].broadcast_to([P, GH, P]), ALU.mult)
                t = V(v.tensor_tensor, after_c, after_c, bs[:, :].rearrange("p (h e) -> p h e", h=GH), ALU.add,
                      after=[t_kv])
                t_st = [t]
                bs.free = [t]
            for h in range(GH):
                ins = pe.matmul(bo[:, h * 64:h * 64 + 64], VN[o:o + 64, h, :], H[o:o + 64, QK + h, ck], start=False,
                                stop=True, skip_group_check=True)
            t_o = PE.done(ins)
            bo.free = [A(s.activation, M[:, 4:8, ck], bo[:, 0:256].rearrange("p (h t) -> p h t", h=GH), ACT.Copy,
                         after=[t_o, V.sem.token()])]
        mo = M[:, 4:8, :].rearrange("p a t -> p (a t)")
        A(s.activation, wide(24), mo, ACT.Square, after=[V.sem.token()] + pr.tensor_now())
        mix_tok[0:4] = [A.sem.token()] * 4

        def gdn_out(h):
            mix_tok[4 + h] = V(v.tensor_tensor, M[:, 4 + h, :], M[:, 4 + h, :], H[:, 12 + h, :], ALU.mult)
        head_norm(lambda h: M[:, 4 + h, :], mo, 24, 28, lambda h: vec2("gdn_norm"), gdn_out)

        tok = output_gemm(mix_tile(mix_tok), add_gated(mod[:, 16:24]), square_step)
        ready = rms_norm_all(tok, GF, mod[:, 24:32], split=True)

        def gate_up(at, j, ready=None):
            tmp = TMP[:, j % 2, 0:T]

            def evac(bank, tok):
                t = V(v.tensor_tensor, tmp, bank[:, :], tmp, ALU.mult, after=[tok, A.sem.token()])
                split_hidden(at, tmp, t)
                return [t]
            gemm_split(u_split, KT, lambda bank, tok: [A(s.activation, tmp, bank[:, :], ACT.Silu,
                                                         after=[tok, V.sem.token()])], ready)
            gemm_split(u_split, KT, evac, ready)
        pairs = BODY // 2
        for a in range(0, FF2_T, HALF):
            tiles = min(HALF, FF2_T - a)
            for j in range(pairs):
                gate_up(j, j, ready)
            with pr.loop(f"gate_up{a}", tiles // pairs - 1, fence=False) as i:
                for j in range(pairs):
                    gate_up(i * pairs + (pairs + j), j)
            output_gemm(down_tile(tiles, a + HALF >= FF2_T), add_gated(mod[:, 40:48]),
                        square_step if a + HALF >= FF2_T else None)
            ready = None

    rms_norm_all(pr.tensor_now(), vec1("final"), None)
    stored = pr.count("stored")
    for b in range(NTB):
        for half in range(2):
            bank = B[4 + half]
            PE.wait(bank.free, *now())
            for k in range(4):
                ins = pe.transpose(bank[:, k * P:k * P + P], U[:, 4 * half + k, b * P:b * P + P], ident)
            tok = PE.done(ins)
            t = A(s.activation, M[:, 2 * b + half, :], bank[:, :], ACT.Copy, after=[tok])
            bank.free = [t]
    A.wait(A.sem.token())
    A.done(s.dma_start(io["out"].rearrange("(b p) d -> p b d", p=P),
                       M[:, :, :].rearrange("p (b h) t -> p b (h t)", b=NTB)), stored, 16)
    A.wait(stored.token())
    assert pr.panel == n_panels, (pr.panel, n_panels)
    assert ada.made.const * GROUP + N_START == N_ADA
    return pr.found


def kernel(**inputs):
    import concourse.bacc as bacc
    from concourse.bass_utils import run_bass_kernel_spmd

    i = {k: np.asarray(a) for k, a in inputs.items()}
    arrays = {
        "x": np.ascontiguousarray(i["x"][0]),
        "consts": constants(),
        "vec1": vectors1(i),
        "vec2": np.stack([vectors2(i, l) for l in range(L2)]),
    }
    arrays["stream"], arrays["ada"] = weight_streams(i)

    def program(plan):
        nc = bacc.Bacc("TRN2", target_bir_lowering=False, num_devices=1)
        io = {k: nc.dram_tensor(k, a.shape, F32, kind="ExternalInput").ap() for k, a in arrays.items()}
        io["out"] = nc.dram_tensor("out", (T, D), F32, kind="ExternalOutput").ap()
        return nc, build(nc, io, N_START + N_MAIN, plan)

    _, plan = program({})
    nc, again = program(plan)
    assert again == plan
    r = run_bass_kernel_spmd(nc, [arrays], core_ids=[0])
    return r.results[0]["out"].reshape(1, T, D)
```
